# Optimizing a Trainium2 kernel written in Bass

```python
import math
import jax, jax.numpy as jnp
from jax import lax
import numpy as np
import jax
import jax.numpy as jnp

D_MODEL = 1024
BATCH = 1
SEQ = 256
DEPTH = 1

N_META = 16
D_MIX = D_MODEL
D_HYENA = D_MIX // 2
D_HGRN = D_MIX - D_HYENA
HYENA_ORDER = 2
SHORT_CONV = 3
FILTER_EMB = 33
FILTER_BANDS = (FILTER_EMB - 1) // 2
FILTER_HIDDEN = 64
DECAY_TARGET = 1e-2
FAST_DECAY_PCT = 0.3
SLOW_DECAY_PCT = 1.5
HGRN_HEAD_DIM = 128
HGRN_HEADS = D_HGRN // HGRN_HEAD_DIM
CHUNK = 64
N_GROUPS = 8
EXPERTS_PER_GROUP = 8
N_EXPERTS = N_GROUPS * EXPERTS_PER_GROUP
TOP_K = 2
D_EXPERT = D_MODEL // 2
MOE_BLOCK = 128
D_HYENA_PROJ = (HYENA_ORDER + 1) * D_HYENA
D_HGRN_PROJ = 5 * D_HGRN
D_IN_PROJ = D_HYENA_PROJ + D_HGRN_PROJ
EPS = 1e-6


def rms_norm(x, gain):
    xf = x.astype(jnp.float32)
    y = xf * lax.rsqrt(jnp.mean(xf * xf, axis=-1, keepdims=True) + EPS)
    return (y * gain.astype(jnp.float32)).astype(x.dtype)

def centred_short_conv(u, w, b):
    L = u.shape[1]
    half = SHORT_CONV // 2
    up = jnp.pad(u, ((0, 0), (half, SHORT_CONV - 1 - half), (0, 0)))
    y = b
    for j in range(SHORT_CONV):
        y = y + up[:, j:j + L] * w[j]
    return y

def hyena_filter_spectra(L, w1, b1, w2, b2, w3, freq):
    f32 = jnp.float32
    pos = jnp.arange(L, dtype=f32)
    t = pos / max(L - 1, 1)
    bands = jnp.linspace(1e-4, FILTER_BANDS - 1, FILTER_BANDS, dtype=f32)
    ang = (2.0 * math.pi / L) * pos[:, None] * bands[None, :]
    z = jnp.concatenate([t[:, None], jnp.cos(ang), -jnp.sin(ang)], axis=-1)
    fr = freq.astype(f32)
    hid = jnp.sin(fr * (z @ w1.astype(f32) + b1.astype(f32)))
    hid = jnp.sin(fr * (hid @ w2.astype(f32) + b2.astype(f32)))
    filt = (hid @ w3.astype(f32)).reshape(L, 2, HYENA_ORDER, D_HYENA)
    deltas = jnp.abs(jnp.linspace(math.log(DECAY_TARGET) / SLOW_DECAY_PCT,
                                  math.log(DECAY_TARGET) / FAST_DECAY_PCT, D_HYENA, dtype=f32))
    window = jnp.exp(-t[:, None] * deltas[None, :])
    filt = filt * window[:, None, None, :]
    h_fwd, h_bwd = filt[:, 0], filt[:, 1]
    two_sided = jnp.concatenate([h_fwd, jnp.zeros_like(h_fwd[:1]), h_bwd[:0:-1]], axis=0)
    return jnp.fft.rfft(two_sided, axis=0)

def fft_long_conv(u, spec, skip):
    L = u.shape[1]
    uf = u.astype(jnp.float32)
    y = jnp.fft.irfft(jnp.fft.rfft(uf, n=2 * L, axis=1) * spec[None], n=2 * L, axis=1)[:, :L]
    return (y + uf * skip.astype(jnp.float32)).astype(u.dtype)

def hyena_mixer(p, conv_w, conv_b, w1, b1, w2, b2, w3, freq, skip):
    L = p.shape[1]
    u = centred_short_conv(p, conv_w, conv_b)
    z = u[..., :D_HYENA]
    spectra = hyena_filter_spectra(L, w1, b1, w2, b2, w3, freq)
    for n in range(HYENA_ORDER):
        gate = u[..., (n + 1) * D_HYENA:(n + 2) * D_HYENA]
        z = gate * fft_long_conv(z, spectra[:, n], skip[n])
    return z

def chunked_gated_linear_scan(q, k, v, log_f):
    B, T, H, DK = q.shape
    DV = v.shape[-1]
    N = T // CHUNK
    q, k, v, log_f = [a.reshape(B, N, CHUNK, H, a.shape[-1]) for a in (q, k, v, log_f)]
    b = jnp.cumsum(log_f, axis=2)
    b_last = b[:, :, -1]
    b_mid = b[:, :, CHUNK // 2][:, :, None]
    scores = jnp.einsum('bnthd,bnshd->bnhts', q * jnp.exp(b - b_mid), k * jnp.exp(b_mid - b))
    lower_tri = jnp.tril(jnp.ones((CHUNK, CHUNK), dtype=bool))
    scores = jnp.where(lower_tri, scores, 0.0)
    o_intra = jnp.einsum('bnhts,bnshv->bnthv', scores, v)
    chunk_state = jnp.einsum('bnshd,bnshv->bnhdv', k * jnp.exp(b_last[:, :, None] - b), v)
    chunk_decay = jnp.exp(b_last)

    def step(S, inp):
        dec, U = inp
        return dec[..., None] * S + U, S

    S0 = jnp.zeros((B, H, DK, DV), q.dtype)
    _, S_in = lax.scan(step, S0, (jnp.moveaxis(chunk_decay, 1, 0), jnp.moveaxis(chunk_state, 1, 0)))
    S_in = jnp.moveaxis(S_in, 0, 1)
    o_inter = jnp.einsum('bnthd,bnhdv->bnthv', q * jnp.exp(b), S_in)
    return (o_intra + o_inter).reshape(B, T, H, DV)

def hgrn2_mixer(p, lb_f, lb_b, norm_w):
    f32 = jnp.float32
    B, L, _ = p.shape
    q, f_fwd, f_bwd, i_in, g = [p[..., j * D_HGRN:(j + 1) * D_HGRN] for j in range(5)]

    def heads(a):
        return a.reshape(B, L, HGRN_HEADS, HGRN_HEAD_DIM)

    qh = heads(jax.nn.silu(q.astype(f32)))
    vh = heads(i_in.astype(f32))

    def forget(logit, lb):
        lb = lb.astype(f32)
        f = lb + (1.0 - lb) * jax.nn.sigmoid(logit.astype(f32))
        return heads(1.0 - f), heads(jnp.log(f))

    k_f, lf_f = forget(f_fwd, lb_f)
    k_b, lf_b = forget(f_bwd, lb_b)
    n_pad = (-N_META) % CHUNK

    def pad(a):
        return jnp.pad(a, ((0, 0), (n_pad, 0), (0, 0), (0, 0)))

    def flip(a):
        return a[:, ::-1]

    qp, vp = pad(qh), pad(vh)
    o_f = chunked_gated_linear_scan(qp, pad(k_f), vp, pad(lf_f))
    o_b = flip(chunked_gated_linear_scan(flip(qp), flip(pad(k_b)), flip(vp), flip(pad(lf_b))))
    o = (o_f + o_b)[:, n_pad:]
    o = o * lax.rsqrt(jnp.mean(o * o, axis=-1, keepdims=True) + EPS)
    o = o.reshape(B, L, D_HGRN) * norm_w.astype(f32) * jax.nn.silu(g.astype(f32))
    return o.astype(p.dtype)

def hier_moe(h, w_rg, w_re, w_gate, w_up, w_down):
    f32 = jnp.float32
    B, L, D = h.shape
    n_tok = B * L
    hf = h.reshape(n_tok, D)
    g_logits = (hf @ w_rg).astype(f32)
    g_sel = jnp.argmax(g_logits, axis=-1)
    p_group = jnp.take_along_axis(jax.nn.softmax(g_logits, axis=-1), g_sel[:, None], axis=-1)
    e_logits = jnp.einsum('nd,dge->nge', hf, w_re).astype(f32)
    e_logits = e_logits[jnp.arange(n_tok), g_sel]
    p_top, e_top = lax.top_k(jax.nn.softmax(e_logits, axis=-1), TOP_K)
    gate = p_group * p_top / jnp.sum(p_top, axis=-1, keepdims=True)
    expert_id = (g_sel[:, None] * EXPERTS_PER_GROUP + e_top).reshape(-1).astype(jnp.int32)

    M = n_tok * TOP_K
    n_blocks = -(-M // MOE_BLOCK) + N_EXPERTS
    n_slots = n_blocks * MOE_BLOCK
    order = jnp.argsort(expert_id)
    eid_s = expert_id[order]
    tok_s = (jnp.arange(M, dtype=jnp.int32) // TOP_K)[order]
    gate_s = gate.reshape(-1)[order]
    counts = jnp.bincount(expert_id, length=N_EXPERTS)
    padded = (counts + MOE_BLOCK - 1) // MOE_BLOCK * MOE_BLOCK
    start = jnp.cumsum(counts) - counts
    pend = jnp.cumsum(padded)
    dest = (pend - padded)[eid_s] + jnp.arange(M, dtype=jnp.int32) - start[eid_s]
    tok_buf = jnp.zeros((n_slots,), jnp.int32).at[dest].set(tok_s)
    gate_buf = jnp.zeros((n_slots,), f32).at[dest].set(gate_s)
    block_eid = jnp.minimum(
        jnp.searchsorted(pend, jnp.arange(n_blocks, dtype=pend.dtype) * MOE_BLOCK, side='right'),
        N_EXPERTS - 1)
    xb = hf[tok_buf].reshape(n_blocks, MOE_BLOCK, D)

    def expert_block(args):
        xe, e = args
        return (jax.nn.silu(xe @ w_gate[e]) * (xe @ w_up[e])) @ w_down[e]

    yb = lax.map(expert_block, (xb, block_eid)).reshape(n_slots, D)
    y = jnp.zeros_like(hf).at[tok_buf].add(yb * gate_buf[:, None].astype(yb.dtype))
    return y.reshape(B, L, D)

def first_inputs(seed: int = 0) -> dict:
    key = jax.random.key(seed)
    ks = jax.random.split(key, 25)

    def nrm(k, shape, scale):
        return scale * jax.random.normal(k, shape, jnp.float32)

    return {
        'x': nrm(ks[0], (BATCH, SEQ, D_MODEL), 1.0),
        'meta_tokens': nrm(ks[1], (N_META, D_MODEL), 1.0),
        'w_in': nrm(ks[2], (DEPTH, D_MODEL, D_IN_PROJ), D_MODEL ** -0.5),
        'conv_w': nrm(ks[3], (DEPTH, SHORT_CONV, D_HYENA_PROJ), SHORT_CONV ** -0.5),
        'conv_b': nrm(ks[4], (DEPTH, D_HYENA_PROJ), 0.01),
        'filt_w1': nrm(ks[5], (DEPTH, FILTER_EMB, FILTER_HIDDEN), FILTER_EMB ** -0.5),
        'filt_b1': nrm(ks[6], (DEPTH, FILTER_HIDDEN), 0.1),
        'filt_w2': nrm(ks[7], (DEPTH, FILTER_HIDDEN, FILTER_HIDDEN), FILTER_HIDDEN ** -0.5),
        'filt_b2': nrm(ks[8], (DEPTH, FILTER_HIDDEN), 0.1),
        'filt_w3': nrm(ks[9], (DEPTH, FILTER_HIDDEN, 2 * HYENA_ORDER * D_HYENA), 0.02),
        'filt_freq': 1.0 + nrm(ks[10], (DEPTH, FILTER_HIDDEN), 0.01),
        'filt_skip': nrm(ks[11], (DEPTH, HYENA_ORDER, D_HYENA), 1.0),
        'hyena_norm': 1.0 + nrm(ks[12], (DEPTH, D_HYENA), 0.01),
        'lb_fwd': nrm(ks[13], (DEPTH + 1, D_HGRN), 0.1),
        'lb_bwd': nrm(ks[14], (DEPTH + 1, D_HGRN), 0.1),
        'hgrn_norm': 1.0 + nrm(ks[15], (DEPTH, D_HGRN), 0.01),
        'w_out': nrm(ks[16], (DEPTH, D_MIX, D_MODEL), D_MIX ** -0.5),
        'norm_mix': 1.0 + nrm(ks[17], (DEPTH, D_MODEL), 0.01),
        'norm_ffn': 1.0 + nrm(ks[18], (DEPTH, D_MODEL), 0.01),
        'w_router_group': nrm(ks[19], (DEPTH, D_MODEL, N_GROUPS), D_MODEL ** -0.5),
        'w_router_expert': nrm(ks[20], (DEPTH, D_MODEL, N_GROUPS, EXPERTS_PER_GROUP), D_MODEL ** -0.5),
        'w_gate': nrm(ks[21], (DEPTH, N_EXPERTS, D_MODEL, D_EXPERT), D_MODEL ** -0.5),
        'w_up': nrm(ks[22], (DEPTH, N_EXPERTS, D_MODEL, D_EXPERT), D_MODEL ** -0.5),
        'w_down': nrm(ks[23], (DEPTH, N_EXPERTS, D_EXPERT, D_MODEL), D_EXPERT ** -0.5),
        'norm_final': 1.0 + nrm(ks[24], (D_MODEL,), 0.01),
    }

def first_block(x, meta_tokens, w_in, conv_w, conv_b, filt_w1, filt_b1, filt_w2, filt_b2, filt_w3,
              filt_freq, filt_skip, hyena_norm, lb_fwd, lb_bwd, hgrn_norm, w_out, norm_mix, norm_ffn,
              w_router_group, w_router_expert, w_gate, w_up, w_down, norm_final):
    B = x.shape[0]
    meta = jnp.broadcast_to(meta_tokens[None].astype(x.dtype), (B, N_META, x.shape[-1]))
    h = jnp.concatenate([meta, x], axis=1)
    lbf_all = jnp.cumsum(jax.nn.softmax(lb_fwd.astype(jnp.float32), axis=0), axis=0)
    lbb_all = jnp.cumsum(jax.nn.softmax(lb_bwd.astype(jnp.float32), axis=0), axis=0)
    for l in range(DEPTH):
        a = rms_norm(h, norm_mix[l])
        p = a @ w_in[l]
        y_hy = hyena_mixer(p[..., :D_HYENA_PROJ], conv_w[l], conv_b[l], filt_w1[l], filt_b1[l],
                           filt_w2[l], filt_b2[l], filt_w3[l], filt_freq[l], filt_skip[l])
        y_hy = rms_norm(y_hy, hyena_norm[l])
        y_hg = hgrn2_mixer(p[..., D_HYENA_PROJ:], lbf_all[l], lbb_all[l], hgrn_norm[l])
        h = h + jnp.concatenate([y_hy, y_hg], axis=-1) @ w_out[l]
        h = h + hier_moe(rms_norm(h, norm_ffn[l]), w_router_group[l], w_router_expert[l],
                         w_gate[l], w_up[l], w_down[l])
    h = rms_norm(h, norm_final)
    return h[:, N_META:]


DEPTH_2 = 2

N_MEM = 256
N_BRANCH = 5
BRANCH_WIDTH = D_MODEL // 2
N_HEADS = 4
HEAD_DIM = BRANCH_WIDTH // N_HEADS
SB_BLOCK = 128
GMLP_BLOCK = 128
GM_GROUPS = 4
CONV_WIDTH = 4
ROPE_BASE = 10000.0


def _in_sizes():
    w, h = BRANCH_WIDTH, N_HEADS
    return ([w] * 4
            + [w] * 5 + [h, h]
            + [w] * 3
            + [w] * 4
            + [w] * 2
            + [N_BRANCH * D_MODEL])

def rms_norm_2(x, g):
    xf = x.astype(jnp.float32)
    y = xf * lax.rsqrt(jnp.mean(xf * xf, axis=-1, keepdims=True) + EPS)
    return (y * g.astype(jnp.float32)).astype(x.dtype)

def layer_norm(x, g, b):
    xf = x.astype(jnp.float32)
    mu = jnp.mean(xf, axis=-1, keepdims=True)
    var = jnp.mean(jnp.square(xf - mu), axis=-1, keepdims=True)
    y = (xf - mu) * lax.rsqrt(var + EPS)
    return (y * g.astype(jnp.float32) + b.astype(jnp.float32)).astype(x.dtype)

def head_norm(t):
    tf = t.astype(jnp.float32)
    mu = jnp.mean(tf, axis=-1, keepdims=True)
    var = jnp.mean(jnp.square(tf - mu), axis=-1, keepdims=True)
    return (tf - mu) * lax.rsqrt(var + EPS)

def causal_conv(x, w):
    k = w.shape[0]
    return lax.conv_general_dilated(
        x, w[:, None, :].astype(x.dtype), window_strides=(1,), padding=((k - 1, 0),),
        dimension_numbers=('NWC', 'WIO', 'NWC'), feature_group_count=x.shape[-1])

def rotary(t, positions):
    half = t.shape[-1] // 2
    inv_freq = ROPE_BASE ** (-jnp.arange(half, dtype=jnp.float32) / half)
    ang = positions.astype(jnp.float32)[..., None] * inv_freq
    cos, sin = jnp.cos(ang)[:, :, None, :], jnp.sin(ang)[:, :, None, :]
    tf = t.astype(jnp.float32)
    t1, t2 = tf[..., :half], tf[..., half:]
    return jnp.concatenate([t1 * cos - t2 * sin, t1 * sin + t2 * cos], axis=-1)

def to_chunks(t):
    b, s, h = t.shape[:3]
    t = t.astype(jnp.float32).reshape(b, s // CHUNK, CHUNK, h, *t.shape[3:])
    return jnp.moveaxis(t, 3, 1)

def from_chunks(t):
    b, h, nc, l, d = t.shape
    return jnp.moveaxis(t, 1, 3).reshape(b, nc * l, h, d)

def stick_breaking(q, k, v):
    b, s, h, d = q.shape
    nb = s // SB_BLOCK
    qb = q.reshape(b, nb, SB_BLOCK, h, d).transpose(1, 0, 3, 2, 4)
    kf = k.transpose(0, 2, 1, 3).astype(jnp.float32)
    vf = v.transpose(0, 2, 1, 3).astype(jnp.float32)
    key_pos = jnp.arange(s)
    scale = d ** -0.5

    def block(args):
        q_blk, i = args
        z = jnp.einsum('bhqd,bhkd->bhqk', q_blk.astype(jnp.float32), kf) * scale
        q_pos = i * SB_BLOCK + jnp.arange(SB_BLOCK)
        valid = key_pos[None, :] < q_pos[:, None]
        log_keep = jnp.where(valid, -jax.nn.softplus(z), 0.0)
        later = lax.cumsum(log_keep, axis=3, reverse=True) - log_keep
        w = jnp.where(valid, jnp.exp(jax.nn.log_sigmoid(z) + later), 0.0)
        return jnp.einsum('bhqk,bhkd->bhqd', w, vf)

    out = lax.map(block, (qb, jnp.arange(nb)))
    return out.transpose(1, 0, 3, 2, 4).reshape(b, s, h, d).astype(q.dtype)

def mlstm(q, k, v, i_pre, f_pre):
    b_, s_, h_, d = q.shape
    qc, kc, vc = to_chunks(q), to_chunks(k) * d ** -0.5, to_chunks(v)
    ic = to_chunks(i_pre)
    bcum = jnp.cumsum(jax.nn.log_sigmoid(to_chunks(f_pre)), axis=-1)
    g = bcum + lax.cummax(ic - bcum, axis=3)
    b_last, a_last = bcum[..., -1], g[..., -1]
    w_end = jnp.exp(b_last[..., None] - bcum + ic - a_last[..., None])
    kv_loc = jnp.einsum('bhcld,bhcle->bhcde', kc * w_end[..., None], vc)
    n_loc = jnp.einsum('bhcl,bhcld->bhcd', w_end, kc)

    def step(carry, inp):
        c_st, n_st, m_st = carry
        bl, al, kv, nl = inp
        m_new = jnp.maximum(bl + m_st, al)
        d_old = jnp.exp(bl + m_st - m_new)
        d_loc = jnp.exp(al - m_new)
        c_new = d_old[..., None, None] * c_st + d_loc[..., None, None] * kv
        n_new = d_old[..., None] * n_st + d_loc[..., None] * nl
        return (c_new, n_new, m_new), (c_st, n_st, m_st)

    init = (jnp.zeros((b_, h_, d, d), jnp.float32), jnp.zeros((b_, h_, d), jnp.float32),
            jnp.zeros((b_, h_), jnp.float32))
    xs = (jnp.moveaxis(b_last, 2, 0), jnp.moveaxis(a_last, 2, 0),
          jnp.moveaxis(kv_loc, 2, 0), jnp.moveaxis(n_loc, 2, 0))
    _, (c_prev, n_prev, m_prev) = lax.scan(step, init, xs)
    c_prev = jnp.moveaxis(c_prev, 0, 2)
    n_prev = jnp.moveaxis(n_prev, 0, 2)
    m_prev = jnp.moveaxis(m_prev, 0, 2)

    m_t = jnp.maximum(bcum + m_prev[..., None], g)
    d_inter = jnp.exp(bcum + m_prev[..., None] - m_t)
    num = d_inter[..., None] * jnp.einsum('bhcld,bhcde->bhcle', qc, c_prev)
    den = d_inter * jnp.einsum('bhcld,bhcd->bhcl', qc, n_prev)
    causal = jnp.tril(jnp.ones((CHUNK, CHUNK), dtype=bool))
    log_d = bcum[..., :, None] - bcum[..., None, :] + ic[..., None, :] - m_t[..., :, None]
    d_intra = jnp.exp(jnp.where(causal, log_d, -jnp.inf))
    sc = jnp.einsum('bhctd,bhcsd->bhcts', qc, kc) * d_intra
    num = num + jnp.einsum('bhcts,bhcse->bhcte', sc, vc)
    den = den + jnp.sum(sc, axis=-1)
    h = num / jnp.maximum(jnp.abs(den), jnp.exp(-m_t))[..., None]
    return from_chunks(h)

def retention(q, k, v):
    b_, s_, h_, d = q.shape
    qc, kc, vc = to_chunks(q), to_chunks(k) * d ** -0.5, to_chunks(v)
    log_gamma = jnp.log(1.0 - 2.0 ** (-5.0 - jnp.arange(h_, dtype=jnp.float32)))
    idx = jnp.arange(CHUNK, dtype=jnp.float32)
    intra_decay = jnp.exp(log_gamma[:, None, None] * jnp.abs(idx[:, None] - idx[None, :]))
    sc = jnp.einsum('bhcnd,bhcmd->bhcnm', qc, kc) * intra_decay[:, None]
    intra = jnp.einsum('bhcnm,bhcme->bhcne', sc, vc)
    w_end = jnp.exp(log_gamma[:, None] * (CHUNK - 1 - idx))
    kv_loc = jnp.einsum('bhcld,bhcle->bhcde', kc * w_end[None, :, None, :, None], vc)
    chunk_decay = jnp.exp(log_gamma * CHUNK)[None, :, None, None]

    def step(state, kv):
        return chunk_decay * state + kv, state

    _, s_prev = lax.scan(step, jnp.zeros((b_, h_, d, d), jnp.float32), jnp.moveaxis(kv_loc, 2, 0))
    s_prev = jnp.moveaxis(s_prev, 0, 2)
    w_q = jnp.exp(log_gamma[:, None] * (idx + 1.0))
    inter = w_q[:, None, :, None] * jnp.einsum('bhcnd,bhcde->bhcne', qc, s_prev)
    return from_chunks(intra + inter)

def spatial_gating(u, v, ln_g, ln_b, w_s, b_s):
    b_, s_, w = u.shape
    v = layer_norm(v, ln_g, ln_b)
    vb = v.reshape(b_, s_ // GMLP_BLOCK, GMLP_BLOCK, GM_GROUPS, w // GM_GROUPS)
    chunk_id = jnp.arange(GMLP_BLOCK) // CHUNK
    mask = chunk_id[None, :] <= chunk_id[:, None]
    mixed = jnp.einsum('gpq,bnqgc->bnpgc', jnp.where(mask, w_s, 0.0).astype(v.dtype), vb)
    mixed = mixed + b_s.T[:, :, None].astype(v.dtype)
    return u * mixed.reshape(b_, s_, w)

def memory_attention(q, mem_k, mem_v):
    logits = jnp.einsum('bshd,bmhd->bhsm', q.astype(jnp.float32), mem_k.astype(jnp.float32))
    p = jax.nn.softmax(logits * q.shape[-1] ** -0.5, axis=-1)
    return jnp.einsum('bhsm,bmhd->bshd', p, mem_v.astype(jnp.float32)).astype(q.dtype)

def hybrid_layer(x, mem, positions, norm_pre, norm_post, w_in, b_igate, b_fgate, conv_q, conv_k,
                 gm_ln_g, gm_ln_b, gm_ws, gm_bs, mem_norm, w_mem_kv, w_up, w_out):
    b_, s_, _ = x.shape
    w = BRANCH_WIDTH
    heads = lambda t: t.reshape(t.shape[0], t.shape[1], N_HEADS, HEAD_DIM)
    flat = lambda t: t.reshape(b_, s_, w).astype(x.dtype)

    h = rms_norm_2(x, norm_pre)
    proj = h @ w_in
    split_points = [int(p) for p in np.cumsum(_in_sizes())[:-1]]
    (sb_q, sb_k, sb_v, sb_z,
     ml_q, ml_k, ml_v, ml_o, ml_z, ml_i, ml_f,
     gm_u, gm_v, gm_z,
     rt_q, rt_k, rt_v, rt_z,
     xa_q, xa_z, gates) = jnp.split(proj, split_points, axis=-1)

    y_sb = flat(stick_breaking(heads(sb_q), heads(sb_k), heads(sb_v)))
    q_ml = jax.nn.silu(causal_conv(ml_q, conv_q))
    k_ml = jax.nn.silu(causal_conv(ml_k, conv_k))
    h_ml = mlstm(heads(q_ml), heads(k_ml), heads(ml_v), ml_i + b_igate, ml_f + b_fgate)
    y_ml = flat(head_norm(h_ml)) * jax.nn.sigmoid(ml_o)
    y_gm = spatial_gating(jax.nn.gelu(gm_u), jax.nn.gelu(gm_v), gm_ln_g, gm_ln_b, gm_ws, gm_bs)
    y_rt = flat(head_norm(retention(rotary(heads(rt_q), positions), rotary(heads(rt_k), positions),
                                    heads(rt_v))))
    mkv = rms_norm_2(mem, mem_norm) @ w_mem_kv
    mem_k, mem_v = jnp.split(mkv, 2, axis=-1)
    y_xa = flat(memory_attention(heads(xa_q), heads(mem_k), heads(mem_v)))

    ys = jnp.stack([y_sb * jax.nn.silu(sb_z), y_ml * jax.nn.silu(ml_z), y_gm * jax.nn.silu(gm_z),
                    y_rt * jax.nn.silu(rt_z), y_xa * jax.nn.silu(xa_z)], axis=2)
    up = jnp.einsum('bsnw,nwd->bsnd', ys, w_up)
    merged = jnp.sum(jax.nn.sigmoid(gates.reshape(b_, s_, N_BRANCH, D_MODEL)) * up, axis=2)
    out = merged @ w_out
    return x + rms_norm_2(out, norm_post)

def second_inputs(seed: int = 0) -> dict:
    key = jax.random.key(seed)
    ks = jax.random.split(key, 20)
    f32 = jnp.float32
    nrm = lambda k, shape, scale: jax.random.normal(k, shape, f32) * scale
    w = BRANCH_WIDTH
    d_in = sum(_in_sizes())
    x = nrm(ks[0], (BATCH, SEQ, D_MODEL), 1.0)
    mem = nrm(ks[1], (BATCH, N_MEM, D_MODEL), 1.0)
    offset = jax.random.randint(ks[2], (BATCH, 1), 0, 4096, dtype=jnp.int32)
    positions = offset + jnp.arange(SEQ, dtype=jnp.int32)[None, :]
    norm_pre = 1.0 + nrm(ks[3], (DEPTH_2, D_MODEL), 0.02)
    norm_post = 1.0 + nrm(ks[4], (DEPTH_2, D_MODEL), 0.02)
    w_in = nrm(ks[5], (DEPTH_2, D_MODEL, d_in), D_MODEL ** -0.5)
    b_igate = nrm(ks[6], (DEPTH_2, N_HEADS), 0.1)
    b_fgate = jnp.linspace(3.0, 6.0, N_HEADS, dtype=f32)[None, :] + nrm(ks[7], (DEPTH_2, N_HEADS), 0.1)
    conv_q = nrm(ks[8], (DEPTH_2, CONV_WIDTH, w), CONV_WIDTH ** -0.5)
    conv_k = nrm(ks[9], (DEPTH_2, CONV_WIDTH, w), CONV_WIDTH ** -0.5)
    gm_ln_g = 1.0 + nrm(ks[10], (DEPTH_2, w), 0.02)
    gm_ln_b = nrm(ks[11], (DEPTH_2, w), 0.02)
    gm_ws = nrm(ks[12], (DEPTH_2, GM_GROUPS, GMLP_BLOCK, GMLP_BLOCK), GMLP_BLOCK ** -0.5)
    gm_bs = 1.0 + nrm(ks[13], (DEPTH_2, GM_GROUPS, GMLP_BLOCK), 0.02)
    mem_norm = 1.0 + nrm(ks[14], (DEPTH_2, D_MODEL), 0.02)
    w_mem_kv = nrm(ks[15], (DEPTH_2, D_MODEL, 2 * w), D_MODEL ** -0.5)
    w_up = nrm(ks[16], (DEPTH_2, N_BRANCH, w, D_MODEL), w ** -0.5)
    w_out = nrm(ks[17], (DEPTH_2, D_MODEL, D_MODEL), D_MODEL ** -0.5)
    return {"x": x, "mem": mem, "positions": positions, "norm_pre": norm_pre, "norm_post": norm_post,
            "w_in": w_in, "b_igate": b_igate, "b_fgate": b_fgate, "conv_q": conv_q, "conv_k": conv_k,
            "gm_ln_g": gm_ln_g, "gm_ln_b": gm_ln_b, "gm_ws": gm_ws, "gm_bs": gm_bs,
            "mem_norm": mem_norm, "w_mem_kv": w_mem_kv, "w_up": w_up, "w_out": w_out}

def second_block(x, mem, positions, norm_pre, norm_post, w_in, b_igate, b_fgate, conv_q, conv_k,
              gm_ln_g, gm_ln_b, gm_ws, gm_bs, mem_norm, w_mem_kv, w_up, w_out):
    for l in range(DEPTH_2):
        x = hybrid_layer(x, mem, positions, norm_pre[l], norm_post[l], w_in[l], b_igate[l], b_fgate[l],
                         conv_q[l], conv_k[l], gm_ln_g[l], gm_ln_b[l], gm_ws[l], gm_bs[l],
                         mem_norm[l], w_mem_kv[l], w_up[l], w_out[l])
    return x


_first_inputs = second_inputs


def second_inputs(seed=0):
    import zlib

    import numpy as np

    out = dict(_first_inputs(seed))
    spreads = {}
    factors = {'b_igate': 8.0, 'gm_ln_g': 7.293, 'gm_ln_b': 6.949, 'gm_bs': 6.163, 'mem_norm': 8.0}
    for name, (base, spread) in spreads.items():
        noise = np.random.default_rng([zlib.crc32(name.encode()), seed]).standard_normal(out[name].shape)
        drawn = base * np.exp(spread * noise) if base else spread * noise
        out[name] = jnp.asarray(drawn.astype(out[name].dtype))
    for name, factor in factors.items():
        out[name] = (out[name] * factor).astype(out[name].dtype)
    return out


_narrow_inputs = second_inputs


def second_inputs(seed=0):
    out = dict(_narrow_inputs(seed))
    wider = {'b_igate': 12.0, 'gm_ln_g': 5.15, 'gm_ln_b': 5.38, 'gm_bs': 5.19}
    for name, times in wider.items():
        mean = out[name].mean()
        out[name] = (mean + times * (out[name] - mean)).astype(out[name].dtype)
    return out


def setup_inputs(seed=0):
    out = dict(first_inputs(seed))
    for name, value in second_inputs(seed + 1).items():
        if name != "x":
            out[name + "_2"] = value
    return out


def reference(
    x, meta_tokens, w_in, conv_w, conv_b, filt_w1, filt_b1, filt_w2, filt_b2, filt_w3,
    filt_freq, filt_skip, hyena_norm, lb_fwd, lb_bwd, hgrn_norm, w_out, norm_mix, norm_ffn,
    w_router_group, w_router_expert, w_gate, w_up, w_down, norm_final, mem_2, positions_2,
    norm_pre_2, norm_post_2, w_in_2, b_igate_2, b_fgate_2, conv_q_2, conv_k_2, gm_ln_g_2,
    gm_ln_b_2, gm_ws_2, gm_bs_2, mem_norm_2, w_mem_kv_2, w_up_2, w_out_2,
):
    x = first_block(
        x, meta_tokens, w_in, conv_w, conv_b, filt_w1, filt_b1, filt_w2, filt_b2, filt_w3,
        filt_freq, filt_skip, hyena_norm, lb_fwd, lb_bwd, hgrn_norm, w_out, norm_mix, norm_ffn,
        w_router_group, w_router_expert, w_gate, w_up, w_down, norm_final,
    )
    return second_block(
        x, mem_2, positions_2, norm_pre_2, norm_post_2, w_in_2, b_igate_2, b_fgate_2, conv_q_2,
        conv_k_2, gm_ln_g_2, gm_ln_b_2, gm_ws_2, gm_bs_2, mem_norm_2, w_mem_kv_2, w_up_2,
        w_out_2,
    )


_drawn_inputs = setup_inputs


def setup_inputs(seed=0):
    import zlib

    import numpy as np

    out = dict(_drawn_inputs(seed))
    spreads = {}
    factors = {'lb_bwd': 4.615,
     'b_fgate_2': 26.088,
     'hgrn_norm': 3.975,
     'filt_freq': 3.375,
     'hyena_norm': 2.772,
     'norm_ffn': 3.011}
    for name, (base, spread) in spreads.items():
        noise = np.random.default_rng([zlib.crc32(name.encode()), seed]).standard_normal(out[name].shape)
        drawn = base * np.exp(spread * noise) if base else spread * noise
        out[name] = jnp.asarray(drawn.astype(out[name].dtype))
    for name, factor in factors.items():
        out[name] = (out[name] * factor).astype(out[name].dtype)
    return out
```

```python
import math
from contextlib import ExitStack

import numpy as np
import concourse.bass as bass
from concourse import mybir

F32 = mybir.dt.float32
I32 = mybir.dt.int32
ALU = mybir.AluOpType
ACT = mybir.ActivationFunctionType
AX = mybir.AxisListType.X

P = 128
D = 1024
KD = D // P
SEQ = 256
META = 16
T = META + SEQ
HALF = D // 2
HY = 3 * HALF // P
HG = 5 * HALF // P
CH = 64
PADT = (-META) % CH
TP = T + PADT
NCH = TP // CH
NF = T
TW = [P, P, T - 2 * P]
NE, NG, EPG = 64, 8, 8
CAP = 32
GRP = 4
NGRP = NE // GRP
FE = HALF
LAYERS = 2
NH, HD = 4, 128
NC2 = SEQ // CH
NBR = 5
EPS = 1e-6
MAGIC = 12582912.0
TWO_PI_HI = 6.28125
TWO_PI_LO = 2 * math.pi - 6.28125
BIG = 1e30
SCALE = HD ** -0.5

WSLOT = 4096
RING = 6
RING1 = 4
SHARED_W = 28300


class Pack:

    def __init__(self):
        self.parts, self.at, self.n = [], {}, 0

    def add(self, name, a):
        a = np.asarray(a, np.float32)
        full = np.zeros((P, a.shape[1]), np.float32)
        full[: a.shape[0]] = a
        self.at[name] = (self.n, a.shape[1])
        self.parts.append(full)
        self.n += a.shape[1]

    def array(self):
        return np.ascontiguousarray(np.concatenate(self.parts, axis=1))


def tiles_of(a):
    out = np.zeros((3 * P, a.shape[1]), np.float32)
    out[: a.shape[0]] = a
    return out.reshape(3, P, -1).transpose(1, 0, 2).reshape(P, -1)


def shape_constants():
    c = Pack()
    i = np.arange(P)
    c.add("ident", np.eye(P))
    c.add("ones", np.ones((P, P)))
    c.add("before", i[:, None] < i[None, :])
    c.add("notbefore", i[:, None] >= i[None, :])
    rot = np.zeros((P, P))
    rot[np.arange(64) + 64, np.arange(64)] = -1
    rot[np.arange(64), np.arange(64) + 64] = 1
    c.add("rot", rot)
    mq = np.zeros((P, 2, SEQ))
    for kt in range(2):
        mq[:, kt] = (kt * P + i)[:, None] < np.arange(SEQ)[None, :]
    c.add("keymask", mq.reshape(P, -1))
    s = np.arange(P) % CH
    t = np.arange(CH)
    c.add("causal", s[:, None] <= t[None, :])
    c.add("anticausal", s[:, None] >= t[None, :])
    c.add("causal_neg", np.where(s[:, None] <= t[None, :], 0.0, -BIG))
    lg = np.log(1.0 - 2.0 ** (-5.0 - np.arange(NH)))
    c.add("rt_decay", (np.exp(lg[None, :, None] * np.abs(s[:, None, None] - t[None, None, :])) * SCALE).reshape(P, -1))
    c.add("rt_wq", np.broadcast_to(np.exp(lg[:, None] * (t + 1.0))[None], (P, NH, CH)).reshape(P, -1))
    c.add("rt_wend", np.exp(lg[None, :] * (CH - 1 - s)[:, None]) * SCALE)
    half = HD // 2
    inv = (np.float32(10000.0) ** (-(np.arange(half, dtype=np.float32) / np.float32(half)))).astype(np.float32)
    c.add("inv_freq", np.concatenate([inv, inv])[:, None])
    sel = np.zeros((4, 4, P))
    sel[np.arange(4), np.arange(4)] = 1
    c.add("sel", sel.reshape(4, -1))
    c.add("run", np.broadcast_to((np.arange(TP) % CH != 0)[None], (P, TP)))
    c.add("restart", np.broadcast_to(np.where(np.arange(SEQ) % CH, 0.0, -BIG)[None], (4, SEQ)))
    c.add("slots", np.broadcast_to(np.arange(CAP)[None], (P, CAP)))
    c.add("eight", np.broadcast_to(np.arange(8)[None], (P, 8)))
    c.add("eps", np.full((P, 1), EPS))
    c.add("zero", np.zeros((P, 1)))
    return c


def filter_constants():
    c = Pack()
    th = np.pi * (2 * np.arange(NF) + 1) / (2 * T)
    ang = np.arange(T)[:, None] * th[None, :]
    c.add("cos", tiles_of(np.cos(ang)))
    c.add("sin", tiles_of(np.sin(ang)))
    c.add("icos", tiles_of(np.cos(ang).T / T))
    c.add("isin", tiles_of(np.sin(ang).T / T))
    return c


def filter_features():
    c = Pack()
    f = np.float32
    pos = np.arange(T, dtype=f)
    t = (pos / f(T - 1)).astype(f)
    bands = np.linspace(1e-4, 15, 16, dtype=f)
    ang = (f(2.0 * math.pi / T) * pos[:, None] * bands[None, :]).astype(f)
    z = np.concatenate([t[:, None], np.cos(ang), -np.sin(ang)], axis=-1)
    c.add("features", z.T)
    deltas = np.abs(np.linspace(math.log(1e-2) / 1.5, math.log(1e-2) / 0.3, HALF, dtype=f))
    c.add("window", tiles_of(np.exp(-t[:, None] * deltas[None, :])))
    return c


def cols(v):
    v = np.asarray(v)
    return v.reshape(-1, P).T


def first_params(a):
    c = Pack()
    c.add("norm_mix", cols(a["norm_mix"]))
    c.add("norm_ffn", cols(a["norm_ffn"]))
    c.add("norm_final", cols(a["norm_final"]))
    c.add("conv_w", cols(a["conv_w"]))
    c.add("conv_b", cols(a["conv_b"]))
    c.add("skip", cols(a["filt_skip"]))
    c.add("hyena_norm", cols(a["hyena_norm"]))
    c.add("lb", np.concatenate([cols(a["lb_fwd"]), cols(a["lb_bwd"])], axis=1))
    c.add("hgrn_norm", cols(a["hgrn_norm"]))
    c.add("filt_b1", np.asarray(a["filt_b1"]).T)
    c.add("filt_b2", np.asarray(a["filt_b2"]).T)
    c.add("filt_freq", np.asarray(a["filt_freq"]).T)
    return c


def layer_params(a, l):
    c = Pack()
    c.add("norm_pre", cols(a["norm_pre_2"][l]))
    c.add("norm_post", cols(a["norm_post_2"][l]))
    c.add("mem_norm", cols(a["mem_norm_2"][l]))
    c.add("conv_q", cols(a["conv_q_2"][l]))
    c.add("conv_k", cols(a["conv_k_2"][l]))
    c.add("b_i", np.asarray(a["b_igate_2"][l])[:, None])
    c.add("b_f", np.asarray(a["b_fgate_2"][l])[:, None])
    return c


class Chain:

    def __init__(self, eng, sem):
        self.eng, self.sem, self.base, self.n = eng, sem, 0, 0

    def tick(self, ins):
        self.n += 1
        ins.then_inc(self.sem, 1)

    def link(self, ins):
        self.tick(ins)
        self.eng.wait_ge(self.sem, self.base + self.n)

    def turn(self, i, per, start):
        self.base, self.n = start + i * per, 0

    def end_turn(self, per):
        assert self.n == per, (self.sem, self.n)


class Layout:

    def __init__(self, arena, at=0):
        self.arena, self.at = arena, at

    def take(self, *dims):
        n = int(np.prod(dims))
        v = self.arena[:, self.at:self.at + n]
        self.at += n
        if len(dims) == 2:
            v = v.rearrange("p (a b) -> p a b", b=dims[1])
        elif len(dims) == 3:
            v = v.rearrange("p (a b c) -> p a b c", b=dims[1], c=dims[2])
        return v



def norm_squares(act, src, squares, done):
    act.activation(squares, src, ACT.Square).then_inc(done, 1)


def norm_sum(pe, ones, squares, n, out, done):
    for k in range(n):
        last = pe.matmul(out, ones, squares[:, k, :], start=(k == 0), stop=(k == n - 1))
    last.then_inc(done, 1)


def norm_rstd(act, chain, out, total, width, eps, done):
    chain.link(act.activation(out, total, ACT.Ln, bias=eps, scale=1.0 / width))
    act.activation(out, out, ACT.Exp, scale=-0.5).then_inc(done, 1)


def build_program(nc, d, spot, stop_after=None):
    with ExitStack() as ctx:
        named = {}

        def sem(name):
            if name not in named:
                named[name] = nc.alloc_semaphore(name)
            return named[name]

        ring = ctx.enter_context(nc.sbuf_tensor("ring", [P, RING, WSLOT], F32))
        arena = ctx.enter_context(nc.sbuf_tensor("arena", [P, SHARED_W], F32))
        rounds = ctx.enter_context(nc.sbuf_tensor("rounds", [P, 2], I32))
        pos_i = ctx.enter_context(nc.sbuf_tensor("pos_i", [P, SEQ], I32))
        ps = ctx.enter_context(nc.psum_tensor("ps", [P, 8, 512], F32))

        lay = Layout(arena)
        n_const = sum(w for _, w in spot["shape"].values())
        const = lay.take(n_const)
        param1 = lay.take(sum(w for _, w in spot["first"].values()))
        lb = lay.take(2, 2, 4)
        h = lay.take(KD, T)
        a = lay.take(KD, T)
        rstd = lay.take(T)
        free_at = lay.at

        def C(name, rows=P):
            at, w = spot["shape"][name]
            return const[0:rows, at:at + w]

        def P1(name, i=None, rows=P):
            at, w = spot["first"][name]
            return param1[0:rows, at:at + w] if i is None else param1[0:rows, at + i:at + i + 1]

        ident, ones, eps = C("ident"), C("ones"), C("eps")

        m1 = Layout(arena, free_at)
        four = m1.take(4, 3, NF)
        cosm, sinm, icos, isin = (four[:, j] for j in range(4))
        conv = m1.take(HY, T)
        hg = m1.take(HG, TP)
        assert m1.at <= SHARED_W, m1.at
        scratch = ring[:, RING1:RING, :].rearrange("p a b -> p (a b)")
        m2 = Layout(scratch)
        filt = m2.take(3, 4, HALF)
        padded = m2.take(4, T + 2)
        sig = m2.take(2, T)
        padded4 = padded.rearrange("p a b -> p (a b)")[:, 0:4 * T].rearrange("p (a b) -> p a b", b=T)
        assert m2.at <= 2 * WSLOT

        def xr(v):
            return v.rearrange("p a b -> p (a b)")
        feat = hg[:, :, :].rearrange("p a b -> p (a b)")
        m3 = Layout(feat)
        zT = m3.take(T)
        window = m3.take(3, HALF)
        fw1 = m3.take(64)
        fw2 = m3.take(64)
        fw3 = m3.take(4, HALF)
        hid = m3.take(T)
        wrap = m3.take(T)
        assert m3.at <= HG * TP

        UNITS = [("mem_k", "strip"), ("mem_v", "nat"), ("xa_q", "strip"), ("xa_z", "strip"),
                 ("sb_q", "strip"), ("sb_k", "strip"), ("sb_v", "nat"), ("sb_z", "strip"),
                 ("ml_q", "strip"), ("ml_k", "strip"), ("ml_v", "nat"), ("ml_o", "strip"), ("ml_z", "strip"),
                 ("gm_u", "strip"), ("gm_v", "nat"), ("gm_z", "strip"),
                 ("rt_q", "strip"), ("rt_k", "strip"), ("rt_v", "nat"), ("rt_z", "strip")]
        UNIT_AT = {n: i for i, (n, _) in enumerate(UNITS)}
        JOB_AT, at = {}, 0
        JOB_ENDS = []
        for n, kind in UNITS:
            JOB_AT[n] = at
            at += 4 if kind == "strip" else 2
            JOB_ENDS.append(at)
        PAIRS = KD * NBR
        MERGE_AT = at
        for _ in range(PAIRS // 2):
            at += 4
            JOB_ENDS.append(at)
        OUT_AT = at
        for _ in range(2):
            at += 4
            JOB_ENDS.append(at)
        JOBS = at
        NU = len(JOB_ENDS)
        assert JOBS % 2 == 0 and NU % RING == 0

        ly = Layout(arena, free_at)
        param2 = ly.take(sum(w for _, w in spot["layer"].values()))
        w_if = ly.take(KD, 8)
        rope = ly.take(2, SEQ)
        y_all = ly.take(NBR, 4, SEQ)
        esig = ly.take(2, SEQ)
        gm_ws = ly.take(4, P)
        gm_rows = ly.take(3, HALF)
        mean_of = ly.take(P)
        ra = ly.at
        rb = ra + 4200
        rw = rb + 3080
        la = Layout(arena, ra)
        xa_q = la.take(4, SEQ)
        xa_l = la.take(2, 2, SEQ)
        xa_t = la.take(2, 2, SEQ)
        xa_s = la.take(8, 4)
        la = Layout(arena, ra)
        ml_v = la.take(2, NH, HD + 1)
        ml_q, ml_k, ml_o = la.take(4, SEQ), la.take(4, SEQ), la.take(4, SEQ)
        assert la.at <= rb
        ml_qk = arena[:, ra + 2 * NH * (HD + 1):ra + 2 * NH * (HD + 1) + 8 * SEQ]
        la = Layout(arena, ra)
        merged = la.take(KD, SEQ)
        post_sq = la.take(KD, SEQ)
        assert la.at <= rb
        post = y_all.rearrange("p a b c -> p (a b c)")[:, 0:KD * SEQ].rearrange("p (a b) -> p a b", b=SEQ)
        l2 = Layout(arena, rb)
        b_q, b_k, b_v = l2.take(4, SEQ), l2.take(4, SEQ), l2.take(2, HALF)
        assert l2.at <= rw
        l2 = Layout(arena, rb)
        mem_t = l2.take(KD, SEQ)
        lw = Layout(arena, rw)
        mem_k, mem_v = lw.take(4, SEQ), lw.take(2, HALF)
        mem_sq = lw.take(KD, SEQ)
        lw = Layout(arena, rw + 2 * KD * P)
        sb_z, sb_sp, sb_w = lw.take(2, 2 * SEQ), lw.take(2 * SEQ), lw.take(2 * SEQ)
        keyneg = lw.take(2 * SEQ)
        assert lw.at <= SHARED_W, (lw.at, SHARED_W)
        lw = Layout(arena, rw)
        wide = lw.take(8, SEQ + 4)
        wide_flat = arena[:, rw:rw + 8 * SEQ]
        lw = Layout(arena, rw)
        ml_rows = lw.take(776)
        ml_bc = lw.take(776)
        ml_d, ml_s = lw.take(2, CH), lw.take(2, CH)
        ml_st, ml_nb = lw.take(3, HD + 1), lw.take(3, P)
        ml_kw, ml_qd = lw.take(2, P), lw.take(SEQ)
        ml_col = lw.take(16)
        ml_g = lw.take(5, SEQ)
        ml_c = lw.take(6, 8)
        assert lw.at <= SHARED_W, (lw.at, SHARED_W)
        lw = Layout(arena, rw)
        gm_st, gm_mv, gm_x = lw.take(2, 8), lw.take(2, 2), lw.take(2, P)
        lw = Layout(arena, rw)
        rt_t = lw.take(2, 2 * SEQ)
        rt_s, rt_st = lw.take(2, CH), lw.take(3, P)
        rt_kw, rt_qd = lw.take(2, P), lw.take(SEQ)
        hn_sq = lw.take(4, SEQ)
        hn_r = lw.take(4, SEQ)
        assert lw.at <= SHARED_W
        hn_mem = esig[:, 0, :]
        JEXP_AT, at = {}, 0
        for n in ("xa_z", "sb_z", "ml_o", "ml_z", "gm_z", "rt_z"):
            JEXP_AT[n] = at
            at += 4
        JEXPS = at
        ACT_LINKS = 17
        DVE_LINKS = 281

        def P2(name, i=0, rows=P):
            at, w = spot["layer"][name]
            return param2[0:rows, at + i:at + i + 1]

        def halves(v, par):
            return v.rearrange("p (a r t) -> p a r t", r=2, t=CH)[:, :, par, :]

        def evacuated(eng, l, j):
            eng.wait_ge(sem(f"job_out{j % 2}"), l * (JOBS // 2) + j // 2 + 1)

        def unit_evacuated(eng, l, name):
            j = JOB_ENDS[UNIT_AT[name]]
            evacuated(eng, l, j - 2)
            evacuated(eng, l, j - 1)

        def layers_sync(sp):
            sp.dma_start(pos_i[:, :], d["positions"].partition_broadcast(P)).then_inc(sem("in_pos"), 16)
            with sp.Fori(0, LAYERS) as l:
                w2 = d["w_layers"]
                for u in range(NU):
                    s = u % RING
                    if u < RING:
                        if u == 0:
                            sp.wait_ge(sem("slots_open"), l + 1)
                    else:
                        sp.wait_ge(sem("job"), l * JOBS + JOB_ENDS[u - RING])
                    width = 3072 if len(UNITS) <= u < len(UNITS) + PAIRS // 2 else WSLOT
                    sp.dma_start(ring[:, s, 0:width], w2[bass.ds(l * NU + u, 1), :, 0:width].rearrange("a p n -> (a p) n")).then_inc(sem(f"w3_in{s}"), 16)
                    if u == RING - 1:
                        sp.wait_ge(sem("layer_open"), l + 1)
                        for dst, name in ((param2, "param2"), (xr(w_if), "w_if"), (xr(gm_ws), "gm_ws")):
                            sp.dma_start(dst, d[name][bass.ds(l, 1)].rearrange("a p n -> (a p) n")).then_inc(sem("in_layer"), 16)
                        sp.dma_start(xr(mem_t), d["mem"]).then_inc(sem("in_mem"), 16)
                        sp.dma_start(xr(gm_rows), d["gm_rows"][bass.ds(l, 1), :].rearrange("a n -> (a n)").partition_broadcast(P)).then_inc(sem("in_rows"), 16)
            sp.wait_ge(sem("x_out"), LAYERS * 1)
            sp.dma_start(d["out"].rearrange("(k p) t -> p k t", p=P), x_tok).then_inc(sem("out"), 16)
            sp.wait_ge(sem("out"), 16)

        def layers_pe(pe):
            pe.sem_inc(sem("slots_open"), 1)
            pe.sem_inc(sem("layer_open"), 1)
            with pe.Fori(0, LAYERS) as l:
                def w(name, per, k):
                    pe.wait_ge(sem(name), l * per + k)

                def unit_in(u):
                    w(f"w3_in{u % RING}", 16 * NU // RING, 16 * (u // RING + 1))

                def bank_free(j):
                    w(f"job_out{j % 2}", JOBS // 2, j // 2)

                def project(name, lhs):
                    u = UNIT_AT[name]
                    unit_in(u)
                    t = ring[:, u % RING, :].rearrange("p (s k m) -> p s k m", s=4, k=KD)
                    if UNITS[u][1] == "strip":
                        for s in range(4):
                            j = JOB_AT[name] + s
                            bank_free(j)
                            for k in range(KD):
                                last = pe.matmul(ps[:, j % 2, 0:SEQ], t[:, s, k, :], lhs[:, k, :], start=(k == 0), stop=(k == KD - 1))
                            last.then_inc(sem("job"), 1)
                    else:
                        for m in range(2):
                            j = JOB_AT[name] + m
                            bank_free(j)
                            for k in range(KD):
                                last = pe.matmul(ps[:, j % 2, :], lhs[:, k, m * P:(m + 1) * P], t[:, :, k, :], start=(k == 0), stop=(k == KD - 1))
                            last.then_inc(sem("job"), 1)

                w("mem_sq", 1, 1)
                norm_sum(pe, ones, mem_sq, KD, ps[:, 2, 0:SEQ], sem("ss_mem"))
                w("sq_pre", 1, 1)
                norm_sum(pe, ones, an, KD, ps[:, 3, 0:SEQ], sem("ss_pre"))
                w("mem_n", KD, KD)
                project("mem_k", mem_t)
                project("mem_v", mem_t)
                w("pre_n", KD, KD)
                for n in ("xa_q", "xa_z", "sb_q", "sb_k", "sb_v", "sb_z"):
                    project(n, an)

                unit_evacuated(pe, l, "xa_q")

                def xa_logits(hd):
                    if hd >= 2:
                        w("xa_e", 2 * NH, 2 * hd - 2)
                    for st in range(2):
                        last = pe.matmul(ps[:, 2 + hd % 2, st * SEQ:(st + 1) * SEQ], xa_q[:, hd, st * P:(st + 1) * P], mem_k[:, hd, :], start=True, stop=True)
                    last.then_inc(sem("xl_ps"), 1)
                xa_logits(0)
                for hd in range(NH):
                    if hd + 1 < NH:
                        xa_logits(hd + 1)
                    w("xa_p", NH, hd + 1)
                    if hd >= 2:
                        w("xa_t", NH, hd - 1)
                    for st in range(2):
                        for mt in range(2):
                            last = pe.transpose(ps[:, 4 + hd % 2, mt * SEQ + st * P:mt * SEQ + (st + 1) * P],
                                                xa_l[:, hd % 2, st, mt * P:(mt + 1) * P], ident)
                    last.then_inc(sem("xt_ps"), 1)
                    w("xa_t", NH, hd + 1)
                    if hd >= 2:
                        w("xa_y", NH, hd - 1)
                    for mt in range(2):
                        last = pe.matmul(ps[:, 6 + hd % 2, 0:SEQ], mem_v[:, mt, hd * P:(hd + 1) * P], xa_t[:, hd % 2, mt, :], start=(mt == 0), stop=(mt == 1))
                    last.then_inc(sem("xo_ps"), 1)

                unit_evacuated(pe, l, "sb_z")

                def sb_logits(hd):
                    w("sb_zc", NH, hd - 1) if hd >= 2 else None
                    for kt in range(2):
                        last = pe.matmul(ps[:, 2 + hd % 2, kt * SEQ:(kt + 1) * SEQ], b_k[:, hd, kt * P:(kt + 1) * P], b_q[:, hd, :], start=True, stop=True)
                    last.then_inc(sem("sz_ps"), 1)
                sb_logits(0)
                for hd in range(NH):
                    if hd + 1 < NH:
                        sb_logits(hd + 1)
                    w("sb_sp", NH, hd + 1)
                    if hd == 0:
                        w("xa_y", NH, NH)
                    bank = ps[:, 4 + hd % 2, :]
                    pe.matmul(bank[:, 0:SEQ], C("notbefore"), sb_sp[:, 0:SEQ], start=True, stop=False)
                    pe.matmul(bank[:, 0:SEQ], ones, sb_sp[:, SEQ:2 * SEQ], start=False, stop=True)
                    pe.matmul(bank[:, SEQ:2 * SEQ], C("notbefore"), sb_sp[:, SEQ:2 * SEQ], start=True, stop=True).then_inc(sem("sr_ps"), 1)
                    w("sb_e", NH, hd + 1)
                    if hd >= 2:
                        w("sb_y", NH, hd - 1)
                    for kt in range(2):
                        last = pe.matmul(ps[:, 6 + hd % 2, 0:SEQ], b_v[:, kt, hd * P:(hd + 1) * P], sb_w[:, kt * SEQ:(kt + 1) * SEQ], start=(kt == 0), stop=(kt == 1))
                    last.then_inc(sem("so_ps"), 1)

                for n in ("ml_q", "ml_k", "ml_v", "ml_o", "ml_z"):
                    project(n, an)
                w("in_layer", 48, 48)
                w("sb_y", NH, NH)
                for i in range(2):
                    for k in range(KD):
                        last = pe.matmul(ps[0:4, 2 + i, 0:SEQ], w_if[:, k, 4 * i:4 * i + 4], an[:, k, :], start=(k == 0), stop=(k == KD - 1))
                last.then_inc(sem("mg_ps"), 1)
                for n in ("gm_u", "gm_v", "gm_z"):
                    project(n, an)
                w("mg_e", 1, 1)
                for i, row in enumerate((ml_g[0:4, 0, :], ml_g[0:4, 2, :])):
                    for tt in range(2):
                        last = pe.matmul(ps[:, 3, 8 * i + 4 * tt:8 * i + 4 * tt + 4], row[:, tt * P:(tt + 1) * P], ident[0:4, 0:4], start=True, stop=True)
                last.then_inc(sem("mc_ps"), 1)
                w("ml_col", 1, 1)
                w("ml_qk", 1, 1)
                unit_evacuated(pe, l, "ml_z")
                for hd in range(NH):
                    if hd >= 1:
                        w("ml_h", NH, hd)
                    sel = C("sel", 4).rearrange("p (h m) -> p h m", h=4)[:, hd, :]
                    pe.matmul(ps[:, 2, :], sel, ml_rows[0:4, 0:512], start=True, stop=True)
                    pe.matmul(ps[:, 3, 0:264], sel, ml_rows[0:4, 512:776], start=True, stop=True).then_inc(sem("mb_ps"), 1)
                    for c in range(NC2):
                        par, tt = c % 2, c // 2
                        last = pe.matmul(ps[CH * par:CH * (par + 1), 4, tt * CH:(tt + 1) * CH], ml_k[:, hd, c * CH:(c + 1) * CH],
                                         ml_q[:, hd, c * CH:(c + 1) * CH], start=True, stop=True)
                    last.then_inc(sem("ms_ps"), 1)
                    for tt in range(2):
                        last = pe.transpose(ps[:, 5, tt * P:(tt + 1) * P], ml_k[:, hd, tt * P:(tt + 1) * P], ident)
                    last.then_inc(sem("mk_ps"), 1)
                    w("ml_kw", 2 * NH, 2 * hd + 2)
                    for c in (0, 2, 1):
                        par, tt = c % 2, c // 2
                        last = pe.matmul(ps[:, 6 + par, tt * (HD + 1):(tt + 1) * (HD + 1)], ml_kw[CH * par:CH * (par + 1), tt, :],
                                         ml_v[CH * par:CH * (par + 1), tt, hd, :], start=True, stop=True)
                    last.then_inc(sem("mu_ps"), 1)
                    w("ml_bc", 2 * NH, 2 * hd + 2)
                    w("ml_s", NH, hd + 1)
                    w("ml_st", NH, hd + 1)
                    w("ml_qd", NH, hd + 1)
                    for par in range(2):
                        for tt in range(2):
                            c = 2 * tt + par
                            num = ps[:, 2 + par, tt * CH:(tt + 1) * CH]
                            den = ps[:, 2 + par, P + tt * CH:P + (tt + 1) * CH]
                            s = ml_s[CH * par:CH * (par + 1), tt, :]
                            pe.matmul(num, ml_v[CH * par:CH * (par + 1), tt, hd, 0:HD], s, start=(tt == 0), stop=False, skip_group_check=True)
                            last = pe.matmul(den, ones[CH * par:CH * (par + 1), :], s, start=False, stop=False, skip_group_check=True)
                            if c:
                                qd = ml_qd[:, c * CH:(c + 1) * CH]
                                pe.matmul(num, ml_st[:, c - 1, 0:HD], qd, start=False, stop=False, skip_group_check=True)
                                last = pe.matmul(den, ml_nb[:, c - 1, :], qd, start=False, stop=False, skip_group_check=True)
                    last.then_inc(sem("mo_ps"), 1)

                def head_norm(src, tag):
                    for i in range(2):
                        last = pe.matmul(ps[:, 2 + i, :], mean_of, xr(src[:, 2 * i:2 * i + 2, :]), start=True, stop=True)
                    last.then_inc(sem(f"{tag}_mean"), 1)
                    w(f"{tag}_sq", 1, 1)
                    for i in range(2):
                        last = pe.matmul(ps[:, 4 + i, :], mean_of, xr(hn_sq[:, 2 * i:2 * i + 2, :]), start=True, stop=True)
                    last.then_inc(sem(f"{tag}_var"), 1)

                w("ml_h", NH, NH)
                head_norm(ml_q, "mlh")

                w("gm_n", 1, 1)
                w("mlh_c", 1, 1)
                for g in range(4):
                    for nb in range(2):
                        last = pe.matmul(ps[:, 2 + g // 2, (g % 2) * SEQ + nb * P:(g % 2) * SEQ + (nb + 1) * P], b_v[:, nb, g * P:(g + 1) * P],
                                         gm_ws[:, g, :], start=True, stop=True)
                last.then_inc(sem("gm_ps"), 1)

                for n in ("rt_q", "rt_k", "rt_v", "rt_z"):
                    project(n, an)
                unit_evacuated(pe, l, "rt_z")
                w("gm_y", 4, 4)
                w("mlh_r", 1, 1)
                for i, src in enumerate((b_q, b_q, b_k, b_k)):
                    pe.matmul(ps[:, 2 + i, :], C("rot"), xr(src[:, 2 * (i % 2):2 * (i % 2) + 2, :]), start=True, stop=True).then_inc(sem("rr_ps"), 1)
                w("rt_rot", 4, 4)
                for hd in range(NH):
                    if hd >= 1:
                        w("rt_s", NH, hd)
                        w("rt_kw", NH, hd)
                    for c in range(NC2):
                        par, tt = c % 2, c // 2
                        last = pe.matmul(ps[CH * par:CH * (par + 1), 2, tt * CH:(tt + 1) * CH], b_k[:, hd, c * CH:(c + 1) * CH],
                                         b_q[:, hd, c * CH:(c + 1) * CH], start=True, stop=True)
                    last.then_inc(sem("rs_ps"), 1)
                    for tt in range(2):
                        last = pe.transpose(ps[:, 3, tt * P:(tt + 1) * P], b_k[:, hd, tt * P:(tt + 1) * P], ident)
                    last.then_inc(sem("rk_ps"), 1)
                    w("rt_kw", NH, hd + 1)
                    if hd >= 1:
                        w("rt_st", NH, hd)
                    for c in (0, 2, 1):
                        par, tt = c % 2, c // 2
                        last = pe.matmul(ps[:, 6 + par, tt * P:(tt + 1) * P], rt_kw[CH * par:CH * (par + 1), tt, :],
                                         b_v[CH * par:CH * (par + 1), tt, hd * P:(hd + 1) * P], start=True, stop=True)
                    last.then_inc(sem("ru_ps"), 1)
                    w("rt_s", NH, hd + 1)
                    w("rt_st", NH, hd + 1)
                    w("rt_qd", NH, hd + 1)
                    if hd >= 1:
                        w("rt_h", 2 * NH, 2 * hd)
                    for par in range(2):
                        for tt in range(2):
                            c = 2 * tt + par
                            out = ps[:, 4 + par, tt * CH:(tt + 1) * CH]
                            last = pe.matmul(out, b_v[CH * par:CH * (par + 1), tt, hd * P:(hd + 1) * P], rt_s[CH * par:CH * (par + 1), tt, :],
                                             start=(tt == 0), stop=False, skip_group_check=True)
                            if c:
                                last = pe.matmul(out, rt_st[:, c - 1, :], rt_qd[:, c * CH:(c + 1) * CH], start=False, stop=False, skip_group_check=True)
                    last.then_inc(sem("ro_ps"), 1)
                w("rt_h", 2 * NH, 2 * NH)
                head_norm(b_q, "rth")

                w("xa_y", NH, NH)
                w("ml_y", 1, 1)
                for p in range(PAIRS):
                    c, n = p // NBR, p % NBR
                    u = len(UNITS) + p // 2
                    if p % 2 == 0:
                        unit_in(u)
                    if n == 3 and c == 0:
                        w("rt_y", 1, 1)
                    t = ring[:, u % RING, (p % 2) * 1536:(p % 2 + 1) * 1536].rearrange("p (k m) -> p k m", m=P)
                    j = MERGE_AT + 2 * p
                    bank_free(j)
                    for k in range(KD):
                        last = pe.matmul(ps[:, j % 2, 0:SEQ], t[:, k, :], an[:, k, :], start=(k == 0), stop=(k == KD - 1))
                    last.then_inc(sem("job"), 1)
                    bank_free(j + 1)
                    for k in range(4):
                        last = pe.matmul(ps[:, (j + 1) % 2, 0:SEQ], t[:, KD + k, :], y_all[:, n, k, :], start=(k == 0), stop=(k == 3))
                    last.then_inc(sem("job"), 1)
                w("merged", PAIRS, PAIRS)
                for i in range(KD):
                    u = len(UNITS) + PAIRS // 2 + i // 4
                    if i % 4 == 0:
                        unit_in(u)
                    t = ring[:, u % RING, :].rearrange("p (s k m) -> p s k m", s=4, k=KD)
                    j = OUT_AT + i
                    bank_free(j)
                    for k in range(KD):
                        last = pe.matmul(ps[:, j % 2, 0:SEQ], t[:, i % 4, k, :], merged[:, k, :], start=(k == 0), stop=(k == KD - 1))
                    last.then_inc(sem("job"), 1)
                w("post_sq", 1, 1)
                pe.sem_inc(sem("slots_open"), 1)
                norm_sum(pe, ones, post_sq, KD, ps[:, 2, 0:SEQ], sem("ss_post"))
                w("x_out", 1, 1)
                pe.sem_inc(sem("layer_open"), 1)

        def layers_act(act):
            act.wait_ge(sem("rope_arg"), 1)
            act.activation(xr(rope), xr(rope), ACT.Sin).then_inc(sem("rope"), 1)
            lc = Chain(act, sem("act_layer_chain"))
            per = ACT_LINKS
            with act.Fori(0, LAYERS) as l:
                lc.turn(l, per, 0)
                link = lc.link

                def w(name, per, k):
                    act.wait_ge(sem(name), l * per + k)

                def take(name, dst, scale=None):
                    kind = UNITS[UNIT_AT[name]][1]
                    for i in range(4 if kind == "strip" else 2):
                        j = JOB_AT[name] + i
                        w("job", JOBS, j + 1)
                        src = ps[:, j % 2, 0:SEQ] if kind == "strip" else ps[:, j % 2, :]
                        if name == "ml_v":
                            src = src.rearrange("p (h n) -> p h n", h=NH)
                        if scale:
                            ins = act.mul(dst(i), src, scale)
                        else:
                            ins = act.copy(dst(i), src)
                        ins.then_inc(sem(f"job_out{j % 2}"), 1)

                def exps(name):
                    for i in range(4):
                        j = JOB_AT[name] + i
                        w("job", JOBS, j + 1)
                        act.activation(esig[:, j % 2, :], ps[:, j % 2, 0:SEQ], ACT.Exp, scale=-1.0).then_inc(sem("jexp"), 1)

                w("in_mem", 16, 16)
                norm_squares(act, mem_t, mem_sq, sem("mem_sq"))
                w("layer_open", 1, 1)
                norm_squares(act, x_tok, an, sem("sq_pre"))
                w("ss_mem", 1, 1)
                norm_rstd(act, lc, hn_mem, ps[:, 2, 0:SEQ], D, eps, sem("mem_r"))
                w("ss_pre", 1, 1)
                norm_rstd(act, lc, rstd[:, 0:SEQ], ps[:, 3, 0:SEQ], D, eps, sem("pre_r"))
                take("mem_k", lambda i: mem_k[:, i, :])
                take("mem_v", lambda i: mem_v[:, i, :])
                take("xa_q", lambda i: xa_q[:, i, :])
                exps("xa_z")
                take("sb_q", lambda i: b_q[:, i, :], SCALE)
                take("sb_k", lambda i: b_k[:, i, :])
                take("sb_v", lambda i: b_v[:, i, :])
                exps("sb_z")
                for hd in range(NH):
                    w("xa_max", NH, hd + 1)
                    for st in range(2):
                        act.activation(xa_l[:, hd % 2, st, :], ps[:, 2 + hd % 2, st * SEQ:(st + 1) * SEQ], ACT.Exp, scale=SCALE,
                                       bias=xa_s[:, 2 * hd, st:st + 1], accum_out=xa_s[:, 2 * hd + 1, st:st + 1]).then_inc(sem("xa_e"), 1)
                    w("xt_ps", NH, hd + 1)
                    if hd >= 2:
                        w("xo_ps", NH, hd - 1)
                    act.copy(xr(xa_t[:, hd % 2]), ps[:, 4 + hd % 2, :]).then_inc(sem("xa_t"), 1)
                for hd in range(NH):
                    w("sz_ps", NH, hd + 1)
                    if hd >= 2:
                        w("sb_d", NH, hd - 1)
                    act.copy(sb_z[:, hd % 2, :], ps[:, 2 + hd % 2, :]).then_inc(sem("sb_zc"), 1)
                    w("sb_zc", NH, hd + 1)
                    if hd >= 1:
                        w("sr_ps", NH, hd)
                    link(act.activation(sb_sp, sb_z[:, hd % 2, :], ACT.Abs))
                    link(act.activation(sb_sp, sb_sp, ACT.Exp, scale=-1.0))
                    act.activation(sb_sp, sb_sp, ACT.Ln, bias=ones[:, 0:1]).then_inc(sem("sb_ln"), 1)
                    w("sb_d", NH, hd + 1)
                    act.activation(sb_w, sb_w, ACT.Exp).then_inc(sem("sb_e"), 1)
                w("ml_pads", 1, 1)
                take("ml_q", lambda i: wide[:, i, 3:3 + SEQ])
                take("ml_k", lambda i: wide[:, 4 + i, 3:3 + SEQ])
                take("ml_v", lambda i: ml_v[:, i, :, 0:HD])
                exps("ml_o")
                exps("ml_z")
                w("ml_conv", 1, 1)
                act.activation(wide_flat, ml_qk, ACT.Exp, scale=-1.0).then_inc(sem("ml_qke"), 1)
                w("mg_x", 1, 1)
                link(act.activation(ml_g[0:4, 2, :], ml_g[0:4, 1, :], ACT.Abs))
                link(act.activation(ml_g[0:4, 2, :], ml_g[0:4, 2, :], ACT.Exp, scale=-1.0))
                act.activation(ml_g[0:4, 2, :], ml_g[0:4, 2, :], ACT.Ln, bias=ones[0:4, 0:1]).then_inc(sem("mg_l"), 1)
                take("gm_u", lambda i: b_q[:, i, :])
                take("gm_v", lambda i: b_v[:, i, :])
                exps("gm_z")
                w("mg_r", 1, 1)
                link(act.activation(ml_rows[0:4, SEQ:776], ml_rows[0:4, SEQ:776], ACT.Exp))
                act.activation(ml_g[0:4, 2, :], ml_g[0:4, 2, :], ACT.Exp).then_inc(sem("mg_e"), 1)
                w("mc_ps", 1, 1)
                act.copy(ml_col, ps[:, 3, 0:16]).then_inc(sem("ml_col"), 1)
                for hd in range(NH):
                    w("mb_ps", NH, hd + 1)
                    if hd >= 1:
                        w("ml_h", NH, hd)
                    act.copy(ml_bc[:, 0:512], ps[:, 2, :]).then_inc(sem("ml_bc"), 1)
                    act.copy(ml_bc[:, 512:776], ps[:, 3, 0:264]).then_inc(sem("ml_bc"), 1)
                    w("ml_dx", 2 * NH, 2 * hd + 2)
                    for c in range(NC2):
                        par, tt = c % 2, c // 2
                        v = ml_d[CH * par:CH * (par + 1), tt, :]
                        act.activation(v, v, ACT.Exp, bias=ml_col[CH * par:CH * (par + 1), tt * 4 + hd:tt * 4 + hd + 1]).then_inc(sem("ml_de"), 1)

                def head_norm(src, tag):
                    w(f"{tag}_c", 1, 1)
                    act.activation(xr(hn_sq), xr(src), ACT.Square).then_inc(sem(f"{tag}_sq"), 1)
                    w(f"{tag}_var", 1, 1)
                    link(act.activation(xr(hn_r), ps[:, 4:6, :].rearrange("p a b -> p (a b)"), ACT.Ln, bias=eps))
                    act.activation(xr(hn_r), xr(hn_r), ACT.Exp, scale=-0.5).then_inc(sem(f"{tag}_r"), 1)

                head_norm(ml_q, "mlh")
                unit_evacuated(act, l, "gm_v")
                act.activation(xr(b_q), xr(b_q), ACT.Gelu_apprx_tanh).then_inc(sem("gm_gelu"), 1)
                act.activation(xr(b_v), xr(b_v), ACT.Gelu_apprx_tanh).then_inc(sem("gm_gelu"), 1)
                w("gm_var", 1, 1)
                link(act.activation(gm_mv[:, :, 1], gm_mv[:, :, 1], ACT.Ln, bias=eps))
                act.activation(gm_mv[:, :, 1], gm_mv[:, :, 1], ACT.Exp, scale=-0.5).then_inc(sem("gm_r"), 1)
                w("gm_y", 4, 4)
                take("rt_q", lambda i: b_q[:, i, :])
                take("rt_k", lambda i: b_k[:, i, :])
                take("rt_v", lambda i: b_v[:, i, :])
                exps("rt_z")
                head_norm(b_q, "rth")
                for p in range(PAIRS):
                    j = MERGE_AT + 2 * p
                    w("job", JOBS, j + 1)
                    if p >= 2:
                        w("merged", PAIRS, p - 1)
                    act.activation(esig[:, p % 2, :], ps[:, j % 2, 0:SEQ], ACT.Exp, scale=-1.0).then_inc(sem(f"job_out{j % 2}"), 1)
                for i in range(KD):
                    j = OUT_AT + i
                    w("job", JOBS, j + 1)
                    act.copy(post[:, i, :], ps[:, j % 2, 0:SEQ]).then_inc(sem(f"job_out{j % 2}"), 1)
                evacuated(act, l, JOBS - 2)
                evacuated(act, l, JOBS - 1)
                norm_squares(act, xr(post), xr(post_sq), sem("post_sq"))
                w("ss_post", 1, 1)
                norm_rstd(act, lc, rstd[:, 0:SEQ], ps[:, 2, 0:SEQ], D, eps, sem("post_r"))
                lc.end_turn(per)

        def layers_dve(dve):
            vc = Chain(dve, sem("dve_layer_chain"))
            link, tick = vc.link, vc.tick
            dve.wait_ge(sem("in_pos"), 16)
            ang = esig[:, 0, :]
            tmp = esig[:, 1, :]
            link(dve.tensor_copy(ang, pos_i[:, :]))
            link(dve.tensor_scalar(ang, ang, C("inv_freq"), None, ALU.mult))
            for i, turn in ((0, 0.0), (1, 0.25)):
                r = rope[:, i, :]
                link(dve.tensor_scalar(tmp, ang, 0.5 / math.pi, turn, ALU.mult, ALU.add))
                link(dve.tensor_scalar(tmp, tmp, MAGIC, None, ALU.add))
                link(dve.tensor_scalar(tmp, tmp, -MAGIC, None, ALU.add))
                link(dve.scalar_tensor_tensor(r, tmp, -TWO_PI_HI, ang, ALU.mult, ALU.add))
                link(dve.scalar_tensor_tensor(r, tmp, -TWO_PI_LO, r, ALU.mult, ALU.add))
                link(dve.tensor_scalar(r, r, 2 * math.pi * turn, None, ALU.add))
                link(dve.tensor_scalar(r, r, math.pi * (1 - 1e-7), -math.pi * (1 - 1e-7), ALU.min, ALU.max))
            dve.nop().then_inc(sem("rope_arg"), 1)
            link(dve.tensor_scalar(mean_of, ones, 1.0 / P, None, ALU.mult))
            start, per = vc.n, DVE_LINKS
            with dve.Fori(0, LAYERS) as l:
                vc.turn(l, per, start)

                def w(name, per, k):
                    dve.wait_ge(sem(name), l * per + k)

                def gates(name, dst, silu=True):
                    for i in range(4):
                        j = JOB_AT[name] + i
                        w("jexp", JEXPS, JEXP_AT[name] + i + 1)
                        e = esig[:, j % 2, :]
                        out = sem(f"job_out{j % 2}")
                        link(dve.tensor_scalar(e, e, 1.0, None, ALU.add))
                        if silu:
                            link(dve.reciprocal(e, e))
                            dve.tensor_tensor(dst[:, i, :], ps[:, j % 2, 0:SEQ], e, ALU.mult).then_inc(out, 1)
                        else:
                            dve.reciprocal(dst[:, i, :], e).then_inc(out, 1)

                w("mem_r", 1, 1)
                w("in_layer", 48, 48)
                for k in range(KD):
                    dve.scalar_tensor_tensor(mem_t[:, k, :], mem_t[:, k, :], P2("mem_norm", k), hn_mem, ALU.mult, ALU.mult).then_inc(sem("mem_n"), 1)
                w("pre_r", 1, 1)
                for k in range(KD):
                    dve.scalar_tensor_tensor(an[:, k, :], x_tok[:, k, :], P2("norm_pre", k), rstd[:, 0:SEQ], ALU.mult, ALU.mult).then_inc(sem("pre_n"), 1)
                dve.memset(gm_ws[CH:P, :, 0:CH], 0.0).then_inc(sem("gm_mask"), 1)
                link(dve.tensor_scalar(keyneg, C("keymask"), BIG, -BIG, ALU.mult, ALU.add))
                gates("xa_z", y_all[:, 4])
                gates("sb_z", y_all[:, 0])
                unit_evacuated(dve, l, "sb_z")
                for hd in range(NH):
                    w("xl_ps", NH, hd + 1)
                    mx = xa_s[:, 2 * hd, 0:2]
                    link(dve.tensor_reduce(mx, ps[:, 2 + hd % 2, :].rearrange("p (s m) -> p s m", s=2), AX, ALU.max))
                    dve.tensor_scalar(mx, mx, -SCALE, None, ALU.mult).then_inc(sem("xa_max"), 1)
                    w("xa_e", 2 * NH, 2 * hd + 2)
                    sm = xa_s[:, 2 * hd + 1, 0:2]
                    link(dve.reciprocal(sm, sm))
                    p_ = xa_l[:, hd % 2]
                    dve.tensor_tensor(p_, p_, sm.unsqueeze(2).to_broadcast([P, 2, SEQ]), ALU.mult).then_inc(sem("xa_p"), 1)
                    w("xo_ps", NH, hd + 1)
                    y = y_all[:, 4, hd, :]
                    dve.tensor_tensor(y, y, ps[:, 6 + hd % 2, 0:SEQ], ALU.mult).then_inc(sem("xa_y"), 1)
                for hd in range(NH):
                    z = sb_z[:, hd % 2, :]
                    w("sb_ln", NH, hd + 1)
                    link(dve.scalar_tensor_tensor(sb_sp, z, 0.0, sb_sp, ALU.max, ALU.add))
                    dve.tensor_tensor(sb_sp, sb_sp, C("keymask"), ALU.mult).then_inc(sem("sb_sp"), 1)
                    w("sr_ps", NH, hd + 1)
                    if hd >= 1:
                        w("so_ps", NH, hd)
                    link(dve.tensor_tensor(sb_w, z, ps[:, 4 + hd % 2, :], ALU.subtract))
                    dve.tensor_tensor(sb_w, sb_w, keyneg, ALU.add).then_inc(sem("sb_d"), 1)
                    w("so_ps", NH, hd + 1)
                    y = y_all[:, 0, hd, :]
                    dve.tensor_tensor(y, y, ps[:, 6 + hd % 2, 0:SEQ], ALU.mult).then_inc(sem("sb_y"), 1)
                w("sb_y", NH, NH)
                tick(dve.memset(ml_v[:, :, :, HD:HD + 1], 1.0))
                dve.memset(wide[:, :, 0:3], 0.0).then_inc(sem("ml_pads"), 1)
                for i in range(8):
                    name, tap = ("ml_q", "conv_q") if i < 4 else ("ml_k", "conv_k")
                    evacuated(dve, l, JOB_AT[name] + i % 4)
                    dst = (ml_q if i < 4 else ml_k)[:, i % 4, :]
                    link(dve.tensor_scalar(dst, wide[:, i, 0:SEQ], P2(tap, i % 4), None, ALU.mult))
                    for t in range(1, 4):
                        ins = dve.scalar_tensor_tensor(dst, wide[:, i, t:t + SEQ], P2(tap, 4 * t + i % 4), dst, ALU.mult, ALU.add)
                        if i == 7 and t == 3:
                            ins.then_inc(sem("ml_conv"), 1)
                        else:
                            link(ins)
                gates("ml_o", ml_o, silu=False)
                gates("ml_z", y_all[:, 1])
                w("ml_qke", 1, 1)
                link(dve.tensor_scalar(wide_flat, wide_flat, 1.0, None, ALU.add))
                link(dve.reciprocal(wide_flat, wide_flat))
                w("ml_conv", 1, 1)
                link(dve.tensor_tensor(xr(ml_q), xr(ml_q), wide_flat[:, 0:4 * SEQ], ALU.mult))
                dve.scalar_tensor_tensor(xr(ml_k), xr(ml_k), SCALE, wide_flat[:, 4 * SEQ:8 * SEQ], ALU.mult, ALU.mult).then_inc(sem("ml_qk"), 1)
                w("ml_qk", 1, 1)
                g0, g1, g2, g3, g4 = (ml_g[0:4, i, :] for i in range(5))
                w("mg_ps", 1, 1)
                link(dve.tensor_scalar(g0, ps[0:4, 2, 0:SEQ], P2("b_i", rows=4), None, ALU.add))
                dve.tensor_scalar(g1, ps[0:4, 3, 0:SEQ], P2("b_f", rows=4), None, ALU.add).then_inc(sem("mg_x"), 1)
                w("mg_l", 1, 1)
                c_bl, c_al, c_m, c_x = ml_c[0:4, 0, 0:4], ml_c[0:4, 1, 0:4], ml_c[0:4, 2, 0:5], ml_c[0:4, 3, 0:4]

                def by_chunk(v):
                    return v.rearrange("p (c t) -> p c t", t=CH)

                def over(v):
                    return v.unsqueeze(2).to_broadcast([4, NC2, CH])

                link(dve.scalar_tensor_tensor(g2, g1, 0.0, g2, ALU.min, ALU.subtract))
                link(dve.tensor_tensor_scan(g3, C("run", 4)[:, 0:SEQ], g2, 0.0, ALU.mult, ALU.add))
                link(dve.tensor_tensor(g0, g0, g3, ALU.subtract))
                link(dve.tensor_tensor_scan(g4, C("restart", 4), g0, -BIG, ALU.add, ALU.max))
                link(dve.tensor_tensor(g4, g4, g3, ALU.add))
                link(dve.tensor_copy(c_bl, g3[:, CH - 1:SEQ:CH]))
                link(dve.tensor_copy(c_al, g4[:, CH - 1:SEQ:CH]))
                link(dve.memset(c_m[:, 0:1], 0.0))
                link(dve.tensor_tensor_scan(c_m[:, 1:5], c_bl, c_al, 0.0, ALU.add, ALU.max))
                link(dve.tensor_tensor(by_chunk(g1), by_chunk(g3), over(c_m[:, 0:4]), ALU.add))
                link(dve.tensor_tensor(g4, g1, g4, ALU.max))
                rows = ml_rows[0:4, :]
                link(dve.tensor_tensor(rows[:, 0:SEQ], g3, g4, ALU.subtract))
                link(dve.tensor_tensor(rows[:, SEQ:2 * SEQ], g1, g4, ALU.subtract))
                link(dve.tensor_scalar(rows[:, 2 * SEQ:3 * SEQ], g4, -1.0, None, ALU.mult))
                link(dve.tensor_tensor(c_x, c_bl, c_m[:, 0:4], ALU.add))
                link(dve.tensor_tensor(rows[:, 768:772], c_x, c_m[:, 1:5], ALU.subtract))
                link(dve.tensor_tensor(rows[:, 772:776], c_al, c_m[:, 1:5], ALU.subtract))
                link(dve.tensor_tensor(c_x, c_bl, c_al, ALU.subtract))
                dve.tensor_tensor(by_chunk(g2), by_chunk(g0), over(c_x), ALU.add).then_inc(sem("mg_r"), 1)
                gates("gm_z", y_all[:, 2])
                w("ml_col", 1, 1)
                for hd in range(NH):
                    w("ml_bc", 2 * NH, 2 * hd + 2)
                    for par in range(2):
                        q = slice(CH * par, CH * (par + 1))
                        dve.tensor_tensor(ml_d[q], halves(ml_bc[q, 0:SEQ], par), C("causal_neg")[q].unsqueeze(1).to_broadcast([CH, 2, CH]),
                                          ALU.add).then_inc(sem("ml_dx"), 1)
                    w("mk_ps", NH, hd + 1)
                    for tt in range(2):
                        dve.tensor_scalar(ml_kw[:, tt, :], ps[:, 5, tt * P:(tt + 1) * P], ml_col[:, 8 + 4 * tt + hd:9 + 4 * tt + hd], None,
                                          ALU.mult).then_inc(sem("ml_kw"), 1)
                    dve.tensor_tensor(ml_qd, ml_q[:, hd, :], ml_bc[:, SEQ:2 * SEQ], ALU.mult).then_inc(sem("ml_qd"), 1)
                    w("ml_de", 4 * NH, 4 * hd + 4)
                    w("ms_ps", NH, hd + 1)
                    dve.tensor_tensor(ml_s, ml_d, ps[:, 4, 0:P].rearrange("p (a t) -> p a t", t=CH), ALU.mult).then_inc(sem("ml_s"), 1)
                    w("mu_ps", NH, hd + 1)
                    for c in range(3):
                        link(dve.tensor_scalar(ml_st[:, c, :], ps[:, 6 + c % 2, (c // 2) * (HD + 1):(c // 2 + 1) * (HD + 1)],
                                               ml_bc[:, 772 + c:773 + c], None, ALU.mult))
                    for c in (1, 2):
                        link(dve.scalar_tensor_tensor(ml_st[:, c, :], ml_st[:, c - 1, :], ml_bc[:, 768 + c:769 + c], ml_st[:, c, :], ALU.mult, ALU.add))
                    dve.tensor_copy(ml_nb, ml_st[:, :, HD:HD + 1].to_broadcast([P, 3, P])).then_inc(sem("ml_st"), 1)
                    w("mo_ps", NH, hd + 1)
                    for par in range(2):
                        den = ps[:, 2 + par, P:2 * P].rearrange("p (a t) -> p a t", t=CH)
                        link(dve.scalar_tensor_tensor(halves(ml_qd, par), den, -1.0, halves(ml_bc[:, 2 * SEQ:3 * SEQ], par), ALU.mult, ALU.max))
                        link(dve.tensor_tensor(halves(ml_qd, par), halves(ml_qd, par), den, ALU.max))
                    link(dve.reciprocal(ml_qd, ml_qd))
                    link(dve.tensor_tensor(halves(ml_q[:, hd, :], 0), ps[:, 2, 0:P].rearrange("p (a t) -> p a t", t=CH), halves(ml_qd, 0), ALU.mult))
                    dve.tensor_tensor(halves(ml_q[:, hd, :], 1), ps[:, 3, 0:P].rearrange("p (a t) -> p a t", t=CH), halves(ml_qd, 1),
                                      ALU.mult).then_inc(sem("ml_h"), 1)

                def head_norm(src, tag):
                    w(f"{tag}_mean", 1, 1)
                    dve.tensor_tensor(xr(src), xr(src), ps[:, 2:4, :].rearrange("p a b -> p (a b)"), ALU.subtract).then_inc(sem(f"{tag}_c"), 1)
                    w(f"{tag}_c", 1, 1)
                    w(f"{tag}_r", 1, 1)
                    link(dve.tensor_tensor(xr(src), xr(src), xr(hn_r), ALU.mult))

                w("ml_h", NH, NH)
                head_norm(ml_q, "mlh")
                link(dve.tensor_tensor(xr(ml_q), xr(ml_q), xr(ml_o), ALU.mult))
                dve.tensor_tensor(xr(y_all[:, 1]), xr(y_all[:, 1]), xr(ml_q), ALU.mult).then_inc(sem("ml_y"), 1)
                w("ml_y", 1, 1)
                w("gm_gelu", 2, 2)
                w("in_rows", 16, 16)
                for m in range(2):
                    link(dve.bn_stats(gm_st[:, m, 0:6], b_v[:, m, :]))
                tick(dve.memset(gm_st[:, :, 6:8], 0.0))
                tick(dve.bn_aggr(gm_mv[:, 0, :], gm_st[:, 0, 0:6]))
                dve.bn_aggr(gm_mv[:, 1, :], gm_st[:, 1, 0:6]).then_inc(sem("gm_var"), 1)
                w("gm_r", 1, 1)
                for m in range(2):
                    link(dve.tensor_scalar(b_v[:, m, :], b_v[:, m, :], gm_mv[:, m, 0:1], gm_mv[:, m, 1:2], ALU.subtract, ALU.mult))
                link(dve.tensor_tensor(b_v, b_v, gm_rows[:, 0, :].unsqueeze(1).to_broadcast([P, 2, HALF]), ALU.mult))
                dve.tensor_tensor(b_v, b_v, gm_rows[:, 1, :].unsqueeze(1).to_broadcast([P, 2, HALF]), ALU.add).then_inc(sem("gm_n"), 1)
                w("gm_ps", 1, 1)
                for g in range(4):
                    link(dve.tensor_tensor(gm_x, ps[:, 2 + g // 2, (g % 2) * SEQ:(g % 2 + 1) * SEQ].rearrange("p (n t) -> p n t", n=2),
                                           gm_rows[:, 2, g * P:(g + 1) * P].unsqueeze(1).to_broadcast([P, 2, P]), ALU.add))
                    link(dve.tensor_tensor(xr(gm_x), xr(gm_x), b_q[:, g, :], ALU.mult))
                    dve.tensor_tensor(y_all[:, 2, g, :], y_all[:, 2, g, :], xr(gm_x), ALU.mult).then_inc(sem("gm_y"), 1)
                    w("gm_y", 4, g + 1)
                gates("rt_z", y_all[:, 3])
                for i, src in enumerate((b_q, b_q, b_k, b_k)):
                    s = src[:, 2 * (i % 2):2 * (i % 2) + 2, :]
                    w("rr_ps", 4, i + 1)
                    t = rt_t[:, i % 2, :].rearrange("p (h t) -> p h t", h=2)
                    tick(dve.tensor_tensor(t, ps[:, 2 + i, :].rearrange("p (h t) -> p h t", h=2), rope[:, 0:1, :].to_broadcast([P, 2, SEQ]), ALU.mult))
                    link(dve.tensor_tensor(s, s, rope[:, 1:2, :].to_broadcast([P, 2, SEQ]), ALU.mult))
                    dve.tensor_tensor(s, s, t, ALU.add).then_inc(sem("rt_rot"), 1)
                    w("rt_rot", 4, i + 1)
                for hd in range(NH):
                    gamma = float(np.log(1.0 - 2.0 ** (-5.0 - hd)))
                    w("rs_ps", NH, hd + 1)
                    decay_h = C("rt_decay").rearrange("p (h t) -> p h t", h=NH)[:, hd:hd + 1, :].to_broadcast([P, 2, CH])
                    if hd >= 1:
                        w("ro_ps", NH, hd)
                    dve.tensor_tensor(rt_s, ps[:, 2, 0:P].rearrange("p (a t) -> p a t", t=CH), decay_h, ALU.mult).then_inc(sem("rt_s"), 1)
                    wq = C("rt_wq").rearrange("p (h t) -> p h t", h=NH)[:, hd:hd + 1, :].to_broadcast([P, NC2, CH])
                    dve.tensor_tensor(rt_qd.rearrange("p (c t) -> p c t", t=CH), b_q[:, hd, :].rearrange("p (c t) -> p c t", t=CH), wq, ALU.mult).then_inc(sem("rt_qd"), 1)
                    w("rk_ps", NH, hd + 1)
                    dve.tensor_scalar(xr(rt_kw), ps[:, 3, 0:2 * P], C("rt_wend")[:, hd:hd + 1], None, ALU.mult).then_inc(sem("rt_kw"), 1)
                    w("ru_ps", NH, hd + 1)
                    link(dve.tensor_copy(rt_st[:, 0, :], ps[:, 6, 0:P]))
                    link(dve.scalar_tensor_tensor(rt_st[:, 1, :], rt_st[:, 0, :], math.exp(gamma * CH), ps[:, 7, 0:P], ALU.mult, ALU.add))
                    dve.scalar_tensor_tensor(rt_st[:, 2, :], rt_st[:, 1, :], math.exp(gamma * CH), ps[:, 6, P:2 * P], ALU.mult, ALU.add).then_inc(sem("rt_st"), 1)
                    w("ro_ps", NH, hd + 1)
                    for par in range(2):
                        dve.tensor_copy(halves(b_q[:, hd, :], par), ps[:, 4 + par, 0:P].rearrange("p (a t) -> p a t", t=CH)).then_inc(sem("rt_h"), 1)
                w("rt_h", 2 * NH, 2 * NH)
                head_norm(b_q, "rth")
                dve.tensor_tensor(xr(y_all[:, 3]), xr(y_all[:, 3]), xr(b_q), ALU.mult).then_inc(sem("rt_y"), 1)
                for p in range(PAIRS):
                    c, n = p // NBR, p % NBR
                    j = MERGE_AT + 2 * p
                    evacuated(dve, l, j)
                    e = esig[:, p % 2, :]
                    link(dve.tensor_scalar(e, e, 1.0, None, ALU.add))
                    link(dve.reciprocal(e, e))
                    w("job", JOBS, j + 2)
                    out = e if n else merged[:, c, :]
                    dve.tensor_tensor(out, ps[:, (j + 1) % 2, 0:SEQ], e, ALU.mult).then_inc(sem(f"job_out{(j + 1) % 2}"), 1)
                    evacuated(dve, l, j + 1)
                    if n:
                        dve.tensor_tensor(merged[:, c, :], merged[:, c, :], e, ALU.add).then_inc(sem("merged"), 1)
                    else:
                        dve.nop().then_inc(sem("merged"), 1)
                    w("merged", PAIRS, p + 1)
                w("post_r", 1, 1)
                for k in range(KD):
                    tick(dve.scalar_tensor_tensor(post[:, k, :], post[:, k, :], P2("norm_post", k), rstd[:, 0:SEQ], ALU.mult, ALU.mult))
                dve.wait_ge(vc.sem, vc.base + vc.n)
                dve.tensor_tensor(x_tok, x_tok, post, ALU.add).then_inc(sem("x_out"), 1)
                w("x_out", 1, 1)
                vc.end_turn(per)

        spectra = m1.take(3, 4, HALF)
        tail = m1.at - 3 * 4 * HALF
        assert m1.at <= SHARED_W, m1.at
        m4 = Layout(filt.rearrange("p a b c -> p (a b c)"))
        zt = m4.take(3, HALF)
        yf = m4.take(3, 2, HALF)
        prod = m4.take(2, HALF)
        m5 = Layout(arena, tail)
        f_k, f_lf, f_cum, f_rel, f_q, f_kk, f_qe, f_kd = (m5.take(2, TP) for _ in range(8))
        kd_t = m5.take(NCH - 1, P)
        assert m5.at <= SHARED_W, m5.at
        m6 = Layout(scratch)
        vt = m6.take(NCH, HALF)
        sc_m = m6.take(2, TP)
        states = m6.take(2, (NCH - 1) * P)
        decay = m6.take(2, NCH)
        head_sq = m6.take(4, T)
        assert m6.at <= 2 * WSLOT

        e1 = Layout(arena, free_at)
        xn = e1.take(2, D)
        router = e1.take(KD, NG + NE)
        logits = e1.take(2, NG + NE)
        pick = e1.take(2, NE)
        slot_of = e1.take(2, NE)
        chosen = e1.take(2, NE)
        small = e1.take(24, 16)
        onehot = e1.take(2, P)
        weighted = e1.take(2, P)
        xg = e1.take(KD, P)
        back = e1.take(SEQ)
        gate_e = e1.take(FE)
        mid = e1.take(FE)
        mid_t = e1.take(FE // P, P)
        y_slot = e1.take(D)
        assert e1.at <= SHARED_W

        x_tok = h[:, :, META:T]
        an = a[:, :, 0:SEQ]

        def xr(v):
            return v.rearrange("p a b -> p (a b)")

        block_one = nc.Block()
        block = block_one.__enter__()

        def job_evacuated(eng, j):
            eng.wait_ge(sem(f"strip_out{j % 2}"), j // 2 + 1)

        def strip_at(j):
            return ps[:, j % 2, 0:T]

        @block.sync
        def _(sp):
            sp.dma_start(const, d["const"]).then_inc(sem("in_const"), 16)
            sp.dma_start(param1, d["param1"]).then_inc(sem("in_param1"), 16)
            sp.dma_start(feat[0:33, 0:T], d["features"][0:33, 0:T]).then_inc(sem("in_feat"), 16)
            sp.dma_start(fw1[0:33, :], d["filt_w1"]).then_inc(sem("in_feat"), 16)
            sp.dma_start(fw2[0:64, :], d["filt_w2"]).then_inc(sem("in_feat"), 16)
            sp.dma_start(xr(h), d["h"]).then_inc(sem("in_h"), 16)
            sp.dma_start(fw3[0:64, :, :], d["filt_w3"].rearrange("k (a b) -> k a b", b=HALF)).then_inc(sem("in_w3"), 16)
            sp.dma_start(xr(window), d["features"][:, T:T + 3 * HALF]).then_inc(sem("in_w3"), 16)
            sp.dma_start(four.rearrange("p a b c -> p (a b c)"), d["fourier"]).then_inc(sem("in_four"), 16)
            for u in range(10):
                if u >= RING1:
                    sp.wait_ge(sem("strip"), 4 * (u - RING1 + 1))
                sp.dma_start(ring[:, u % RING1, :], d["w_first"][u]).then_inc(sem(f"w1_in{u % RING1}"), 16)
            sp.wait_ge(sem("xn"), 16)
            sp.dma_start(xr(router), d["router"]).then_inc(sem("in_router"), 16)
            sp.wait_ge(sem("rounds"), 1)
            n_rounds = sp.value_load(rounds[0:1, 0:1], min_val=1, max_val=SEQ // CAP)
            with sp.Fori(0, n_rounds) as r:
                with sp.Fori(0, NGRP) as g:
                    for v in range(12):
                        s = (v + 2) % RING
                        sp.wait_ge(sem("unit_free"), (r * NGRP + g) * 12 + v + 1)
                        if v < 8:
                            src = d["w_gate" if v < 4 else "w_up"][bass.ds(g * GRP, GRP), (v % 4) * 2 * P:(v % 4 + 1) * 2 * P, :]
                            for k in range(2):
                                sp.dma_start(ring[:, s, k * 2048:(k + 1) * 2048].rearrange("p (e n) -> p e n", n=FE),
                                             src[:, k * P:(k + 1) * P, :].rearrange("e p n -> p e n")).then_inc(sem(f"w2_in{s}"), 16)
                        else:
                            src = d["w_down"][bass.ds(g * GRP, GRP), (v - 8) * P:(v - 7) * P, :]
                            for k in range(2):
                                sp.dma_start(ring[:, s, k * 2048:(k + 1) * 2048].rearrange("p (e n) -> p e n", n=D),
                                             src[2 * k:2 * k + 2].rearrange("e p n -> p e n")).then_inc(sem(f"w2_in{s}"), 16)
            if stop_after == "experts":
                sp.wait_ge(sem("x_final"), 8)
                sp.dma_start(d["out"].rearrange("(k p) t -> p k t", p=P), x_tok).then_inc(sem("out"), 16)
                sp.wait_ge(sem("out"), 16)

        @block.tensor
        def _(pe):
            def strip(j, unit, s, rhs, n):
                if j % 4 == 0:
                    pe.wait_ge(sem(f"w1_in{unit % RING1}"), 16 * (unit // RING1 + 1))
                if j >= 2:
                    job_evacuated(pe, j - 2)
                w = ring[:, unit % RING1, :].rearrange("p (s k m) -> p s k m", s=4, k=KD)
                for k in range(KD):
                    last = pe.matmul(ps[:, j % 2, 0:n], w[:, s, k, :], rhs(k), start=(k == 0), stop=(k == KD - 1))
                last.then_inc(sem("strip"), 1)

            pe.wait_ge(sem("in_feat"), 48)
            pe.matmul(ps[0:64, 2, 0:T], fw1[0:33, :], zT[0:33, :], start=True, stop=True).then_inc(sem("hid"), 1)
            pe.wait_ge(sem("sq_mix"), 1)
            pe.wait_ge(sem("in_const"), 16)
            norm_sum(pe, ones, a, KD, ps[:, 3, 0:T], sem("ss_mix"))
            pe.wait_ge(sem("hid_act"), 1)
            pe.matmul(ps[0:64, 2, 0:T], fw2[0:64, :], hid[0:64, :], start=True, stop=True).then_inc(sem("hid"), 1)
            pe.wait_ge(sem("hid_act"), 2)
            pe.wait_ge(sem("in_w3"), 32)
            n = 0
            for tt in range(3):
                for c in range(4):
                    if n >= 4:
                        pe.wait_ge(sem("filt"), n - 3)
                    pe.matmul(ps[0:TW[tt], 4 + n % 4, :], hid[0:64, tt * P:tt * P + TW[tt]], fw3[0:64, c, :],
                              start=True, stop=True).then_inc(sem("filt_ps"), 1)
                    n += 1
            pe.wait_ge(sem("in_four"), 16)
            pe.wait_ge(sem("filt_sd"), 4)
            n = 0
            for o in range(2):
                for part, basis in ((0, cosm), (1, sinm)):
                    for ft in range(3):
                        if n >= 4:
                            pe.wait_ge(sem("spectrum"), n - 3)
                        else:
                            pe.wait_ge(sem("filt"), 12)
                        for tt in range(3):
                            last = pe.matmul(ps[0:TW[ft], 4 + n % 4, :], basis[0:TW[tt], tt, ft * P:ft * P + TW[ft]],
                                             filt[0:TW[tt], tt, 2 * part + o, :], start=(tt == 0), stop=(tt == 2))
                        last.then_inc(sem("spectrum_ps"), 1)
                        n += 1
            pe.wait_ge(sem("normed_mix"), KD)
            for j in range(HY + HG):
                strip(j, j // 4, j % 4, lambda k: a[:, k, :], T)
            for o in range(2):
                pe.wait_ge(sem("z"), 4 * (o + 1))
                if o == 0:
                    pe.wait_ge(sem("spectrum"), 12)
                for tt in range(3):
                    if tt == 2:
                        pe.wait_ge(sem("zt"), 3 * o + 1)
                    for c in range(4):
                        last = pe.transpose(ps[0:TW[tt], 2 + tt % 2, c * P:(c + 1) * P], conv[:, c, tt * P:tt * P + TW[tt]], ident)
                    last.then_inc(sem("zt_ps"), 1)
                pe.wait_ge(sem("zt"), 3 * (o + 1))
                for ft in range(3):
                    n = 3 * o + ft
                    if n >= 2:
                        pe.wait_ge(sem("yf"), n - 1)
                    for part, basis in ((0, cosm), (1, sinm)):
                        for tt in range(3):
                            last = pe.matmul(ps[0:TW[ft], 4 + 2 * (n % 2) + part, :], basis[0:TW[tt], tt, ft * P:ft * P + TW[ft]],
                                             zt[0:TW[tt], tt, :], start=(tt == 0), stop=(tt == 2))
                    last.then_inc(sem("uf_ps"), 1)
                pe.wait_ge(sem("yf"), 3 * (o + 1))
                for c in range(4):
                    if c >= 2:
                        pe.wait_ge(sem("z"), 4 * (o + 1) + c - 1)
                    for ft in range(3):
                        for part, basis in ((0, icos), (1, isin)):
                            last = pe.matmul(ps[:, 2 + c % 2, 0:T], yf[0:TW[ft], ft, part, c * P:(c + 1) * P],
                                             basis[0:TW[ft], ft, :], start=(ft == 0 and part == 0), stop=(ft == 2 and part == 1))
                    last.then_inc(sem("conv_ps"), 1)
            for c in range(NCH):
                job_evacuated(pe, 26)
                job_evacuated(pe, 27)
                if c >= 2:
                    pe.wait_ge(sem("vt"), c - 1)
                elif c == 0:
                    pe.wait_ge(sem("z"), 12)
                for hd in range(NH):
                    last = pe.transpose(ps[0:CH, 4 + c % 2, hd * P:(hd + 1) * P], hg[:, 12 + hd, c * CH:(c + 1) * CH], ident)
                last.then_inc(sem("vt_ps"), 1)
            pe.wait_ge(sem("sq_hy"), 1)
            job_evacuated(pe, HY + HG - 2)
            norm_sum(pe, ones, padded4, 4, ps[:, 0, 0:T], sem("ss_hy"))
            for it in range(2 * NH):
                hd, bwd = it // 2, it % 2
                b = it % 2
                out = 5 + hd % 2
                pe.wait_ge(sem("scan_in"), it + 1)
                if it >= 1:
                    pe.wait_ge(sem("scores"), it)
                    pe.wait_ge(sem("keys_t"), it)
                if it == 0:
                    pe.wait_ge(sem("vt"), NCH)
                for c in range(NCH):
                    last = pe.matmul(ps[0:CH, 2, c * CH:(c + 1) * CH], f_kk[:, b, c * CH:(c + 1) * CH],
                                     f_q[:, b, c * CH:(c + 1) * CH], start=(c == 0), stop=(c == NCH - 1), skip_group_check=True)
                last.then_inc(sem("scores_ps"), 1)
                for i in range(NCH - 1):
                    c = i + bwd
                    last = pe.transpose(ps[0:CH, 3, i * P:(i + 1) * P], f_kd[:, b, c * CH:(c + 1) * CH], ident)
                last.then_inc(sem("keys_ps"), 1)
                pe.wait_ge(sem("keys_t"), it + 1)
                if it >= 1:
                    pe.wait_ge(sem("state"), it)
                for i in range(NCH - 1):
                    c = i + bwd
                    last = pe.matmul(ps[:, 4, i * P:(i + 1) * P], kd_t[0:CH, i, :], vt[0:CH, c, hd * P:(hd + 1) * P],
                                     start=(i == 0), stop=(i == NCH - 2), skip_group_check=True)
                last.then_inc(sem("state_ps"), 1)
                pe.wait_ge(sem("scores"), it + 1)
                pe.wait_ge(sem("state"), it + 1)
                if hd >= 2 and not bwd:
                    pe.wait_ge(sem("head"), hd - 1)
                for c in range(NCH):
                    last = pe.matmul(ps[:, out, c * CH:(c + 1) * CH], vt[0:CH, c, hd * P:(hd + 1) * P],
                                     sc_m[0:CH, b, c * CH:(c + 1) * CH], start=(c == 0 and not bwd), stop=False, skip_group_check=True)
                    if c != (NCH - 1 if bwd else 0):
                        i = c if bwd else c - 1
                        last = pe.matmul(ps[:, out, c * CH:(c + 1) * CH], states[:, b, i * P:(i + 1) * P],
                                         f_qe[:, b, c * CH:(c + 1) * CH], start=False, stop=False, skip_group_check=True)
                last.then_inc(sem("scan_ps"), 1)
            for hd in range(NH):
                if hd == 0:
                    pe.wait_ge(sem("sq_head"), 1)
                pe.matmul(ps[:, [2, 3, 4, 7][hd], 0:T], ones, head_sq[:, hd, :], start=True, stop=True).then_inc(sem("ss_head"), 1)
            pe.wait_ge(sem("mixed_hg"), NH)
            pe.wait_ge(sem("mixed_hy"), NH)
            pe.sem_inc(sem("unit_free"), 4)
            for j in range(HY + HG, HY + HG + KD):
                strip(j, j // 4, j % 4, lambda k: conv[:, k, META:T] if k < 4 else hg[:, k - 4, TP - SEQ:TP], SEQ)
            pe.wait_ge(sem("sq_ffn"), 1)
            pe.sem_inc(sem("unit_free"), 2)
            norm_sum(pe, ones, a[:, :, 0:SEQ], KD, ps[:, 2, 0:SEQ], sem("ss_ffn"))

            pe.wait_ge(sem("normed_ffn"), KD)
            n = 0
            for tt in range(2):
                for k in range(KD):
                    if n >= 4:
                        pe.wait_ge(sem("xn"), n - 3)
                    pe.transpose(ps[:, 3 + n % 4, 0:P], a[:, k, tt * P:(tt + 1) * P], ident).then_inc(sem("xn_ps"), 1)
                    n += 1
            pe.wait_ge(sem("in_router"), 16)
            for tt in range(2):
                for k in range(KD):
                    last = pe.matmul(ps[:, 7, tt * (NG + NE):(tt + 1) * (NG + NE)], a[:, k, tt * P:(tt + 1) * P], router[:, k, :],
                                     start=(k == 0), stop=(k == KD - 1))
            last.then_inc(sem("logits_ps"), 1)
            pe.wait_ge(sem("chosen"), 1)
            pe.matmul(ps[:, 7, 0:NE], C("before"), chosen[:, 0, :], start=True, stop=True)
            pe.matmul(ps[:, 7, NE:2 * NE], ones, chosen[:, 0, :], start=True, stop=False)
            pe.matmul(ps[:, 7, NE:2 * NE], C("before"), chosen[:, 1, :], start=False, stop=True)
            pe.matmul(ps[:, 7, 2 * NE:3 * NE], ones, chosen[:, 0, :], start=True, stop=False)
            pe.matmul(ps[:, 7, 2 * NE:3 * NE], ones, chosen[:, 1, :], start=False, stop=True).then_inc(sem("slots_ps"), 1)

            pe.wait_ge(sem("rounds"), 1)
            n_rounds = pe.value_load(rounds[0:1, 0:1], min_val=1, max_val=SEQ // CAP)
            with pe.Fori(0, n_rounds) as r:
                with pe.Fori(0, NGRP) as g:
                    it = pe.snap(r * NGRP + g)
                    pe.wait_ge(sem("onehot"), it + 1)
                    for k in range(KD):
                        for tt in range(2):
                            last = pe.matmul(ps[:, 4 + k // 4, (k % 4) * P:(k % 4 + 1) * P], xn[:, tt, k * P:(k + 1) * P],
                                             onehot[:, tt, :], start=(tt == 0), stop=(tt == 1))
                    last.then_inc(sem("gather_ps"), 1)
                    for tt in range(2):
                        last = pe.transpose(ps[:, 7, tt * P:(tt + 1) * P], weighted[:, tt, :], ident)
                    last.then_inc(sem("back_ps"), 1)
                    pe.wait_ge(sem("xg"), 2 * it + 2)
                    for v in range(8):
                        s = (v + 2) % RING
                        pe.wait_ge(sem(f"w2_in{s}"), it * 64 + (v // RING + 1) * 32)
                        w = ring[:, s, :].rearrange("p (k e n) -> p k e n", k=2, n=FE)
                        for k in range(2):
                            for e in range(GRP):
                                last = pe.matmul(ps[CAP * e:CAP * (e + 1), v // 4, :], xg[:, (v % 4) * 2 + k, CAP * e:CAP * (e + 1)],
                                                 w[:, k, e, :], start=(v % 4 == 0 and k == 0), stop=(v % 4 == 3 and k == 1))
                        last.then_inc(sem("unit_free"), 1)
                    pe.wait_ge(sem("mid"), it + 1)
                    for c in range(FE // P):
                        last = pe.transpose(ps[:, 6, c * P:(c + 1) * P], mid[:, c * P:(c + 1) * P], ident)
                    last.then_inc(sem("mid_ps"), 1)
                    pe.wait_ge(sem("mid_t"), it + 1)
                    for v in range(8, 12):
                        s = (v + 2) % RING
                        pe.wait_ge(sem(f"w2_in{s}"), it * 64 + (v // RING + 1) * 32)
                        w = ring[:, s, :].rearrange("p (e n) -> p e n", n=D)
                        for half in range(2):
                            for e in range(GRP):
                                last = pe.matmul(ps[CAP * e:CAP * (e + 1), 2 + half, :], mid_t[:, v - 8, CAP * e:CAP * (e + 1)],
                                                 w[:, e, half * 512:(half + 1) * 512], start=(v == 8), stop=(v == 11))
                        last.then_inc(sem("unit_free"), 1)
                    pe.wait_ge(sem("y_slot"), 2 * it + 2)
                    for k in range(KD):
                        last = pe.matmul(ps[:, 4 + k // 2, (k % 2) * SEQ:(k % 2 + 1) * SEQ], y_slot[:, k * P:(k + 1) * P], back,
                                         start=True, stop=True)
                    last.then_inc(sem("scatter_ps"), 1)
            pe.wait_ge(sem("sq_final"), 1)
            norm_sum(pe, ones, an, KD, ps[:, 0, 0:SEQ], sem("ss_final"))

        @block.scalar
        def _(act):
            ac = Chain(act, sem("act_chain"))
            act.wait_ge(sem("in_h"), 16)
            norm_squares(act, xr(h), xr(a), sem("sq_mix"))
            act.wait_ge(sem("in_const"), 16)
            act.wait_ge(sem("ss_mix"), 1)
            norm_rstd(act, ac, rstd, ps[:, 3, 0:T], D, eps, sem("rstd_mix"))
            for i in range(2):
                act.wait_ge(sem("hid_arg"), i + 1)
                act.activation(hid[0:64, :], hid[0:64, :], ACT.Sin).then_inc(sem("hid_act"), 1)
            for n in range(12):
                o, part, ft = n // 6, n // 3 % 2, n % 3
                act.wait_ge(sem("spectrum_ps"), n + 1)
                act.copy(spectra[0:TW[ft], ft, 2 * o + part, :], ps[0:TW[ft], 4 + n % 4, :]).then_inc(sem("spectrum"), 1)
            act.wait_ge(sem("lb_diff"), 1)
            act.activation(lb[:, :, 0, :], lb[:, :, 0, :], ACT.Exp).then_inc(sem("lb_exp"), 1)
            for j in range(HY + HG):
                act.wait_ge(sem("strip"), j + 1)
                if j < HY:
                    if j == 0:
                        act.wait_ge(sem("edges"), 1)
                    if j >= 4:
                        act.wait_ge(sem("convolved"), j - 3)
                    act.copy(padded[:, j % 4, 1:T + 1], strip_at(j)).then_inc(sem(f"strip_out{j % 2}"), 1)
                elif 24 <= j < 28:
                    act.wait_ge(sem("hg_zero"), 1)
                    act.copy(hg[:, j - HY, PADT:TP], strip_at(j)).then_inc(sem(f"strip_out{j % 2}"), 1)
                else:
                    act.activation(sig[:, j % 2, :], strip_at(j), ACT.Exp, scale=-1.0).then_inc(sem("strip_exp"), 1)
            for c in range(NCH):
                act.wait_ge(sem("vt_ps"), c + 1)
                act.copy(vt[0:CH, c, :], ps[0:CH, 4 + c % 2, :]).then_inc(sem("vt"), 1)
            act.wait_ge(sem("z"), 12)
            act.activation(xr(padded4), xr(conv[:, 0:4, :]), ACT.Square).then_inc(sem("sq_hy"), 1)
            act.wait_ge(sem("ss_hy"), 1)
            norm_rstd(act, ac, rstd, ps[:, 0, 0:T], HALF, eps, sem("rstd_hy"))
            for it in range(2 * NH):
                b = it % 2
                act.wait_ge(sem("forget"), it + 1)
                act.activation(f_lf[:, b, PADT:TP], f_lf[:, b, PADT:TP], ACT.Ln).then_inc(sem("log_f"), 1)
                act.wait_ge(sem("cum"), it + 1)
                act.activation(f_q[:, b, :], f_rel[:, b, :], ACT.Exp).then_inc(sem("scan_exp"), 1)
                act.activation(f_kk[:, b, :], f_rel[:, b, :], ACT.Exp, scale=-1.0).then_inc(sem("scan_exp"), 1)
                act.activation(f_qe[:, b, :], f_cum[:, b, :], ACT.Exp).then_inc(sem("scan_exp"), 1)
                act.activation(f_kd[:, b, :], f_kd[:, b, :], ACT.Exp).then_inc(sem("scan_exp"), 1)
                last_of = f_cum[:, b, 0:TP:CH] if it % 2 else f_cum[:, b, CH - 1:TP:CH]
                act.activation(decay[:, b, :], last_of, ACT.Exp).then_inc(sem("scan_exp"), 1)
                act.wait_ge(sem("keys_ps"), it + 1)
                if it >= 1:
                    act.wait_ge(sem("state_ps"), it)
                act.copy(xr(kd_t[0:CH]), ps[0:CH, 3, 0:(NCH - 1) * P]).then_inc(sem("keys_t"), 1)
            act.wait_ge(sem("head"), NH)
            act.activation(head_sq, hg[:, 4:8, PADT:TP], ACT.Square).then_inc(sem("sq_head"), 1)
            for hd in range(NH):
                act.wait_ge(sem("ss_head"), hd + 1)
                norm_rstd(act, ac, head_sq[:, hd, :], ps[:, [2, 3, 4, 7][hd], 0:T], P, eps, sem("rstd_head"))
            act.wait_ge(sem("strip_out0"), 20)
            act.wait_ge(sem("strip_out1"), 20)
            norm_squares(act, x_tok, an, sem("sq_ffn"))
            act.wait_ge(sem("ss_ffn"), 1)
            norm_rstd(act, ac, rstd[:, 0:SEQ], ps[:, 2, 0:SEQ], D, eps, sem("rstd_ffn"))
            act.wait_ge(sem("route_arg"), 1)
            act.activation(small[:, 4:6, 0:8], small[:, 4:6, 0:8], ACT.Exp).then_inc(sem("route_exp"), 1)
            act.activation(small[:, 14:16, 0:1], small[:, 14:16, 0:1], ACT.Exp).then_inc(sem("route_exp"), 1)
            act.wait_ge(sem("rounds"), 1)
            n_rounds = act.value_load(rounds[0:1, 0:1], min_val=1, max_val=SEQ // CAP)
            with act.Fori(0, n_rounds) as r:
                with act.Fori(0, NGRP) as g:
                    it = act.snap(r * NGRP + g)
                    act.wait_ge(sem("back_ps"), it + 1)
                    act.copy(back, ps[:, 7, 0:SEQ]).then_inc(sem("back"), 1)
                    act.wait_ge(sem("unit_free"), it * 12 + 6 + 4)
                    act.activation(gate_e, ps[:, 0, :], ACT.Exp, scale=-1.0).then_inc(sem("gate_exp"), 1)
                    act.wait_ge(sem("mid_ps"), it + 1)
                    act.copy(xr(mid_t), ps[:, 6, :]).then_inc(sem("mid_t"), 1)
            act.wait_ge(sem("experts_done"), 1)
            norm_squares(act, x_tok, an, sem("sq_final"))
            act.wait_ge(sem("ss_final"), 1)
            norm_rstd(act, ac, rstd[:, 0:SEQ], ps[:, 0, 0:SEQ], D, eps, sem("rstd_final"))

        @block.vector
        def _(dve):
            vc = Chain(dve, sem("dve_chain"))
            link, tick = vc.link, vc.tick
            dve.memset(padded[:, :, 0:1], 0.0)
            dve.memset(padded[:, :, T + 1:T + 2], 0.0).then_inc(sem("edges"), 1)
            dve.wait_ge(sem("in_param1"), 16)
            for i in range(2):
                dve.wait_ge(sem("hid"), i + 1)
                ph, wr = hid[0:64, :], wrap[0:64, :]
                link(dve.tensor_scalar(ph, ps[0:64, 2, 0:T], P1(f"filt_b{i + 1}", rows=64), P1("filt_freq", rows=64), ALU.add, ALU.mult))
                link(dve.tensor_scalar(wr, ph, 0.5 / math.pi, MAGIC, ALU.mult, ALU.add))
                link(dve.tensor_scalar(wr, wr, -MAGIC, None, ALU.add))
                link(dve.scalar_tensor_tensor(ph, wr, -TWO_PI_HI, ph, ALU.mult, ALU.add))
                link(dve.scalar_tensor_tensor(ph, wr, -TWO_PI_LO, ph, ALU.mult, ALU.add))
                dve.tensor_scalar(ph, ph, math.pi * (1 - 1e-7), -math.pi * (1 - 1e-7), ALU.min, ALU.max).then_inc(sem("hid_arg"), 1)
                if i == 0:
                    dve.wait_ge(sem("rstd_mix"), 1)
                    dve.wait_ge(sem("ss_mix"), 1)
                    for k in range(KD):
                        dve.scalar_tensor_tensor(a[:, k, :], h[:, k, :], P1("norm_mix", k), rstd, ALU.mult, ALU.mult).then_inc(sem("normed_mix"), 1)
            dve.wait_ge(sem("in_w3"), 32)
            n = 0
            for tt in range(3):
                for c in range(4):
                    dve.wait_ge(sem("filt_ps"), n + 1)
                    dve.tensor_tensor(filt[0:TW[tt], tt, c, :], ps[0:TW[tt], 4 + n % 4, :], window[0:TW[tt], tt, :], ALU.mult).then_inc(sem("filt"), 1)
                    n += 1
            dve.wait_ge(sem("filt"), 12)
            link(dve.memset(filt[0:1, 0, 2:4, :], 0.0))
            for rows, tiles in ((P, slice(0, 2)), (TW[2], slice(2, 3))):
                fwd = filt[0:rows, tiles, 0:2, :].rearrange("p t o n -> p t (o n)")
                bwd = filt[0:rows, tiles, 2:4, :].rearrange("p t o n -> p t (o n)")
                dve.tensor_tensor(bwd, fwd, bwd, ALU.subtract).then_inc(sem("filt_sd"), 1)
                dve.wait_ge(sem("filt_sd"), 1 if rows == P else 3)
                dve.scalar_tensor_tensor(fwd, fwd, 2.0, bwd, ALU.mult, ALU.subtract).then_inc(sem("filt_sd"), 1)
            raw = P1("lb").rearrange("p (d r h) -> p d r h", d=2, r=2)
            dve.tensor_tensor(lb[:, :, 0, :], raw[:, :, 1, :], raw[:, :, 0, :], ALU.subtract).then_inc(sem("lb_diff"), 1)
            dve.wait_ge(sem("lb_exp"), 1)
            link(dve.tensor_scalar(lb[:, :, 1, :], lb[:, :, 0, :], 1.0, None, ALU.add))
            link(dve.reciprocal(lb[:, :, 0, :], lb[:, :, 1, :]))
            link(dve.tensor_scalar(lb[:, :, 1, :], lb[:, :, 0, :], -1.0, 1.0, ALU.mult, ALU.add))
            dve.wait_ge(sem("filt_ps"), 12)
            link(dve.memset(hg[:, :, 0:PADT], 0.0))
            dve.memset(hg[:, 0:1, 0:1], 0.0).then_inc(sem("hg_zero"), 1)
            for j in range(HY + HG):
                if j < HY:
                    job_evacuated(dve, j)
                    src = padded[:, j % 4, :]
                    y = conv[:, j, :]
                    link(dve.tensor_scalar(y, src[:, 0:T], P1("conv_w", j), P1("conv_b", j), ALU.mult, ALU.add))
                    link(dve.scalar_tensor_tensor(y, src[:, 1:T + 1], P1("conv_w", HY + j), y, ALU.mult, ALU.add))
                    dve.scalar_tensor_tensor(y, src[:, 2:T + 2], P1("conv_w", 2 * HY + j), y, ALU.mult, ALU.add).then_inc(sem("convolved"), 1)
                    if j < 4:
                        dve.wait_ge(sem("convolved"), j + 1)
                        dve.nop().then_inc(sem("z"), 1)
                elif not 24 <= j < 28:
                    dve.wait_ge(sem("strip_exp"), j - HY + 1 - (4 if j >= 28 else 0))
                    e = sig[:, j % 2, :]
                    y = hg[:, j - HY, PADT:TP]
                    link(dve.tensor_scalar(e, e, 1.0, None, ALU.add))
                    out = sem(f"strip_out{j % 2}")
                    if 16 <= j < 24:
                        dve.reciprocal(y, e).then_inc(out, 1)
                    else:
                        link(dve.reciprocal(e, e))
                        dve.tensor_tensor(y, strip_at(j), e, ALU.mult).then_inc(out, 1)
            dve.wait_ge(sem("spectrum"), 12)
            for o in range(2):
                for tt in range(3):
                    dve.wait_ge(sem("zt_ps"), 3 * o + tt + 1)
                    dve.tensor_copy(zt[0:TW[tt], tt, :], ps[0:TW[tt], 2 + tt % 2, :]).then_inc(sem("zt"), 1)
                for ft in range(3):
                    n = 3 * o + ft
                    w = TW[ft]
                    dve.wait_ge(sem("uf_ps"), n + 1)
                    uc, us = ps[0:w, 4 + 2 * (n % 2), :], ps[0:w, 5 + 2 * (n % 2), :]
                    kc, ks = spectra[0:w, ft, 2 * o, :], spectra[0:w, ft, 2 * o + 1, :]
                    yc, ys = yf[0:w, ft, 0, :], yf[0:w, ft, 1, :]
                    t1, t2 = prod[0:w, 0, :], prod[0:w, 1, :]
                    if n == 3:
                        dve.wait_ge(sem("conv_ps"), 4)
                    tick(dve.tensor_tensor(yc, uc, kc, ALU.mult))
                    tick(dve.tensor_tensor(t1, us, ks, ALU.mult))
                    tick(dve.tensor_tensor(ys, uc, ks, ALU.mult))
                    link(dve.tensor_tensor(t2, us, kc, ALU.mult))
                    link(dve.tensor_tensor(yc, yc, t1, ALU.subtract))
                    dve.tensor_tensor(ys, ys, t2, ALU.add).then_inc(sem("yf"), 1)
                    dve.wait_ge(sem("yf"), n + 1)
                for c in range(4):
                    z = conv[:, c, :]
                    dve.wait_ge(sem("conv_ps"), 4 * o + c + 1)
                    link(dve.scalar_tensor_tensor(z, z, P1("skip", 4 * o + c), ps[:, 2 + c % 2, 0:T], ALU.mult, ALU.add))
                    dve.tensor_tensor(z, z, conv[:, 4 * (o + 1) + c, :], ALU.mult).then_inc(sem("z"), 1)
            dve.wait_ge(sem("z"), 12)
            dve.wait_ge(sem("rstd_hy"), 1)
            for c in range(4):
                dve.scalar_tensor_tensor(conv[:, c, :], conv[:, c, :], P1("hyena_norm", c), rstd, ALU.mult, ALU.mult).then_inc(sem("mixed_hy"), 1)
            tick(dve.memset(f_k[:, :, 0:PADT], 0.0))
            link(dve.memset(f_lf[:, :, 0:PADT], 0.0))
            for it in range(2 * NH):
                hd, bwd, b = it // 2, it % 2, it % 2
                if it >= 2:
                    dve.wait_ge(sem("scan_ps"), it - 1)
                s = hg[:, 4 + 4 * bwd + hd, PADT:TP]
                link(dve.tensor_scalar(f_lf[:, b, PADT:TP], s, lb[:, bwd, 1, hd:hd + 1], lb[:, bwd, 0, hd:hd + 1], ALU.mult, ALU.add))
                dve.tensor_scalar(f_k[:, b, PADT:TP], f_lf[:, b, PADT:TP], -1.0, 1.0, ALU.mult, ALU.add).then_inc(sem("forget"), 1)
                dve.wait_ge(sem("log_f"), it + 1)
                order = slice(None, None, -1) if bwd else slice(None)
                cum, rel = f_cum[:, b, :], f_rel[:, b, :]
                link(dve.tensor_tensor_scan(cum[:, order], C("run"), f_lf[:, b, :][:, order], 0.0, ALU.mult, ALU.add))
                c3 = cum.rearrange("p (c t) -> p c t", t=CH)
                mid_at, end_at = (CH - 1 - CH // 2, 0) if bwd else (CH // 2, CH - 1)
                tick(dve.tensor_tensor(rel.rearrange("p (c t) -> p c t", t=CH), c3, c3[:, :, mid_at:mid_at + 1].to_broadcast([P, NCH, CH]), ALU.subtract))
                dve.tensor_tensor(f_kd[:, b, :].rearrange("p (c t) -> p c t", t=CH), c3[:, :, end_at:end_at + 1].to_broadcast([P, NCH, CH]), c3,
                                  ALU.subtract).then_inc(sem("cum"), 1)
                dve.wait_ge(sem("scan_exp"), 5 * it + 5)
                tick(dve.tensor_tensor(f_q[:, b, :], f_q[:, b, :], hg[:, hd, :], ALU.mult))
                tick(dve.tensor_tensor(f_kk[:, b, :], f_kk[:, b, :], f_k[:, b, :], ALU.mult))
                tick(dve.tensor_tensor(f_qe[:, b, :], f_qe[:, b, :], hg[:, hd, :], ALU.mult))
                dve.tensor_tensor(f_kd[:, b, :], f_kd[:, b, :], f_k[:, b, :], ALU.mult).then_inc(sem("scan_in"), 1)
                dve.wait_ge(sem("scores_ps"), it + 1)
                mask = C("anticausal" if bwd else "causal", CH).unsqueeze(1).to_broadcast([CH, NCH, CH])
                dve.tensor_tensor(sc_m[0:CH, b, :].rearrange("p (c t) -> p c t", t=CH), ps[0:CH, 2, 0:TP].rearrange("p (c t) -> p c t", t=CH),
                                  mask, ALU.mult).then_inc(sem("scores"), 1)
                dve.wait_ge(sem("state_ps"), it + 1)
                st = states[:, b, :].rearrange("p (c n) -> p c n", n=P)
                u = ps[:, 4, :].rearrange("p (c n) -> p c n", n=P)
                if bwd:
                    link(dve.tensor_copy(st[:, 3, :], u[:, 3, :]))
                    for i in (2, 1):
                        link(dve.scalar_tensor_tensor(st[:, i, :], st[:, i + 1, :], decay[:, b, i + 1:i + 2], u[:, i, :], ALU.mult, ALU.add))
                    dve.scalar_tensor_tensor(st[:, 0, :], st[:, 1, :], decay[:, b, 1:2], u[:, 0, :], ALU.mult, ALU.add).then_inc(sem("state"), 1)
                    dve.wait_ge(sem("scan_ps"), it + 1)
                    dve.tensor_copy(hg[:, 4 + hd, PADT:TP], ps[:, 5 + hd % 2, PADT:TP]).then_inc(sem("head"), 1)
                else:
                    link(dve.tensor_copy(st[:, 0, :], u[:, 0, :]))
                    for i in (1, 2):
                        link(dve.scalar_tensor_tensor(st[:, i, :], st[:, i - 1, :], decay[:, b, i:i + 1], u[:, i, :], ALU.mult, ALU.add))
                    dve.scalar_tensor_tensor(st[:, 3, :], st[:, 2, :], decay[:, b, 3:4], u[:, 3, :], ALU.mult, ALU.add).then_inc(sem("state"), 1)
            for hd in range(NH):
                dve.wait_ge(sem("rstd_head"), hd + 1)
                o = hg[:, 4 + hd, PADT:TP]
                link(dve.scalar_tensor_tensor(o, o, P1("hgrn_norm", hd), head_sq[:, hd, :], ALU.mult, ALU.mult))
                dve.tensor_tensor(hg[:, hd, PADT:TP], o, hg[:, 16 + hd, PADT:TP], ALU.mult).then_inc(sem("mixed_hg"), 1)
            for c in range(KD):
                j = HY + HG + c
                dve.wait_ge(sem("strip"), j + 1)
                dve.tensor_tensor(h[:, c, META:T], h[:, c, META:T], ps[:, j % 2, 0:SEQ], ALU.add).then_inc(sem(f"strip_out{j % 2}"), 1)
            dve.wait_ge(sem("ss_ffn"), 1)
            dve.wait_ge(sem("rstd_ffn"), 1)
            for k in range(KD):
                dve.scalar_tensor_tensor(an[:, k, :], x_tok[:, k, :], P1("norm_ffn", k), rstd[:, 0:SEQ], ALU.mult, ALU.mult).then_inc(sem("normed_ffn"), 1)
            for n in range(2 * KD):
                dve.wait_ge(sem("xn_ps"), n + 1)
                dve.tensor_copy(xn[:, n // KD, (n % KD) * P:(n % KD + 1) * P], ps[:, 3 + n % 4, 0:P]).then_inc(sem("xn"), 1)

            def sm(i, n=8):
                return small[:, 2 * i:2 * i + 2, 0:n]

            def bc(v, n):
                return v.to_broadcast([P, 2, n])

            def first_max(values, best, hot, t1):
                link(dve.tensor_reduce(best, values, AX, ALU.max))
                link(dve.tensor_tensor(t1, values, bc(best, 8), ALU.is_ge))
                link(dve.tensor_scalar(t1, t1, -64.0, 64.0, ALU.mult, ALU.add))
                link(dve.tensor_tensor(t1, t1, eight, ALU.add))
                link(dve.tensor_reduce(hot[:, :, 0:1], t1, AX, ALU.min))
                link(dve.tensor_copy(first, hot[:, :, 0:1]))
                link(dve.tensor_tensor(hot, eight, bc(first, 8), ALU.is_equal))

            eight = C("eight").unsqueeze(1).to_broadcast([P, 2, 8])
            g_hot, e_sel, e1_hot, e2_hot, t1 = sm(3), sm(4), sm(5), sm(6), sm(8)
            g_max, e1_max, e2_max, second, first, total, top = (sm(i, 1) for i in (0, 1, 9, 7, 10, 11, 3))
            total, w1, w2 = small[:, 22:24, 0:1], small[:, 22:24, 1:2], small[:, 22:24, 2:3]
            dve.wait_ge(sem("logits_ps"), 1)
            link(dve.tensor_copy(xr(logits), ps[:, 7, 0:2 * (NG + NE)]))
            lg, le = logits[:, :, 0:NG], logits[:, :, NG:NG + NE]
            first_max(lg, g_max, g_hot, t1)
            link(dve.tensor_tensor(sm(2), lg, bc(g_max, 8), ALU.subtract))
            link(dve.tensor_tensor(pick.rearrange("p t (g e) -> p t g e", g=NG), le.rearrange("p t (g e) -> p t g e", g=NG),
                                   g_hot.unsqueeze(3).to_broadcast([P, 2, NG, EPG]), ALU.mult))
            for tt in range(2):
                link(dve.tensor_reduce(e_sel[:, tt, :], pick[:, tt, :].rearrange("p (g e) -> p e g", g=NG), AX, ALU.add))
            first_max(e_sel, e1_max, e1_hot, t1)
            link(dve.scalar_tensor_tensor(e_sel, e1_hot, -BIG, e_sel, ALU.mult, ALU.add))
            first_max(e_sel, e2_max, e2_hot, t1)
            dve.tensor_tensor(second, e2_max, e1_max, ALU.subtract).then_inc(sem("route_arg"), 1)
            dve.wait_ge(sem("route_exp"), 2)
            link(dve.tensor_reduce(total, sm(2), AX, ALU.add))
            link(dve.tensor_scalar(w1, second, 1.0, None, ALU.add))
            link(dve.tensor_tensor(w1, w1, total, ALU.mult))
            link(dve.reciprocal(w1, w1))
            link(dve.tensor_tensor(w2, w1, second, ALU.mult))
            link(dve.tensor_tensor(t1, e1_hot, e2_hot, ALU.add))
            link(dve.tensor_tensor(e1_hot, e1_hot, bc(w1, 8), ALU.mult))
            link(dve.tensor_tensor(e2_hot, e2_hot, bc(w2, 8), ALU.mult))
            link(dve.tensor_tensor(e1_hot, e1_hot, e2_hot, ALU.add))

            def spread(out, per_expert):
                for tt in range(2):
                    ins = dve.tensor_tensor(out[:, tt, :].rearrange("p (g e) -> p g e", g=NG), g_hot[:, tt, :].unsqueeze(2).to_broadcast([P, NG, EPG]),
                                            per_expert[:, tt, :].unsqueeze(1).to_broadcast([P, NG, EPG]), ALU.mult)
                    link(ins)
            spread(pick, e1_hot)
            spread(chosen, t1)
            dve.nop().then_inc(sem("chosen"), 1)
            dve.wait_ge(sem("slots_ps"), 1)
            link(dve.scalar_tensor_tensor(xr(slot_of), ps[:, 7, 0:2 * NE], 1.0, xr(chosen), ALU.add, ALU.mult))
            link(dve.tensor_scalar(xr(slot_of), xr(slot_of), -1.0, None, ALU.add))
            link(dve.tensor_reduce(first[:, 0, :], ps[:, 7, 2 * NE:3 * NE], AX, ALU.max))
            link(dve.tensor_scalar(first[:, 0, :], first[:, 0, :], 1.0 / CAP, 0.5 - 0.5 / CAP, ALU.mult, ALU.add))
            link(dve.tensor_scalar(first[:, 0, :], first[:, 0, :], MAGIC, -MAGIC, ALU.add, ALU.add))
            dve.tensor_copy(rounds[:, 0:1], first[:, 0, :]).then_inc(sem("rounds"), 1)
            dve.wait_ge(sem("rounds"), 1)
            n_rounds = dve.value_load(rounds[0:1, 0:1], min_val=1, max_val=SEQ // CAP)
            mc = Chain(dve, sem("expert_chain"))
            per = 4
            slots = C("slots").unsqueeze(1).to_broadcast([P, GRP, CAP])
            with dve.Fori(0, n_rounds) as r:
                with dve.Fori(0, NGRP) as g:
                    it = dve.snap(r * NGRP + g)
                    mc.turn(it, per, 0)
                    for tt in range(2):
                        mc.tick(dve.tensor_tensor(onehot[:, tt, :].rearrange("p (e s) -> p e s", e=GRP), slots,
                                                  slot_of[:, tt, bass.ds(g * GRP, GRP)].unsqueeze(2).to_broadcast([P, GRP, CAP]), ALU.is_equal))
                    dve.wait_ge(mc.sem, mc.base + mc.n)
                    for tt in range(2):
                        ins = dve.tensor_tensor(weighted[:, tt, :].rearrange("p (e s) -> p e s", e=GRP), onehot[:, tt, :].rearrange("p (e s) -> p e s", e=GRP),
                                                pick[:, tt, bass.ds(g * GRP, GRP)].unsqueeze(2).to_broadcast([P, GRP, CAP]), ALU.mult)
                    ins.then_inc(sem("onehot"), 1)
                    dve.wait_ge(sem("gather_ps"), it + 1)
                    for j in range(2):
                        dve.tensor_copy(xr(xg[:, 4 * j:4 * j + 4, :]), ps[:, 4 + j, :]).then_inc(sem("xg"), 1)
                    dve.wait_ge(sem("gate_exp"), it + 1)
                    mc.link(dve.tensor_scalar(gate_e, gate_e, 1.0, None, ALU.add))
                    mc.link(dve.reciprocal(gate_e, gate_e))
                    dve.tensor_tensor(gate_e, ps[:, 0, :], gate_e, ALU.mult).then_inc(sem("gated"), 1)
                    dve.wait_ge(sem("gated"), it + 1)
                    dve.wait_ge(sem("unit_free"), it * 12 + 6 + 8)
                    dve.tensor_tensor(mid, gate_e, ps[:, 1, :], ALU.mult).then_inc(sem("mid"), 1)
                    dve.wait_ge(sem("unit_free"), it * 12 + 6 + 12)
                    for half in range(2):
                        dve.tensor_copy(y_slot[:, half * 512:(half + 1) * 512], ps[:, 2 + half, :]).then_inc(sem("y_slot"), 1)
                    dve.wait_ge(sem("back"), it + 1)
                    dve.wait_ge(sem("scatter_ps"), it + 1)
                    for k in range(0, KD, 2):
                        dve.tensor_tensor(x_tok[:, k:k + 2, :], x_tok[:, k:k + 2, :], ps[:, 4 + k // 2, :].rearrange("p (k t) -> p k t", k=2),
                                          ALU.add).then_inc(sem("scattered"), 1)
                    dve.wait_ge(sem("scattered"), it * 4 + 4)
                    mc.end_turn(per)
                dve.tensor_scalar(xr(slot_of), xr(slot_of), -float(CAP), None, ALU.add).then_inc(sem("round_end"), 1)
                dve.wait_ge(sem("round_end"), r + 1)
            dve.nop().then_inc(sem("experts_done"), 1)
            dve.wait_ge(sem("ss_final"), 1)
            dve.wait_ge(sem("rstd_final"), 1)
            for k in range(KD):
                dve.scalar_tensor_tensor(x_tok[:, k, :], x_tok[:, k, :], P1("norm_final", k), rstd[:, 0:SEQ], ALU.mult, ALU.mult).then_inc(sem("x_final"), 1)

        block_one.__exit__(None, None, None)
        if stop_after:
            return
        nc.clear_and_free_semaphores(list(named.values()))
        named.clear()
        nc.all_engine_barrier()
        with nc.Block() as block:
            @block.sync
            def _(sp):
                layers_sync(sp)

            @block.tensor
            def _(pe):
                layers_pe(pe)

            @block.scalar
            def _(act):
                layers_act(act)

            @block.vector
            def _(dve):
                layers_dve(dve)


INPUTS = ["const", "fourier", "features", "param1", "filt_w1", "filt_w2", "filt_w3", "h", "w_first", "router",
          "w_gate", "w_up", "w_down", "positions", "mem", "w_layers", "param2", "w_if", "gm_ws", "gm_rows"]


def strips(w):
    w = np.asarray(w)
    n = w.shape[1] // P
    return w.reshape(KD, P, n, P).transpose(2, 1, 0, 3).reshape(n, P, KD * P)


def units(s):
    return s.reshape(-1, 4, P, KD * P).transpose(0, 2, 1, 3).reshape(-1, P, WSLOT)


def layout(a):
    out = {}
    shape, fourier, features, first = shape_constants(), filter_constants(), filter_features(), first_params(a)
    out["const"], out["fourier"], out["features"], out["param1"] = (c.array() for c in (shape, fourier, features, first))
    for n in ("filt_w1", "filt_w2", "filt_w3"):
        out[n] = a[n][0]
    tokens = np.concatenate([a["meta_tokens"], a["x"][0]], axis=0)
    out["h"] = tokens.T.reshape(KD, P, T).transpose(1, 0, 2).reshape(P, KD * T)
    out["w_first"] = np.concatenate([units(strips(a["w_in"][0])), units(strips(a["w_out"][0]))])
    router = np.concatenate([a["w_router_group"][0], a["w_router_expert"][0].reshape(D, NE)], axis=1)
    out["router"] = router.reshape(KD, P, NG + NE).transpose(1, 0, 2).reshape(P, -1)
    for n in ("w_gate", "w_up", "w_down"):
        out[n] = a[n][0]
    out["positions"] = a["positions_2"].reshape(SEQ)
    out["mem"] = a["mem_2"][0].T.reshape(KD, P, SEQ).transpose(1, 0, 2).reshape(P, -1)
    params = [layer_params(a, l) for l in range(LAYERS)]
    out["param2"] = np.stack([c.array() for c in params])
    w = HALF
    ml, gates = 4 * w, 9 * w
    gm = gates + 8
    rt, xa, mg = gm + 3 * w, gm + 7 * w, gm + 9 * w
    layers = []
    for l in range(LAYERS):
        w_in = a["w_in_2"][l]
        column = [xa, xa + w, 0, w, 2 * w, 3 * w] + [ml + i * w for i in range(5)] + [gm + i * w for i in range(3)] + [rt + i * w for i in range(4)]
        parts = [units(strips(a["w_mem_kv_2"][l]))]
        parts += [units(strips(w_in[:, c:c + w])) for c in column]
        gate = strips(w_in[:, mg:]).reshape(NBR, KD, P, KD * P)
        up = a["w_up_2"][l].reshape(NBR, 4, P, KD, P).transpose(0, 3, 2, 1, 4).reshape(NBR, KD, P, 4 * P)
        pair = np.concatenate([gate, up], axis=3).transpose(1, 0, 2, 3).reshape(-1, 2, P, 1536).transpose(0, 2, 1, 3).reshape(-1, P, 3072)
        parts.append(np.concatenate([pair, np.zeros((len(pair), P, WSLOT - 3072), np.float32)], axis=2))
        parts.append(units(strips(a["w_out_2"][l])))
        layers.append(np.concatenate(parts))
    out["w_layers"] = np.concatenate(layers)
    out["w_if"] = a["w_in_2"][:, :, gates:gates + 8].reshape(LAYERS, KD, P, 8).transpose(0, 2, 1, 3).reshape(LAYERS, P, -1)
    out["gm_ws"] = a["gm_ws_2"].transpose(0, 3, 1, 2).reshape(LAYERS, P, -1)
    out["gm_rows"] = np.stack([a["gm_ln_g_2"], a["gm_ln_b_2"], a["gm_bs_2"].reshape(LAYERS, HALF)], axis=1).reshape(LAYERS, -1)
    return out, {"shape": shape.at, "first": first.at, "layer": params[0].at}


def kernel(stop_after=None, **inputs):
    import concourse.bacc as bacc
    from concourse.bass_utils import run_bass_kernel_spmd

    arrays, spot = layout({k: np.asarray(v) for k, v in inputs.items()})
    nc = bacc.Bacc("TRN2", target_bir_lowering=False, num_devices=1)
    send, d = {}, {}
    for name in INPUTS:
        v = np.ascontiguousarray(arrays[name])
        send[f"in_{name}"] = v
        d[name] = nc.dram_tensor(f"in_{name}", v.shape, mybir.dt.from_np(v.dtype), kind="ExternalInput").ap()
    d["out"] = nc.dram_tensor("out", (D, SEQ), F32, kind="ExternalOutput").ap()
    build_program(nc, d, spot, stop_after)
    r = run_bass_kernel_spmd(nc, [send], core_ids=[0])
    return r.results[0]["out"].T.reshape(1, SEQ, D)
```

```python
import math
from contextlib import ExitStack

import numpy as np
import concourse.bass as bass
from concourse import mybir

F32 = mybir.dt.float32
I32 = mybir.dt.int32
ALU = mybir.AluOpType
ACT = mybir.ActivationFunctionType
AX = mybir.AxisListType.X

P = 128
D = 1024
KD = D // P
SEQ = 256
META = 16
T = META + SEQ
HALF = D // 2
HY = 3 * HALF // P
HG = 5 * HALF // P
CH = 64
PADT = (-META) % CH
TP = T + PADT
NCH = TP // CH
NF = T
TW = [P, P, T - 2 * P]
NE, NG, EPG = 64, 8, 8
CAP = 32
GRP = 4
NGRP = NE // GRP
FE = HALF
LAYERS = 2
NH, HD = 4, 128
NC2 = SEQ // CH
NBR = 5
EPS = 1e-6
MAGIC = 12582912.0
TWO_PI_HI = 6.28125
TWO_PI_LO = 2 * math.pi - 6.28125
BIG = 1e30
SCALE = HD ** -0.5

WSLOT = 4096
RING = 6
RING1 = 4
HEAD_BANKS = (2, 3, 5, 7)
RING2 = 3
UNIT_GROUPS = [("sb_q",), ("sb_k",), ("sb_v",), ("sb_z",), ("mem_k", "xa_q"), ("mem_v",), ("xa_z",), ("ml_q", "ml_k"),
               ("ml_v",), ("ml_o",), ("ml_z",), ("rt_q", "rt_k"), ("rt_v",), ("gm_v",), ("rt_z", "gm_u"), ("gm_z",)]
ON_TOKENS = ("mem_v", "sb_v", "ml_v", "rt_v", "gm_v")
MERGE_ORDER = (4, 0, 1, 3, 2)
SHARED_W = 28300


class Pack:

    def __init__(self):
        self.parts, self.at, self.n = [], {}, 0

    def add(self, name, a):
        a = np.asarray(a, np.float32)
        full = np.zeros((P, a.shape[1]), np.float32)
        full[: a.shape[0]] = a
        self.at[name] = (self.n, a.shape[1])
        self.parts.append(full)
        self.n += a.shape[1]

    def array(self):
        return np.ascontiguousarray(np.concatenate(self.parts, axis=1))


def tiles_of(a):
    out = np.zeros((3 * P, a.shape[1]), np.float32)
    out[: a.shape[0]] = a
    return out.reshape(3, P, -1).transpose(1, 0, 2).reshape(P, -1)


def shape_constants():
    c = Pack()
    i = np.arange(P)
    c.add("ident", np.eye(P))
    c.add("ones", np.ones((P, P)))
    c.add("before", i[:, None] < i[None, :])
    c.add("notbefore", i[:, None] >= i[None, :])
    rot = np.zeros((P, P))
    rot[np.arange(64) + 64, np.arange(64)] = -1
    rot[np.arange(64), np.arange(64) + 64] = 1
    c.add("rot", rot)
    mq = np.zeros((P, 2, SEQ))
    for kt in range(2):
        mq[:, kt] = (kt * P + i)[:, None] < np.arange(SEQ)[None, :]
    c.add("keymask", mq.reshape(P, -1))
    s = np.arange(P) % CH
    t = np.arange(CH)
    c.add("causal", s[:, None] <= t[None, :])
    c.add("anticausal", s[:, None] >= t[None, :])
    c.add("causal_neg", np.where(s[:, None] <= t[None, :], 0.0, -BIG))
    lg = np.log(1.0 - 2.0 ** (-5.0 - np.arange(NH)))
    c.add("rt_decay", (np.exp(lg[None, :, None] * np.abs(s[:, None, None] - t[None, None, :])) * SCALE).reshape(P, -1))
    c.add("rt_wq", np.broadcast_to(np.exp(lg[:, None] * (t + 1.0))[None], (P, NH, CH)).reshape(P, -1))
    c.add("rt_wend", np.exp(lg[None, :] * (CH - 1 - s)[:, None]) * SCALE)
    half = HD // 2
    inv = (np.float32(10000.0) ** (-(np.arange(half, dtype=np.float32) / np.float32(half)))).astype(np.float32)
    c.add("inv_freq", np.concatenate([inv, inv])[:, None])
    sel = np.zeros((4, 4, P))
    sel[np.arange(4), np.arange(4)] = 1
    c.add("sel", sel.reshape(4, -1))
    c.add("run", np.broadcast_to((np.arange(TP) % CH != 0)[None], (P, TP)))
    c.add("restart", np.broadcast_to(np.where(np.arange(SEQ) % CH, 0.0, -BIG)[None], (4, SEQ)))
    c.add("slots", np.broadcast_to(np.arange(CAP)[None], (P, CAP)))
    c.add("eight", np.broadcast_to(np.arange(8)[None], (P, 8)))
    c.add("eps", np.full((P, 1), EPS))
    return c


def filter_constants():
    c = Pack()
    th = np.pi * (2 * np.arange(NF) + 1) / (2 * T)
    ang = np.arange(T)[:, None] * th[None, :]
    c.add("cos", tiles_of(np.cos(ang)))
    c.add("sin", tiles_of(np.sin(ang)))
    c.add("icos", tiles_of(np.cos(ang).T / T))
    c.add("isin", tiles_of(np.sin(ang).T / T))
    return c


def filter_features():
    c = Pack()
    f = np.float32
    pos = np.arange(T, dtype=f)
    t = (pos / f(T - 1)).astype(f)
    bands = np.linspace(1e-4, 15, 16, dtype=f)
    ang = (f(2.0 * math.pi / T) * pos[:, None] * bands[None, :]).astype(f)
    z = np.concatenate([t[:, None], np.cos(ang), -np.sin(ang)], axis=-1)
    c.add("features", z.T)
    deltas = np.abs(np.linspace(math.log(1e-2) / 1.5, math.log(1e-2) / 0.3, HALF, dtype=f))
    c.add("window", tiles_of(np.exp(-t[:, None] * deltas[None, :])))
    return c


def cols(v):
    v = np.asarray(v)
    return v.reshape(-1, P).T


def first_params(a):
    c = Pack()
    c.add("norm_mix", cols(a["norm_mix"]))
    c.add("norm_ffn", cols(a["norm_ffn"]))
    c.add("norm_final", cols(a["norm_final"]))
    c.add("conv_w", cols(a["conv_w"]))
    c.add("conv_b", cols(a["conv_b"]))
    c.add("skip", cols(a["filt_skip"]))
    c.add("hyena_norm", cols(a["hyena_norm"]))
    c.add("lb", np.concatenate([cols(a["lb_fwd"]), cols(a["lb_bwd"])], axis=1))
    c.add("hgrn_norm", cols(a["hgrn_norm"]))
    c.add("filt_b1", np.asarray(a["filt_b1"]).T)
    c.add("filt_b2", np.asarray(a["filt_b2"]).T)
    c.add("filt_freq", np.asarray(a["filt_freq"]).T)
    return c


def layer_params(a, l):
    c = Pack()
    c.add("norm_pre", cols(a["norm_pre_2"][l]))
    c.add("norm_post", cols(a["norm_post_2"][l]))
    c.add("mem_norm", cols(a["mem_norm_2"][l]))
    c.add("conv_q", cols(a["conv_q_2"][l]))
    c.add("conv_k", cols(a["conv_k_2"][l]))
    c.add("b_i", np.asarray(a["b_igate_2"][l])[:, None])
    c.add("b_f", np.asarray(a["b_fgate_2"][l])[:, None])
    return c


class Chain:

    def __init__(self, eng, sem):
        self.eng, self.sem, self.base, self.n = eng, sem, 0, 0

    def tick(self, ins):
        self.n += 1
        ins.then_inc(self.sem, 1)

    def link(self, ins):
        self.tick(ins)
        self.eng.wait_ge(self.sem, self.base + self.n)

    def turn(self, i, per, start):
        self.base, self.n = start + i * per, 0

    def end_turn(self, per):
        assert self.n == per, (self.sem, self.n)


class Layout:

    def __init__(self, arena, at=0):
        self.arena, self.at = arena, at

    def take(self, *dims):
        n = int(np.prod(dims))
        v = self.arena[:, self.at:self.at + n]
        self.at += n
        if len(dims) == 2:
            v = v.rearrange("p (a b) -> p a b", b=dims[1])
        elif len(dims) == 3:
            v = v.rearrange("p (a b c) -> p a b c", b=dims[1], c=dims[2])
        return v



def norm_squares(act, src, squares, done):
    act.activation(squares, src, ACT.Square).then_inc(done, 1)


def norm_sum(pe, ones, squares, n, out, done):
    for k in range(n):
        last = pe.matmul(out, ones, squares[:, k, :], start=(k == 0), stop=(k == n - 1))
    last.then_inc(done, 1)


def norm_rstd(act, chain, out, total, width, eps, done):
    chain.link(act.activation(out, total, ACT.Ln, bias=eps, scale=1.0 / width))
    act.activation(out, out, ACT.Exp, scale=-0.5).then_inc(done, 1)


def build_program(nc, d, spot):
    with ExitStack() as ctx:
        named = {}

        def sem(name):
            if name not in named:
                named[name] = nc.alloc_semaphore(name)
            return named[name]

        ring = ctx.enter_context(nc.sbuf_tensor("ring", [P, RING, WSLOT], F32))
        arena = ctx.enter_context(nc.sbuf_tensor("arena", [P, SHARED_W], F32))
        rounds = ctx.enter_context(nc.sbuf_tensor("rounds", [P, 2], I32))
        pos_i = ctx.enter_context(nc.sbuf_tensor("pos_i", [P, SEQ], I32))
        ps = ctx.enter_context(nc.psum_tensor("ps", [P, 8, 512], F32))

        lay = Layout(arena)
        n_const = sum(w for _, w in spot["shape"].values())
        const = lay.take(n_const)
        param1 = lay.take(sum(w for _, w in spot["first"].values()))
        lb = lay.take(2, 2, 4)
        h = lay.take(KD, T)
        a = lay.take(KD, T)
        rstd = lay.take(T)
        w_param2 = sum(w for _, w in spot["layer"].values())
        param2 = lay.take(LAYERS * w_param2)
        rope = lay.take(2, SEQ)
        free_at = lay.at

        def C(name, rows=P):
            at, w = spot["shape"][name]
            return const[0:rows, at:at + w]

        def P1(name, i=None, rows=P):
            at, w = spot["first"][name]
            return param1[0:rows, at:at + w] if i is None else param1[0:rows, at + i:at + i + 1]

        ident, ones, eps = C("ident"), C("ones"), C("eps")

        m1 = Layout(arena, free_at)
        four = m1.take(4, 3, NF)
        cosm, sinm, icos, isin = (four[:, j] for j in range(4))
        conv = m1.take(HY, T)
        hg = m1.take(HG, TP)
        assert m1.at <= SHARED_W, m1.at
        scratch = ring[:, RING1:RING, :].rearrange("p a b -> p (a b)")
        m2 = Layout(scratch)
        filt = m2.take(3, 4, HALF)
        padded = m2.take(4, T + 2)
        sig = m2.take(2, T)
        assert m2.at <= 2 * WSLOT

        def xr(v):
            return v.rearrange("p a b -> p (a b)")
        feat = hg[:, :, :].rearrange("p a b -> p (a b)")
        m3 = Layout(feat)
        zT = m3.take(T)
        window = m3.take(3, HALF)
        fw1 = m3.take(64)
        fw2 = m3.take(64)
        fw3 = m3.take(4, HALF)
        hid = m3.take(T)
        wrap = m3.take(T)
        assert m3.at <= HG * TP

        JOB_AT, STEP_OF, JOB_ENDS, at = {}, {}, [], 0
        for group in UNIT_GROUPS:
            for i, n in enumerate(group):
                JOB_AT[n], STEP_OF[n] = at + i, len(group)
            at += sum(2 if n in ON_TOKENS else 4 for n in group)
            JOB_ENDS += [at - len(group) + 1 + i for i in range(len(group))]
        UNIT_AT = {n: i for i, n in enumerate(n for group in UNIT_GROUPS for n in group)}
        PAIRS = KD * NBR
        MERGE_AT = at
        for _ in range(PAIRS // 2):
            at += 4
            JOB_ENDS.append(at)
        OUT_AT = at
        for _ in range(2):
            at += 4
            JOB_ENDS.append(at)
        JOBS = at
        NU = len(JOB_ENDS)
        assert JOBS % 2 == 0 and NU % RING2 == 0

        def job(name, i):
            return JOB_AT[name] + i * STEP_OF[name]

        ly = Layout(arena, free_at)
        w_if = ly.take(KD, 8)
        y_all = ly.take(NBR, 4, SEQ)
        esig = ly.take(2, SEQ)
        gm_ws = ly.take(4, P)
        gm_rows = ly.take(3, HALF)
        mean_of = ly.take(P)
        xa_s = ly.take(8, 4)
        gm_st, gm_mv, gm_x = ly.take(2, 8), ly.take(2, 2), ly.take(2, P)
        rt_q, rt_k, rt_v = ly.take(4, SEQ), ly.take(4, SEQ), ly.take(2, HALF)
        r_mem = ly.at
        mem_t = ly.take(KD, SEQ)
        ml_qk = arena[:, r_mem:r_mem + 8 * SEQ]
        la = Layout(arena, r_mem)
        ml_q, ml_k = la.take(4, SEQ), la.take(4, SEQ)
        r_two = ly.at
        mem_sq = ly.take(KD, SEQ)
        mem_raw = ly.take(KD, SEQ)
        hn_mem = ly.take(SEQ)
        la = Layout(arena, r_two)
        xa_l, xa_t = la.take(2, 2, SEQ), la.take(2, 2, SEQ)
        la = Layout(arena, r_two)
        gm_u, gm_v = la.take(4, SEQ), la.take(2, HALF)
        assert ly.at <= SHARED_W, (ly.at, SHARED_W)
        spare = ring[:, RING2:RING, :].rearrange("p a b -> p (a b)")
        lw = Layout(spare)
        sb_q, sb_k, sb_v = lw.take(4, SEQ), lw.take(4, SEQ), lw.take(2, HALF)
        sb_z, sb_sp, sb_w = lw.take(2, 2 * SEQ), lw.take(2 * SEQ), lw.take(2 * SEQ)
        keyneg = lw.take(2 * SEQ)
        r_three = lw.at
        lw = Layout(spare)
        wide = lw.take(8, SEQ + 4)
        wide_flat = spare[:, 0:8 * SEQ]
        ml_v = lw.take(2, NH, HD + 1)
        ml_o = lw.take(4, SEQ)
        assert lw.at <= r_three
        lw = Layout(spare)
        hn_sq, hn_r = lw.take(4, SEQ), lw.take(4, SEQ)
        lw = Layout(spare, r_three)
        mem_k, mem_v, xa_q = lw.take(4, SEQ), lw.take(2, HALF), lw.take(4, SEQ)
        lw = Layout(spare, r_three)
        ml_rows = lw.take(776)
        ml_bc = lw.take(776)
        ml_d, ml_s = lw.take(2, CH), lw.take(2, CH)
        ml_st, ml_nb = lw.take(3, HD + 1), lw.take(3, P)
        ml_kw, ml_qd = lw.take(2, P), lw.take(SEQ)
        ml_col = lw.take(16)
        ml_g = lw.take(5, SEQ)
        ml_c = lw.take(6, 8)
        assert lw.at <= (RING - RING2) * WSLOT
        lw = Layout(spare, r_three)
        rt_t = lw.take(2, 2 * SEQ)
        rt_s, rt_st = lw.take(2, CH), lw.take(3, P)
        rt_kw, rt_qd = lw.take(2, P), lw.take(SEQ)
        lw = Layout(spare, r_three)
        merged = lw.take(KD, SEQ)
        post_sq = lw.take(KD, SEQ)
        assert lw.at <= (RING - RING2) * WSLOT
        post = y_all.rearrange("p a b c -> p (a b c)")[:, 0:KD * SEQ].rearrange("p (a b) -> p a b", b=SEQ)
        JEXP_AT = {"sb_z": (0, 1), "xa_z": (4, 1), "ml_z": (8, 1), "rt_z": (12, 1), "gm_z": (16, 1)}
        JEXPS = 20
        ACT_LINKS = 17
        DVE_LINKS = 280

        def P2(l, name, i=0, rows=P):
            at, w = spot["layer"][name]
            return param2[0:rows, bass.ds(l * w_param2 + at + i, 1)]

        def halves(v, par):
            return v.rearrange("p (a r t) -> p a r t", r=2, t=CH)[:, :, par, :]

        def by_tile(v):
            return v.rearrange("p (a t) -> p a t", t=CH)

        def job_done(eng, l, j):
            eng.wait_ge(sem("job"), l * JOBS + JOBS + j + 1)

        def evacuated(eng, l, j):
            eng.wait_ge(sem(f"job_out{j % 2}"), l * (JOBS // 2) + JOBS // 2 + j // 2 + 1)

        def unit_evacuated(eng, l, name):
            last = 1 if name in ON_TOKENS else 3
            if STEP_OF[name] == 1:
                evacuated(eng, l, job(name, last - 1))
            evacuated(eng, l, job(name, last))

        def layers_sync(sp):
            with sp.Fori(0, LAYERS) as l:
                w2 = d["w_layers"]
                for u in range(NU):
                    s = u % RING2
                    before = JOB_ENDS[u - RING2] if u >= RING2 else JOB_ENDS[NU - RING2 + u] - JOBS
                    job_done(sp, l, before - 1)
                    width = 3072 if len(UNIT_AT) <= u < len(UNIT_AT) + PAIRS // 2 else WSLOT
                    sp.dma_start(ring[:, s, 0:width], w2[bass.ds(l * NU + u, 1), :, 0:width].rearrange("a p n -> (a p) n")).then_inc(sem(f"w3_in{s}"), 16)
            out = d["out"].rearrange("(k p) t -> p k t", p=P)
            for k in range(0, KD, 2):
                sp.wait_ge(sem("x_out"), LAYERS * KD + k + 2)
                sp.dma_start(out[:, k:k + 2, :], x_tok[:, k:k + 2, :]).then_inc(sem("out"), 16)
            sp.wait_ge(sem("out"), 16 * KD // 2)

        def layers_pe(pe):
            pe.sem_inc(sem("job"), JOBS)
            pe.sem_inc(sem("job_out0"), JOBS // 2)
            pe.sem_inc(sem("job_out1"), JOBS // 2)
            pe.sem_inc(sem("x_out"), KD)
            with pe.Fori(0, LAYERS) as l:
                def w(name, per, k):
                    pe.wait_ge(sem(name), l * per + k)

                def unit_in(u):
                    w(f"w3_in{u % RING2}", 16 * NU // RING2, 16 * (u // RING2 + 1))

                def strip(name, s, lhs=an):
                    u = UNIT_AT[name]
                    if s == 0:
                        unit_in(u)
                    t = ring[:, u % RING2, :].rearrange("p (s k m) -> p s k m", s=4, k=KD)
                    j = job(name, s)
                    evacuated(pe, l, j - 2)
                    for k in range(KD):
                        if (name, s) == ("sb_q", 0):
                            w("pre_n", KD, k + 1)
                        last = pe.matmul(ps[:, j % 2, 0:SEQ], t[:, s, k, :], lhs[:, k, :], start=(k == 0), stop=(k == KD - 1))
                    last.then_inc(sem("job"), 1)

                def on_tokens(name, m, lhs=an):
                    u = UNIT_AT[name]
                    if m == 0:
                        unit_in(u)
                    t = ring[:, u % RING2, :].rearrange("p (s k m) -> p s k m", s=4, k=KD)
                    j = job(name, m)
                    evacuated(pe, l, j - 2)
                    for k in range(KD):
                        last = pe.matmul(ps[:, j % 2, :], lhs[:, k, m * P:(m + 1) * P], t[:, :, k, :], start=(k == 0), stop=(k == KD - 1))
                    last.then_inc(sem("job"), 1)

                def project(name, lhs=an):
                    for i in range(2 if name in ON_TOKENS else 4):
                        (on_tokens if name in ON_TOKENS else strip)(name, i, lhs)

                for k in range(KD):
                    w("sq_pre", KD, k + 1)
                    last = pe.matmul(ps[:, 3, 0:SEQ], ones, an[:, k, :], start=(k == 0), stop=(k == KD - 1))
                last.then_inc(sem("ss_pre"), 1)
                project("sb_q")
                project("sb_k")
                project("sb_v")

                def sb_logits(hd):
                    if hd >= 2:
                        w("sb_zc", NH, hd - 1)
                    for kt in range(2):
                        last = pe.matmul(ps[:, 2 + hd % 2, kt * SEQ:(kt + 1) * SEQ], sb_k[:, hd, kt * P:(kt + 1) * P], sb_q[:, hd, :], start=True, stop=True)
                    last.then_inc(sem("sz_ps"), 1)
                unit_evacuated(pe, l, "sb_k")
                sb_logits(0)
                project("sb_z")
                unit_evacuated(pe, l, "sb_v")
                w("mem_n", KD, KD)
                for hd in range(NH):
                    if hd + 1 < NH:
                        sb_logits(hd + 1)
                    strip("mem_k", hd, mem_t)
                    w("sb_sp", NH, hd + 1)
                    bank = ps[:, 4 + hd % 2, :]
                    pe.matmul(bank[:, 0:SEQ], C("notbefore"), sb_sp[:, 0:SEQ], start=True, stop=False)
                    pe.matmul(bank[:, 0:SEQ], ones, sb_sp[:, SEQ:2 * SEQ], start=False, stop=True)
                    pe.matmul(bank[:, SEQ:2 * SEQ], C("notbefore"), sb_sp[:, SEQ:2 * SEQ], start=True, stop=True).then_inc(sem("sr_ps"), 1)
                    strip("xa_q", hd)
                    w("sb_e", NH, hd + 1)
                    if hd >= 2:
                        w("sb_y", NH, hd - 1)
                    for kt in range(2):
                        last = pe.matmul(ps[:, 6 + hd % 2, 0:SEQ], sb_v[:, kt, hd * P:(hd + 1) * P], sb_w[:, kt * SEQ:(kt + 1) * SEQ], start=(kt == 0), stop=(kt == 1))
                    last.then_inc(sem("so_ps"), 1)
                project("mem_v", mem_t)

                def xa_logits(hd):
                    if hd >= 2:
                        w("xa_e", 2 * NH, 2 * hd - 2)
                    for st in range(2):
                        last = pe.matmul(ps[:, 2 + hd % 2, st * SEQ:(st + 1) * SEQ], xa_q[:, hd, st * P:(st + 1) * P], mem_k[:, hd, :], start=True, stop=True)
                    last.then_inc(sem("xl_ps"), 1)
                unit_evacuated(pe, l, "xa_q")
                unit_evacuated(pe, l, "mem_k")
                w("sb_y", NH, NH)
                xa_logits(0)
                project("xa_z")
                unit_evacuated(pe, l, "mem_v")
                for hd in range(NH):
                    if hd + 1 < NH:
                        xa_logits(hd + 1)
                    strip("ml_q", hd)
                    w("xa_p", NH, hd + 1)
                    if hd >= 2:
                        w("xa_t", NH, hd - 1)
                    for st in range(2):
                        for mt in range(2):
                            last = pe.transpose(ps[:, 4 + hd % 2, mt * SEQ + st * P:mt * SEQ + (st + 1) * P],
                                                xa_l[:, hd % 2, st, mt * P:(mt + 1) * P], ident)
                    last.then_inc(sem("xt_ps"), 1)
                    strip("ml_k", hd)
                    w("xa_t", NH, hd + 1)
                    if hd >= 2:
                        w("xa_y", NH, hd - 1)
                    for mt in range(2):
                        last = pe.matmul(ps[:, 6 + hd % 2, 0:SEQ], mem_v[:, mt, hd * P:(hd + 1) * P], xa_t[:, hd % 2, mt, :], start=(mt == 0), stop=(mt == 1))
                    last.then_inc(sem("xo_ps"), 1)
                on_tokens("ml_v", 0)
                w("in_layer", 32, 32)
                w("xa_y", NH, NH)
                for i in range(2):
                    for k in range(KD):
                        last = pe.matmul(ps[0:4, 2 + i, 0:SEQ], w_if[:, k, 4 * i:4 * i + 4], an[:, k, :], start=(k == 0), stop=(k == KD - 1))
                last.then_inc(sem("mg_ps"), 1)
                on_tokens("ml_v", 1)
                project("ml_o")
                w("mg_e", 1, 1)
                for i, row in enumerate((ml_g[0:4, 0, :], ml_g[0:4, 2, :])):
                    for tt in range(2):
                        last = pe.matmul(ps[:, 3, 8 * i + 4 * tt:8 * i + 4 * tt + 4], row[:, tt * P:(tt + 1) * P], ident[0:4, 0:4], start=True, stop=True)
                last.then_inc(sem("mc_ps"), 1)
                strip("ml_z", 0)
                w("ml_col", 1, 1)
                w("ml_qk", 1, 1)

                def ml_front(hd):
                    sel = C("sel", 4).rearrange("p (h m) -> p h m", h=4)[:, hd, :]
                    if hd >= 1:
                        w("ml_bc", 2 * NH, 2 * hd)
                    pe.matmul(ps[:, 2, :], sel, ml_rows[0:4, 0:512], start=True, stop=True)
                    pe.matmul(ps[:, 3, 0:264], sel, ml_rows[0:4, 512:776], start=True, stop=True)
                    for c in range(NC2):
                        par, tt = c % 2, c // 2
                        last = pe.matmul(ps[CH * par:CH * (par + 1), 3, 264 + tt * CH:264 + (tt + 1) * CH], ml_k[:, hd, c * CH:(c + 1) * CH],
                                         ml_q[:, hd, c * CH:(c + 1) * CH], start=True, stop=True)
                    last.then_inc(sem("mb_ps"), 1)
                    for tt in range(2):
                        last = pe.transpose(ps[:, 7, 256 + tt * P:256 + (tt + 1) * P], ml_k[:, hd, tt * P:(tt + 1) * P], ident)
                    last.then_inc(sem("mk_ps"), 1)
                ml_front(0)
                strip("ml_z", 1)
                strip("ml_z", 2)
                strip("ml_z", 3)
                unit_evacuated(pe, l, "ml_v")
                for hd in range(NH):
                    w("ml_kw", 2 * NH, 2 * hd + 2)
                    for c in (0, 2, 1):
                        par, tt = c % 2, c // 2
                        last = pe.matmul(ps[:, 6 + par, tt * (HD + 1):(tt + 1) * (HD + 1)], ml_kw[CH * par:CH * (par + 1), tt, :],
                                         ml_v[CH * par:CH * (par + 1), tt, hd, :], start=True, stop=True)
                    last.then_inc(sem("mu_ps"), 1)
                    strip("rt_q", hd)
                    w("ml_s", NH, hd + 1)
                    w("ml_st", NH, hd + 1)
                    w("ml_qd", NH, hd + 1)
                    if hd >= 1:
                        w("ml_h", NH, hd)
                    for par in range(2):
                        for tt in range(2):
                            c = 2 * tt + par
                            num = ps[:, 4 + par, tt * CH:(tt + 1) * CH]
                            den = ps[:, 4 + par, P + tt * CH:P + (tt + 1) * CH]
                            s = ml_s[CH * par:CH * (par + 1), tt, :]
                            pe.matmul(num, ml_v[CH * par:CH * (par + 1), tt, hd, 0:HD], s, start=(tt == 0), stop=False, skip_group_check=True)
                            last = pe.matmul(den, ones[CH * par:CH * (par + 1), :], s, start=False, stop=False, skip_group_check=True)
                            if c:
                                qd = ml_qd[:, c * CH:(c + 1) * CH]
                                pe.matmul(num, ml_st[:, c - 1, 0:HD], qd, start=False, stop=False, skip_group_check=True)
                                last = pe.matmul(den, ml_nb[:, c - 1, :], qd, start=False, stop=False, skip_group_check=True)
                    last.then_inc(sem("mo_ps"), 1)
                    if hd + 1 < NH:
                        ml_front(hd + 1)
                    strip("rt_k", hd)

                def head_mean(src, tag):
                    for i in range(2):
                        last = pe.matmul(ps[:, 2 + i, :], mean_of, xr(src[:, 2 * i:2 * i + 2, :]), start=True, stop=True)
                    last.then_inc(sem(f"{tag}_mean"), 1)

                def head_var(tag):
                    w(f"{tag}_sq", 1, 1)
                    for i in range(2):
                        last = pe.matmul(ps[:, 4 + i, :], mean_of, xr(hn_sq[:, 2 * i:2 * i + 2, :]), start=True, stop=True)
                    last.then_inc(sem(f"{tag}_var"), 1)

                w("ml_h", NH, NH)
                head_mean(ml_q, "mlh")
                on_tokens("rt_v", 0)
                head_var("mlh")
                on_tokens("rt_v", 1)

                unit_evacuated(pe, l, "rt_q")
                unit_evacuated(pe, l, "rt_k")
                w("mlh_c", 1, 1)
                w("mlh_r", 1, 1)
                for i, src in enumerate((rt_q, rt_q, rt_k, rt_k)):
                    pe.matmul(ps[:, 2 + i, :], C("rot"), xr(src[:, 2 * (i % 2):2 * (i % 2) + 2, :]), start=True, stop=True).then_inc(sem("rr_ps"), 1)

                def rt_front(hd):
                    for c in range(NC2):
                        par, tt = c % 2, c // 2
                        last = pe.matmul(ps[CH * par:CH * (par + 1), 2, tt * CH:(tt + 1) * CH], rt_k[:, hd, c * CH:(c + 1) * CH],
                                         rt_q[:, hd, c * CH:(c + 1) * CH], start=True, stop=True)
                    last.then_inc(sem("rs_ps"), 1)
                    for tt in range(2):
                        last = pe.transpose(ps[:, 3, tt * P:(tt + 1) * P], rt_k[:, hd, tt * P:(tt + 1) * P], ident)
                    last.then_inc(sem("rk_ps"), 1)
                on_tokens("gm_v", 0)
                w("rt_rot", 4, 4)
                rt_front(0)
                on_tokens("gm_v", 1)
                unit_evacuated(pe, l, "rt_v")
                for hd in range(NH):
                    w("rt_kw", NH, hd + 1)
                    for c in (0, 2, 1):
                        par, tt = c % 2, c // 2
                        last = pe.matmul(ps[:, 6 + par, tt * P:(tt + 1) * P], rt_kw[CH * par:CH * (par + 1), tt, :],
                                         rt_v[CH * par:CH * (par + 1), tt, hd * P:(hd + 1) * P], start=True, stop=True)
                    last.then_inc(sem("ru_ps"), 1)
                    strip("rt_z", hd)
                    w("rt_s", NH, hd + 1)
                    w("rt_st", NH, hd + 1)
                    w("rt_qd", NH, hd + 1)
                    if hd >= 1:
                        w("rt_h", 2 * NH, 2 * hd)
                    for par in range(2):
                        for tt in range(2):
                            c = 2 * tt + par
                            out = ps[:, 4 + par, tt * CH:(tt + 1) * CH]
                            last = pe.matmul(out, rt_v[CH * par:CH * (par + 1), tt, hd * P:(hd + 1) * P], rt_s[CH * par:CH * (par + 1), tt, :],
                                             start=(tt == 0), stop=False, skip_group_check=True)
                            if c:
                                last = pe.matmul(out, rt_st[:, c - 1, :], rt_qd[:, c * CH:(c + 1) * CH], start=False, stop=False, skip_group_check=True)
                    last.then_inc(sem("ro_ps"), 1)
                    if hd + 1 < NH:
                        rt_front(hd + 1)
                    strip("gm_u", hd)
                w("rt_h", 2 * NH, 2 * NH)
                head_mean(rt_q, "rth")
                strip("gm_z", 0)
                strip("gm_z", 1)
                head_var("rth")
                strip("gm_z", 2)
                strip("gm_z", 3)
                w("gm_n", 1, 1)
                for g in range(4):
                    for nb in range(2):
                        last = pe.matmul(ps[:, 6 + g // 2, (g % 2) * SEQ + nb * P:(g % 2) * SEQ + (nb + 1) * P], gm_v[:, nb, g * P:(g + 1) * P],
                                         gm_ws[:, g, :], start=True, stop=True)
                last.then_inc(sem("gm_ps"), 1)

                for p in range(PAIRS):
                    c, n = p // NBR, MERGE_ORDER[p % NBR]
                    u = len(UNIT_AT) + p // 2
                    if p % 2 == 0:
                        unit_in(u)
                    t = ring[:, u % RING2, (p % 2) * 1536:(p % 2 + 1) * 1536].rearrange("p (k m) -> p k m", m=P)
                    j = MERGE_AT + 2 * p
                    evacuated(pe, l, j - 2)
                    for k in range(KD):
                        last = pe.matmul(ps[:, j % 2, 0:SEQ], t[:, k, :], an[:, k, :], start=(k == 0), stop=(k == KD - 1))
                    last.then_inc(sem("job"), 1)
                    if c == 0:
                        w(*{4: ("xa_y", NH, NH), 0: ("sb_y", NH, NH), 1: ("ml_y", 1, 1), 3: ("rt_y", 1, 1), 2: ("gm_y", 4, 4)}[n])
                    evacuated(pe, l, j - 1)
                    for k in range(4):
                        last = pe.matmul(ps[:, (j + 1) % 2, 0:SEQ], t[:, KD + k, :], y_all[:, n, k, :], start=(k == 0), stop=(k == 3))
                    last.then_inc(sem("job"), 1)
                w("merged", PAIRS, PAIRS - NBR)
                for i in range(KD + 1):
                    if i < KD:
                        u = len(UNIT_AT) + PAIRS // 2 + i // 4
                        if i % 4 == 0:
                            unit_in(u)
                        t = ring[:, u % RING2, :].rearrange("p (s k m) -> p s k m", s=4, k=KD)
                        j = OUT_AT + i
                        evacuated(pe, l, j - 2)
                        for k in range(KD):
                            if i == 0 and k == KD - 1:
                                w("merged", PAIRS, PAIRS)
                            last = pe.matmul(ps[:, j % 2, 0:SEQ], t[:, i % 4, k, :], merged[:, k, :], start=(k == 0), stop=(k == KD - 1))
                        last.then_inc(sem("job"), 1)
                    if i >= 1:
                        w("post_sq", KD, i)
                        last = pe.matmul(ps[:, 2, 0:SEQ], ones, post_sq[:, i - 1, :], start=(i == 1), stop=(i == KD))
                last.then_inc(sem("ss_post"), 1)

        def layers_act(act):
            lc = Chain(act, sem("act_layer_chain"))
            per = ACT_LINKS
            with act.Fori(0, LAYERS) as l:
                lc.turn(l, per, 0)
                link = lc.link

                def w(name, per, k):
                    act.wait_ge(sem(name), l * per + k)

                def take(name, i, dst, scale=None):
                    j = job(name, i)
                    job_done(act, l, j)
                    src = ps[:, j % 2, :] if name in ON_TOKENS else ps[:, j % 2, 0:SEQ]
                    if name == "ml_v":
                        src = src.rearrange("p (h n) -> p h n", h=NH)
                    ins = act.mul(dst, src, scale) if scale else act.copy(dst, src)
                    ins.then_inc(sem(f"job_out{j % 2}"), 1)

                def exp_neg(name, i):
                    j = job(name, i)
                    job_done(act, l, j)
                    act.activation(esig[:, j % 2, :], ps[:, j % 2, 0:SEQ], ACT.Exp, scale=-1.0).then_inc(sem("jexp"), 1)

                for k in range(KD):
                    w("x_out", KD, k + 1)
                    act.activation(an[:, k, :], x_tok[:, k, :], ACT.Square).then_inc(sem("sq_pre"), 1)
                for dst, name in ((w_if, "w_if"), (gm_ws, "gm_ws")):
                    act.dma_start(xr(dst), d[name][bass.ds(l, 1)].rearrange("a p n -> (a p) n")).then_inc(sem("in_layer"), 16)
                act.dma_start(xr(gm_rows), d["gm_rows"][bass.ds(l, 1), :].rearrange("a n -> (a n)").partition_broadcast(P)).then_inc(sem("in_rows"), 16)
                w("ss_pre", 1, 1)
                norm_rstd(act, lc, rstd[:, 0:SEQ], ps[:, 3, 0:SEQ], D, eps, sem("pre_r"))
                for i in range(4):
                    take("sb_q", i, sb_q[:, i, :], SCALE)
                for i in range(4):
                    take("sb_k", i, sb_k[:, i, :])
                for i in range(2):
                    take("sb_v", i, sb_v[:, i, :])

                def sb_softplus(hd):
                    w("sz_ps", NH, hd + 1)
                    act.copy(sb_z[:, hd % 2, :], ps[:, 2 + hd % 2, :]).then_inc(sem("sb_zc"), 1)
                    w("sb_zc", NH, hd + 1)
                    if hd >= 1:
                        w("sr_ps", NH, hd)
                    link(act.activation(sb_sp, sb_z[:, hd % 2, :], ACT.Abs))
                    link(act.activation(sb_sp, sb_sp, ACT.Exp, scale=-1.0))
                    act.activation(sb_sp, sb_sp, ACT.Ln, bias=ones[:, 0:1]).then_inc(sem("sb_ln"), 1)
                sb_softplus(0)
                for i in range(4):
                    exp_neg("sb_z", i)
                for hd in range(NH):
                    take("mem_k", hd, mem_k[:, hd, :])
                    w("sb_d", NH, hd + 1)
                    act.activation(sb_w, sb_w, ACT.Exp).then_inc(sem("sb_e"), 1)
                    if hd + 1 < NH:
                        sb_softplus(hd + 1)
                    take("xa_q", hd, xa_q[:, hd, :])
                for i in range(2):
                    take("mem_v", i, mem_v[:, i, :])

                def xa_exp(hd):
                    w("xa_max", NH, hd + 1)
                    for st in range(2):
                        act.activation(xa_l[:, hd % 2, st, :], ps[:, 2 + hd % 2, st * SEQ:(st + 1) * SEQ], ACT.Exp, scale=SCALE,
                                       bias=xa_s[:, 2 * hd, st:st + 1], accum_out=xa_s[:, 2 * hd + 1, st:st + 1]).then_inc(sem("xa_e"), 1)
                xa_exp(0)
                for i in range(4):
                    exp_neg("xa_z", i)
                w("ml_pads", 1, 1)
                for hd in range(NH):
                    take("ml_q", hd, wide[:, hd, 3:3 + SEQ])
                    w("xt_ps", NH, hd + 1)
                    act.copy(xr(xa_t[:, hd % 2]), ps[:, 4 + hd % 2, :]).then_inc(sem("xa_t"), 1)
                    if hd + 1 < NH:
                        xa_exp(hd + 1)
                    take("ml_k", hd, wide[:, 4 + hd, 3:3 + SEQ])
                w("ml_conv", 1, 1)
                act.activation(wide_flat, ml_qk, ACT.Exp, scale=-1.0).then_inc(sem("ml_qke"), 1)
                take("ml_v", 0, ml_v[:, 0, :, 0:HD])
                w("ml_qkm", 1, 1)
                link(act.activation(wide_flat, wide_flat, ACT.Ln, bias=ones[:, 0:1]))
                act.activation(wide_flat, wide_flat, ACT.Exp, scale=-1.0).then_inc(sem("ml_qks"), 1)
                w("mg_x", 1, 1)
                link(act.activation(ml_g[0:4, 2, :], ml_g[0:4, 1, :], ACT.Abs))
                link(act.activation(ml_g[0:4, 2, :], ml_g[0:4, 2, :], ACT.Exp, scale=-1.0))
                act.activation(ml_g[0:4, 2, :], ml_g[0:4, 2, :], ACT.Ln, bias=ones[0:4, 0:1]).then_inc(sem("mg_l"), 1)
                take("ml_v", 1, ml_v[:, 1, :, 0:HD])
                for i in range(4):
                    j = job("ml_o", i)
                    job_done(act, l, j)
                    act.activation(ml_o[:, i, :], ps[:, j % 2, 0:SEQ], ACT.Exp, scale=-1.0).then_inc(sem(f"job_out{j % 2}"), 1)
                w("mg_r", 1, 1)
                link(act.activation(ml_rows[0:4, SEQ:776], ml_rows[0:4, SEQ:776], ACT.Exp))
                act.activation(ml_g[0:4, 2, :], ml_g[0:4, 2, :], ACT.Exp).then_inc(sem("mg_e"), 1)
                w("mc_ps", 1, 1)
                act.copy(ml_col, ps[:, 3, 0:16]).then_inc(sem("ml_col"), 1)

                def ml_decays(hd):
                    w("mb_ps", NH, hd + 1)
                    if hd >= 1:
                        w("ml_h", NH, hd)
                    act.copy(ml_bc[:, 0:512], ps[:, 2, :]).then_inc(sem("ml_bc"), 1)
                    act.copy(ml_bc[:, 512:776], ps[:, 3, 0:264]).then_inc(sem("ml_bc"), 1)
                    w("ml_dx", 2 * NH, 2 * hd + 2)
                    for c in range(NC2):
                        par, tt = c % 2, c // 2
                        v = ml_d[CH * par:CH * (par + 1), tt, :]
                        act.activation(v, v, ACT.Exp, bias=ml_col[CH * par:CH * (par + 1), tt * 4 + hd:tt * 4 + hd + 1]).then_inc(sem("ml_de"), 1)
                ml_decays(0)
                for i in range(4):
                    exp_neg("ml_z", i)
                for hd in range(NH):
                    take("rt_q", hd, rt_q[:, hd, :])
                    if hd + 1 < NH:
                        ml_decays(hd + 1)
                    take("rt_k", hd, rt_k[:, hd, :])

                def head_squares(src, tag):
                    w(f"{tag}_c", 1, 1)
                    act.activation(xr(hn_sq), xr(src), ACT.Square).then_inc(sem(f"{tag}_sq"), 1)

                def head_rstd(tag):
                    w(f"{tag}_var", 1, 1)
                    link(act.activation(xr(hn_r), ps[:, 4:6, :].rearrange("p a b -> p (a b)"), ACT.Ln, bias=eps))
                    act.activation(xr(hn_r), xr(hn_r), ACT.Exp, scale=-0.5).then_inc(sem(f"{tag}_r"), 1)

                head_squares(ml_q, "mlh")
                take("rt_v", 0, rt_v[:, 0, :])
                head_rstd("mlh")
                take("rt_v", 1, rt_v[:, 1, :])
                for i in range(2):
                    take("gm_v", i, gm_v[:, i, :])
                for hd in range(NH):
                    exp_neg("rt_z", hd)
                    take("gm_u", hd, gm_u[:, hd, :])
                unit_evacuated(act, l, "gm_v")
                act.activation(xr(gm_v), xr(gm_v), ACT.Gelu_apprx_tanh).then_inc(sem("gm_gelu"), 1)
                unit_evacuated(act, l, "gm_u")
                act.activation(xr(gm_u), xr(gm_u), ACT.Gelu_apprx_tanh).then_inc(sem("gm_gelu"), 1)
                head_squares(rt_q, "rth")
                exp_neg("gm_z", 0)
                exp_neg("gm_z", 1)
                w("gm_var", 1, 1)
                link(act.activation(gm_mv[:, :, 1], gm_mv[:, :, 1], ACT.Ln, bias=eps))
                act.activation(gm_mv[:, :, 1], gm_mv[:, :, 1], ACT.Exp, scale=-0.5).then_inc(sem("gm_r"), 1)
                head_rstd("rth")
                exp_neg("gm_z", 2)
                exp_neg("gm_z", 3)
                for p in range(PAIRS):
                    j = MERGE_AT + 2 * p
                    job_done(act, l, j)
                    if p >= 2:
                        w("merged", PAIRS, p - 1)
                    else:
                        evacuated(act, l, job("gm_z", 2 + p))
                    act.activation(esig[:, p % 2, :], ps[:, j % 2, 0:SEQ], ACT.Exp, scale=-1.0).then_inc(sem(f"job_out{j % 2}"), 1)
                for i in range(KD):
                    j = OUT_AT + i
                    job_done(act, l, j)
                    act.activation(post_sq[:, i, :], ps[:, j % 2, 0:SEQ], ACT.Square).then_inc(sem("post_sq"), 1)
                    act.copy(post[:, i, :], ps[:, j % 2, 0:SEQ]).then_inc(sem(f"job_out{j % 2}"), 1)
                w("ss_post", 1, 1)
                norm_rstd(act, lc, rstd[:, 0:SEQ], ps[:, 2, 0:SEQ], D, eps, sem("post_r"))
                lc.end_turn(per)

        def layers_dve(dve):
            vc = Chain(dve, sem("dve_layer_chain"))
            link, tick = vc.link, vc.tick
            link(dve.tensor_scalar(mean_of, ones, 1.0 / P, None, ALU.mult))
            start, per = vc.n, DVE_LINKS
            with dve.Fori(0, LAYERS) as l:
                vc.turn(l, per, start)

                def w(name, per, k):
                    dve.wait_ge(sem(name), l * per + k)

                def gate(name, i, dst):
                    j = job(name, i)
                    at, step = JEXP_AT[name]
                    w("jexp", JEXPS, at + i * step + 1)
                    e = esig[:, j % 2, :]
                    link(dve.tensor_scalar(e, e, 1.0, None, ALU.add))
                    if name == "ml_z":
                        link(dve.scalar_tensor_tensor(e, ml_o[:, i, :], 1.0, e, ALU.add, ALU.mult))
                    link(dve.reciprocal(e, e))
                    dve.tensor_tensor(dst[:, i, :], ps[:, j % 2, 0:SEQ], e, ALU.mult).then_inc(sem(f"job_out{j % 2}"), 1)

                w("pre_r", 1, 1)
                for k in range(KD):
                    dve.scalar_tensor_tensor(an[:, k, :], x_tok[:, k, :], P2(l, "norm_pre", k), rstd[:, 0:SEQ], ALU.mult, ALU.mult).then_inc(sem("pre_n"), 1)
                link(dve.tensor_scalar(keyneg, C("keymask"), BIG, -BIG, ALU.mult, ALU.add))
                for k in range(KD):
                    dve.scalar_tensor_tensor(mem_t[:, k, :], mem_raw[:, k, :], P2(l, "mem_norm", k), hn_mem, ALU.mult, ALU.mult).then_inc(sem("mem_n"), 1)

                def sb_softplus(hd):
                    w("sb_ln", NH, hd + 1)
                    link(dve.scalar_tensor_tensor(sb_sp, sb_z[:, hd % 2, :], 0.0, sb_sp, ALU.max, ALU.add))
                    dve.tensor_tensor(sb_sp, sb_sp, C("keymask"), ALU.mult).then_inc(sem("sb_sp"), 1)
                sb_softplus(0)
                for i in range(4):
                    gate("sb_z", i, y_all[:, 0])
                for hd in range(NH):
                    w("sr_ps", NH, hd + 1)
                    if hd >= 1:
                        w("so_ps", NH, hd)
                    link(dve.tensor_tensor(sb_w, sb_z[:, hd % 2, :], ps[:, 4 + hd % 2, :], ALU.subtract))
                    dve.tensor_tensor(sb_w, sb_w, keyneg, ALU.add).then_inc(sem("sb_d"), 1)
                    if hd + 1 < NH:
                        sb_softplus(hd + 1)
                    w("so_ps", NH, hd + 1)
                    y = y_all[:, 0, hd, :]
                    dve.tensor_tensor(y, y, ps[:, 6 + hd % 2, 0:SEQ], ALU.mult).then_inc(sem("sb_y"), 1)
                w("in_layer", 32, 32)
                tick(dve.memset(gm_ws[CH:P, :, 0:CH], 0.0))
                w("sb_y", NH, NH)
                tick(dve.memset(ml_v[:, :, :, HD:HD + 1], 1.0))
                dve.memset(wide[:, :, 0:3], 0.0).then_inc(sem("ml_pads"), 1)

                def xa_max(hd):
                    w("xl_ps", NH, hd + 1)
                    mx = xa_s[:, 2 * hd, 0:2]
                    link(dve.tensor_reduce(mx, ps[:, 2 + hd % 2, :].rearrange("p (s m) -> p s m", s=2), AX, ALU.max))
                    dve.tensor_scalar(mx, mx, -SCALE, None, ALU.mult).then_inc(sem("xa_max"), 1)

                def xa_share(hd):
                    w("xa_e", 2 * NH, 2 * hd + 2)
                    sm = xa_s[:, 2 * hd + 1, 0:2]
                    link(dve.reciprocal(sm, sm))
                    p_ = xa_l[:, hd % 2]
                    dve.tensor_tensor(p_, p_, sm.unsqueeze(2).to_broadcast([P, 2, SEQ]), ALU.mult).then_inc(sem("xa_p"), 1)

                def convolve(name, hd):
                    evacuated(dve, l, job(name, hd))
                    dst, tap, i = (ml_q, "conv_q", hd) if name == "ml_q" else (ml_k, "conv_k", 4 + hd)
                    dst = dst[:, hd, :]
                    link(dve.tensor_scalar(dst, wide[:, i, 0:SEQ], P2(l, tap, hd), None, ALU.mult))
                    for t in range(1, 4):
                        ins = dve.scalar_tensor_tensor(dst, wide[:, i, t:t + SEQ], P2(l, tap, 4 * t + hd), dst, ALU.mult, ALU.add)
                        if i == 7 and t == 3:
                            ins.then_inc(sem("ml_conv"), 1)
                        else:
                            link(ins)
                xa_max(0)
                xa_share(0)
                for i in range(4):
                    gate("xa_z", i, y_all[:, 4])
                unit_evacuated(dve, l, "mem_v")
                for hd in range(NH):
                    if hd + 1 < NH:
                        xa_max(hd + 1)
                    convolve("ml_q", hd)
                    if hd + 1 < NH:
                        xa_share(hd + 1)
                    if hd >= 1:
                        convolve("ml_k", hd - 1)
                    w("xo_ps", NH, hd + 1)
                    y = y_all[:, 4, hd, :]
                    dve.tensor_tensor(y, y, ps[:, 6 + hd % 2, 0:SEQ], ALU.mult).then_inc(sem("xa_y"), 1)
                convolve("ml_k", NH - 1)
                w("ml_qke", 1, 1)
                dve.tensor_scalar(wide_flat, wide_flat, 1e18, None, ALU.min).then_inc(sem("ml_qkm"), 1)
                w("ml_qks", 1, 1)
                tick(dve.tensor_tensor(xr(ml_q), xr(ml_q), wide_flat[:, 0:4 * SEQ], ALU.mult))
                link(dve.scalar_tensor_tensor(xr(ml_k), xr(ml_k), SCALE, wide_flat[:, 4 * SEQ:8 * SEQ], ALU.mult, ALU.mult))
                dve.nop().then_inc(sem("ml_qk"), 1)
                g0, g1, g2, g3, g4 = (ml_g[0:4, i, :] for i in range(5))
                w("xa_y", NH, NH)
                w("mg_ps", 1, 1)
                link(dve.tensor_scalar(g0, ps[0:4, 2, 0:SEQ], P2(l, "b_i", rows=4), None, ALU.add))
                dve.tensor_scalar(g1, ps[0:4, 3, 0:SEQ], P2(l, "b_f", rows=4), None, ALU.add).then_inc(sem("mg_x"), 1)
                w("mg_l", 1, 1)
                c_bl, c_al, c_m, c_x = ml_c[0:4, 0, 0:4], ml_c[0:4, 1, 0:4], ml_c[0:4, 2, 0:5], ml_c[0:4, 3, 0:4]

                def by_chunk(v):
                    return v.rearrange("p (c t) -> p c t", t=CH)

                def over(v):
                    return v.unsqueeze(2).to_broadcast([4, NC2, CH])

                link(dve.scalar_tensor_tensor(g2, g1, 0.0, g2, ALU.min, ALU.subtract))
                link(dve.tensor_tensor_scan(g3, C("run", 4)[:, 0:SEQ], g2, 0.0, ALU.mult, ALU.add))
                link(dve.tensor_tensor(g0, g0, g3, ALU.subtract))
                link(dve.tensor_tensor_scan(g4, C("restart", 4), g0, -BIG, ALU.add, ALU.max))
                link(dve.tensor_tensor(g4, g4, g3, ALU.add))
                tick(dve.tensor_copy(c_bl, g3[:, CH - 1:SEQ:CH]))
                tick(dve.tensor_copy(c_al, g4[:, CH - 1:SEQ:CH]))
                link(dve.memset(c_m[:, 0:1], 0.0))
                link(dve.tensor_tensor_scan(c_m[:, 1:5], c_bl, c_al, 0.0, ALU.add, ALU.max))
                link(dve.tensor_tensor(by_chunk(g1), by_chunk(g3), over(c_m[:, 0:4]), ALU.add))
                link(dve.tensor_tensor(g4, g1, g4, ALU.max))
                rows = ml_rows[0:4, :]
                tick(dve.tensor_tensor(rows[:, 0:SEQ], g3, g4, ALU.subtract))
                tick(dve.tensor_tensor(rows[:, SEQ:2 * SEQ], g1, g4, ALU.subtract))
                tick(dve.tensor_scalar(rows[:, 2 * SEQ:3 * SEQ], g4, -1.0, None, ALU.mult))
                link(dve.tensor_tensor(c_x, c_bl, c_m[:, 0:4], ALU.add))
                tick(dve.tensor_tensor(rows[:, 768:772], c_x, c_m[:, 1:5], ALU.subtract))
                link(dve.tensor_tensor(rows[:, 772:776], c_al, c_m[:, 1:5], ALU.subtract))
                link(dve.tensor_tensor(c_x, c_bl, c_al, ALU.subtract))
                dve.tensor_tensor(by_chunk(g2), by_chunk(g0), over(c_x), ALU.add).then_inc(sem("mg_r"), 1)
                w("ml_col", 1, 1)

                def ml_front(hd):
                    w("mk_ps", NH, hd + 1)
                    for tt in range(2):
                        dve.tensor_scalar(ml_kw[:, tt, :], ps[:, 7, 256 + tt * P:256 + (tt + 1) * P], ml_col[:, 8 + 4 * tt + hd:9 + 4 * tt + hd], None,
                                          ALU.mult).then_inc(sem("ml_kw"), 1)
                    w("ml_bc", 2 * NH, 2 * hd + 2)
                    for par in range(2):
                        q = slice(CH * par, CH * (par + 1))
                        dve.tensor_tensor(ml_d[q], halves(ml_bc[q, 0:SEQ], par), C("causal_neg")[q].unsqueeze(1).to_broadcast([CH, 2, CH]),
                                          ALU.add).then_inc(sem("ml_dx"), 1)
                    dve.tensor_tensor(ml_qd, ml_q[:, hd, :], ml_bc[:, SEQ:2 * SEQ], ALU.mult).then_inc(sem("ml_qd"), 1)
                    w("ml_de", 4 * NH, 4 * hd + 4)
                    dve.tensor_tensor(ml_s, ml_d, by_tile(ps[:, 3, 264:264 + P]), ALU.mult).then_inc(sem("ml_s"), 1)
                ml_front(0)
                for i in range(3):
                    gate("ml_z", i, y_all[:, 1])
                for hd in range(NH):
                    w("mu_ps", NH, hd + 1)
                    for c in range(3):
                        ins = dve.tensor_scalar(ml_st[:, c, :], ps[:, 6 + c % 2, (c // 2) * (HD + 1):(c // 2 + 1) * (HD + 1)],
                                                ml_bc[:, 772 + c:773 + c], None, ALU.mult)
                        (link if c == 2 else tick)(ins)
                    for c in (1, 2):
                        link(dve.scalar_tensor_tensor(ml_st[:, c, :], ml_st[:, c - 1, :], ml_bc[:, 768 + c:769 + c], ml_st[:, c, :], ALU.mult, ALU.add))
                    dve.tensor_copy(ml_nb, ml_st[:, :, HD:HD + 1].to_broadcast([P, 3, P])).then_inc(sem("ml_st"), 1)
                    if hd == 0:
                        gate("ml_z", 3, y_all[:, 1])
                    w("mo_ps", NH, hd + 1)
                    for par in range(2):
                        den = by_tile(ps[:, 4 + par, P:2 * P])
                        tick(dve.scalar_tensor_tensor(halves(ml_qd, par), den, -1.0, halves(ml_bc[:, 2 * SEQ:3 * SEQ], par), ALU.mult, ALU.max))
                    dve.wait_ge(vc.sem, vc.base + vc.n)
                    for par in range(2):
                        tick(dve.tensor_tensor(halves(ml_qd, par), halves(ml_qd, par), by_tile(ps[:, 4 + par, P:2 * P]), ALU.max))
                    dve.wait_ge(vc.sem, vc.base + vc.n)
                    link(dve.reciprocal(ml_qd, ml_qd))
                    link(dve.tensor_tensor(halves(ml_q[:, hd, :], 0), by_tile(ps[:, 4, 0:P]), halves(ml_qd, 0), ALU.mult))
                    dve.tensor_tensor(halves(ml_q[:, hd, :], 1), by_tile(ps[:, 5, 0:P]), halves(ml_qd, 1), ALU.mult).then_inc(sem("ml_h"), 1)
                    if hd + 1 < NH:
                        ml_front(hd + 1)

                def head_centre(src, tag):
                    w(f"{tag}_mean", 1, 1)
                    dve.tensor_tensor(xr(src), xr(src), ps[:, 2:4, :].rearrange("p a b -> p (a b)"), ALU.subtract).then_inc(sem(f"{tag}_c"), 1)

                def head_scale(src, tag, y, done):
                    w(f"{tag}_c", 1, 1)
                    w(f"{tag}_r", 1, 1)
                    link(dve.tensor_tensor(xr(src), xr(src), xr(hn_r), ALU.mult))
                    dve.tensor_tensor(xr(y), xr(y), xr(src), ALU.mult).then_inc(sem(done), 1)

                w("ml_h", NH, NH)
                head_centre(ml_q, "mlh")
                head_scale(ml_q, "mlh", y_all[:, 1], "ml_y")
                for i, src in enumerate((rt_q, rt_q, rt_k, rt_k)):
                    s = src[:, 2 * (i % 2):2 * (i % 2) + 2, :]
                    w("rr_ps", 4, i + 1)
                    t = rt_t[:, i % 2, :].rearrange("p (h t) -> p h t", h=2)
                    tick(dve.tensor_tensor(t, ps[:, 2 + i, :].rearrange("p (h t) -> p h t", h=2), rope[:, 0:1, :].to_broadcast([P, 2, SEQ]), ALU.mult))
                    link(dve.tensor_tensor(s, s, rope[:, 1:2, :].to_broadcast([P, 2, SEQ]), ALU.mult))
                    dve.tensor_tensor(s, s, t, ALU.add).then_inc(sem("rt_rot"), 1)
                    w("rt_rot", 4, i + 1)

                def rt_front(hd):
                    w("rk_ps", NH, hd + 1)
                    dve.tensor_scalar(xr(rt_kw), ps[:, 3, 0:2 * P], C("rt_wend")[:, hd:hd + 1], None, ALU.mult).then_inc(sem("rt_kw"), 1)
                    w("rs_ps", NH, hd + 1)
                    decay_h = C("rt_decay").rearrange("p (h t) -> p h t", h=NH)[:, hd:hd + 1, :].to_broadcast([P, 2, CH])
                    dve.tensor_tensor(rt_s, by_tile(ps[:, 2, 0:P]), decay_h, ALU.mult).then_inc(sem("rt_s"), 1)
                    wq = C("rt_wq").rearrange("p (h t) -> p h t", h=NH)[:, hd:hd + 1, :].to_broadcast([P, NC2, CH])
                    dve.tensor_tensor(rt_qd.rearrange("p (c t) -> p c t", t=CH), rt_q[:, hd, :].rearrange("p (c t) -> p c t", t=CH), wq, ALU.mult).then_inc(sem("rt_qd"), 1)
                rt_front(0)
                for hd in range(NH):
                    decay = (1.0 - 2.0 ** (-5.0 - hd)) ** CH
                    w("ru_ps", NH, hd + 1)
                    link(dve.tensor_copy(rt_st[:, 0, :], ps[:, 6, 0:P]))
                    link(dve.scalar_tensor_tensor(rt_st[:, 1, :], rt_st[:, 0, :], decay, ps[:, 7, 0:P], ALU.mult, ALU.add))
                    dve.scalar_tensor_tensor(rt_st[:, 2, :], rt_st[:, 1, :], decay, ps[:, 6, P:2 * P], ALU.mult, ALU.add).then_inc(sem("rt_st"), 1)
                    gate("rt_z", hd, y_all[:, 3])
                    w("ro_ps", NH, hd + 1)
                    if hd + 1 < NH:
                        rt_front(hd + 1)
                    for par in range(2):
                        dve.tensor_copy(halves(rt_q[:, hd, :], par), by_tile(ps[:, 4 + par, 0:P])).then_inc(sem("rt_h"), 1)
                w("rt_h", 2 * NH, 2 * NH)
                head_centre(rt_q, "rth")
                w("gm_gelu", 2, 1)
                w("in_rows", 16, 16)
                for m in range(2):
                    link(dve.bn_stats(gm_st[:, m, 0:6], gm_v[:, m, :]))
                tick(dve.memset(gm_st[:, :, 6:8], 0.0))
                tick(dve.bn_aggr(gm_mv[:, 0, :], gm_st[:, 0, 0:6]))
                dve.bn_aggr(gm_mv[:, 1, :], gm_st[:, 1, 0:6]).then_inc(sem("gm_var"), 1)
                gate("gm_z", 0, y_all[:, 2])
                gate("gm_z", 1, y_all[:, 2])
                w("gm_r", 1, 1)
                for m in range(2):
                    link(dve.tensor_scalar(gm_v[:, m, :], gm_v[:, m, :], gm_mv[:, m, 0:1], gm_mv[:, m, 1:2], ALU.subtract, ALU.mult))
                link(dve.tensor_tensor(gm_v, gm_v, gm_rows[:, 0, :].unsqueeze(1).to_broadcast([P, 2, HALF]), ALU.mult))
                dve.tensor_tensor(gm_v, gm_v, gm_rows[:, 1, :].unsqueeze(1).to_broadcast([P, 2, HALF]), ALU.add).then_inc(sem("gm_n"), 1)
                head_scale(rt_q, "rth", y_all[:, 3], "rt_y")
                gate("gm_z", 2, y_all[:, 2])
                gate("gm_z", 3, y_all[:, 2])
                evacuated(dve, l, job("gm_z", 2))
                evacuated(dve, l, job("gm_z", 3))
                w("gm_gelu", 2, 2)
                w("gm_ps", 1, 1)
                for g in range(4):
                    link(dve.tensor_tensor(gm_x, ps[:, 6 + g // 2, (g % 2) * SEQ:(g % 2 + 1) * SEQ].rearrange("p (n t) -> p n t", n=2),
                                           gm_rows[:, 2, g * P:(g + 1) * P].unsqueeze(1).to_broadcast([P, 2, P]), ALU.add))
                    link(dve.tensor_tensor(xr(gm_x), xr(gm_x), gm_u[:, g, :], ALU.mult))
                    dve.tensor_tensor(y_all[:, 2, g, :], y_all[:, 2, g, :], xr(gm_x), ALU.mult).then_inc(sem("gm_y"), 1)
                    w("gm_y", 4, g + 1)
                for p in range(PAIRS):
                    c, n = p // NBR, p % NBR
                    j = MERGE_AT + 2 * p
                    evacuated(dve, l, j)
                    e = esig[:, p % 2, :]
                    link(dve.tensor_scalar(e, e, 1.0, None, ALU.add))
                    link(dve.reciprocal(e, e))
                    job_done(dve, l, j + 1)
                    out = e if n else merged[:, c, :]
                    dve.tensor_tensor(out, ps[:, (j + 1) % 2, 0:SEQ], e, ALU.mult).then_inc(sem(f"job_out{(j + 1) % 2}"), 1)
                    evacuated(dve, l, j + 1)
                    if n:
                        dve.tensor_tensor(merged[:, c, :], merged[:, c, :], e, ALU.add).then_inc(sem("merged"), 1)
                    else:
                        dve.nop().then_inc(sem("merged"), 1)
                    w("merged", PAIRS, p + 1)
                w("post_r", 1, 1)
                for k in range(0, KD, 2):
                    tick(dve.scalar_tensor_tensor(post[:, k, :], post[:, k, :], P2(l, "norm_post", k), rstd[:, 0:SEQ], ALU.mult, ALU.mult))
                    link(dve.scalar_tensor_tensor(post[:, k + 1, :], post[:, k + 1, :], P2(l, "norm_post", k + 1), rstd[:, 0:SEQ], ALU.mult, ALU.mult))
                    for i in (k, k + 1):
                        dve.tensor_tensor(x_tok[:, i, :], x_tok[:, i, :], post[:, i, :], ALU.add).then_inc(sem("x_out"), 1)
                w("x_out", KD, 2 * KD)
                vc.end_turn(per)

        spectra = m1.take(3, 4, HALF)
        assert m1.at <= SHARED_W, m1.at
        m4 = Layout(filt.rearrange("p a b c -> p (a b c)"))
        zt = m4.take(3, HALF)
        yf = m4.take(3, 2, HALF)
        prod = m4.take(2, HALF)
        assert m4.at <= 3 * 4 * HALF
        m5 = Layout(ring[:, RING1 - 2:RING1, :].rearrange("p a b -> p (a b)"))
        f_k, f_lf, f_cum, f_rel, f_q, f_kk, f_qe, f_kd = (m5.take(2, TP) for _ in range(8))
        kd_t = m5.take(NCH - 1, P)
        vt = m5.take(NCH, HALF)
        assert m5.at <= 2 * WSLOT
        m6 = Layout(scratch, m4.at)
        sc_m = m6.take(2, TP)
        states = m6.take(2, (NCH - 1) * P)
        decay = m6.take(2, NCH)
        head_sq, hyena_sq = a[:, 0:4, :], a[:, 4:8, :]
        assert m6.at <= 2 * WSLOT

        e1 = Layout(arena, free_at)
        xn = e1.take(2, D)
        router = e1.take(KD, NG + NE)
        logits = e1.take(2, NG + NE)
        pick = e1.take(2, NE)
        slot_of = e1.take(2, NE)
        chosen = e1.take(2, NE)
        small = e1.take(24, 16)
        onehot = e1.take(2, P)
        weighted = e1.take(2, P)
        xg = e1.take(KD, P)
        back = e1.take(SEQ)
        gate_e = e1.take(FE)
        mid = e1.take(FE)
        mid_t = e1.take(FE // P, P)
        y_slot = e1.take(D)
        assert e1.at <= SHARED_W

        x_tok = h[:, :, META:T]
        an = a[:, :, 0:SEQ]

        def xr(v):
            return v.rearrange("p a b -> p (a b)")

        block_one = ExitStack()
        block = block_one.enter_context(nc.Block())

        def job_evacuated(eng, j):
            eng.wait_ge(sem(f"strip_out{j % 2}"), j // 2 + 1)

        def strip_at(j):
            return ps[:, j % 2, 0:T]

        @block.sync
        def _(sp):
            sp.dma_start(const, d["const"]).then_inc(sem("in_const"), 16)
            sp.dma_start(param1, d["param1"]).then_inc(sem("in_param1"), 16)
            for l in range(LAYERS):
                sp.dma_start(param2[:, l * w_param2:(l + 1) * w_param2], d["param2"][l]).then_inc(sem("in_param2"), 16)
            sp.dma_start(pos_i[:, :], d["positions"].partition_broadcast(P)).then_inc(sem("in_pos"), 16)
            sp.dma_start(feat[0:33, 0:T], d["features"][0:33, 0:T]).then_inc(sem("in_feat"), 16)
            sp.dma_start(fw1[0:33, :], d["filt_w1"]).then_inc(sem("in_feat"), 16)
            sp.dma_start(fw2[0:64, :], d["filt_w2"]).then_inc(sem("in_feat"), 16)
            sp.dma_start(xr(h), d["h"]).then_inc(sem("in_h"), 16)
            sp.dma_start(fw3[0:64, :, :], d["filt_w3"].rearrange("k (a b) -> k a b", b=HALF)).then_inc(sem("in_w3"), 16)
            sp.dma_start(xr(window), d["features"][:, T:T + 3 * HALF]).then_inc(sem("in_w3"), 16)
            sp.dma_start(four.rearrange("p a b c -> p (a b c)"), d["fourier"]).then_inc(sem("in_four"), 16)
            for u in range(10):
                if u >= RING1:
                    sp.wait_ge(sem("strip"), 4 * (u - RING1 + 1))
                sp.dma_start(ring[:, u % RING1, :], d["w_first"][u]).then_inc(sem(f"w1_in{u % RING1}"), 16)

            def expert_unit(v, g, free):
                s = (v + 2) % RING
                sp.wait_ge(sem("unit_free"), free + v + 1)
                for k in range(2):
                    if v < 8:
                        src = d["w_gate" if v < 4 else "w_up"][bass.ds(g * GRP, GRP), ((v % 4) * 2 + k) * P:((v % 4) * 2 + k + 1) * P, :]
                        dst = ring[:, s, k * 2048:(k + 1) * 2048].rearrange("p (e n) -> p e n", n=FE)
                    else:
                        src = d["w_down"][bass.ds(g * GRP + 2 * k, 2), (v - 8) * P:(v - 7) * P, :]
                        dst = ring[:, s, k * 2048:(k + 1) * 2048].rearrange("p (e n) -> p e n", n=D)
                    sp.dma_start(dst, src.rearrange("e p n -> p e n")).then_inc(sem(f"w2_in{s}"), 16)

            for v in range(12):
                expert_unit(v, 0, 0)
            sp.wait_ge(sem("rounds"), 1)
            n_rounds = sp.value_load(rounds[0:1, 0:1], min_val=1, max_val=SEQ // CAP)
            with sp.Fori(1, n_rounds * NGRP) as it:
                g = sp.snap(it % NGRP)
                for v in range(12):
                    expert_unit(v, g, it * 12)
            sp.wait_ge(sem("in_param2"), 16 * LAYERS)

        @block.tensor
        def _(pe):
            def strip(j, unit, s, rhs, n):
                if j % 4 == 0:
                    pe.wait_ge(sem(f"w1_in{unit % RING1}"), 16 * (unit // RING1 + 1))
                if j >= 2:
                    job_evacuated(pe, j - 2)
                w = ring[:, unit % RING1, :].rearrange("p (s k m) -> p s k m", s=4, k=KD)
                for k in range(KD):
                    last = pe.matmul(ps[:, j % 2, 0:n], w[:, s, k, :], rhs(k), start=(k == 0), stop=(k == KD - 1))
                last.then_inc(sem("strip"), 1)

            pe.wait_ge(sem("in_feat"), 48)
            pe.matmul(ps[0:64, 2, 0:T], fw1[0:33, :], zT[0:33, :], start=True, stop=True).then_inc(sem("hid"), 1)
            pe.wait_ge(sem("sq_mix"), 1)
            pe.wait_ge(sem("in_const"), 16)
            norm_sum(pe, ones, a, KD, ps[:, 3, 0:T], sem("ss_mix"))
            pe.wait_ge(sem("hid_act"), 1)
            pe.matmul(ps[0:64, 2, 0:T], fw2[0:64, :], hid[0:64, :], start=True, stop=True).then_inc(sem("hid"), 1)
            pe.wait_ge(sem("hid_act"), 2)
            pe.wait_ge(sem("in_w3"), 32)
            n = 0
            for tt in range(3):
                for c in range(4):
                    if n >= 4:
                        pe.wait_ge(sem("filt"), n - 3)
                    pe.matmul(ps[0:TW[tt], 4 + n % 4, :], hid[0:64, tt * P:tt * P + TW[tt]], fw3[0:64, c, :],
                              start=True, stop=True).then_inc(sem("filt_ps"), 1)
                    n += 1
            pe.wait_ge(sem("normed_mix"), KD)
            for j in range(4):
                strip(j, j // 4, j % 4, lambda k: a[:, k, :], T)
            pe.wait_ge(sem("in_four"), 16)
            pe.wait_ge(sem("filt_sd"), 4)
            n = 0
            for o in range(2):
                for part, basis in ((0, cosm), (1, sinm)):
                    for ft in range(3):
                        if n >= 4:
                            pe.wait_ge(sem("spectrum"), n - 3)
                        else:
                            pe.wait_ge(sem("filt"), 12)
                        for tt in range(3):
                            last = pe.matmul(ps[0:TW[ft], 4 + n % 4, :], basis[0:TW[tt], tt, ft * P:ft * P + TW[ft]],
                                             filt[0:TW[tt], tt, 2 * part + o, :], start=(tt == 0), stop=(tt == 2))
                        last.then_inc(sem("spectrum_ps"), 1)
                        n += 1
            for j in range(4, HY + HG):
                strip(j, j // 4, j % 4, lambda k: a[:, k, :], T)

            def conv_stage(n):
                o, k = n // 8, n % 8
                if k == 0:
                    pe.wait_ge(sem("z"), 4 * (o + 1))
                    if o == 0:
                        pe.wait_ge(sem("spectrum"), 12)
                    for tt in range(3):
                        if tt == 2:
                            pe.wait_ge(sem("zt"), 3 * o + 1)
                        for c in range(4):
                            last = pe.transpose(ps[0:TW[tt], 2 + tt % 2, c * P:(c + 1) * P], conv[:, c, tt * P:tt * P + TW[tt]], ident)
                        last.then_inc(sem("zt_ps"), 1)
                elif k < 4:
                    ft = k - 1
                    pe.wait_ge(sem("zt"), 3 * (o + 1))
                    if 3 * o + ft >= 1:
                        pe.wait_ge(sem("yf"), 3 * o + ft)
                    for part, basis in ((0, cosm), (1, sinm)):
                        for tt in range(3):
                            last = pe.matmul(ps[0:TW[ft], 4 + part, :], basis[0:TW[tt], tt, ft * P:ft * P + TW[ft]],
                                             zt[0:TW[tt], tt, :], start=(tt == 0), stop=(tt == 2))
                    last.then_inc(sem("uf_ps"), 1)
                else:
                    c = k - 4
                    pe.wait_ge(sem("yf"), 3 * (o + 1))
                    if c >= 2:
                        pe.wait_ge(sem("z"), 4 * (o + 1) + c - 1)
                    for ft in range(3):
                        for part, basis in ((0, icos), (1, isin)):
                            last = pe.matmul(ps[:, 2 + c % 2, 0:T], yf[0:TW[ft], ft, part, c * P:(c + 1) * P],
                                             basis[0:TW[ft], ft, :], start=(ft == 0 and part == 0), stop=(ft == 2 and part == 1))
                    last.then_inc(sem("conv_ps"), 1)

            for c in range(NCH):
                job_evacuated(pe, 26)
                job_evacuated(pe, 27)
                if c >= 2:
                    pe.wait_ge(sem("vt"), c - 1)
                elif c == 0:
                    pe.wait_ge(sem("spectrum"), 12)
                for hd in range(NH):
                    last = pe.transpose(ps[0:CH, 6 + c % 2, hd * P:(hd + 1) * P], hg[:, 12 + hd, c * CH:(c + 1) * CH], ident)
                last.then_inc(sem("vt_ps"), 1)
            for n in range(3):
                conv_stage(n)

            def head_sum(hd):
                pe.wait_ge(sem("sq_head"), hd + 1)
                pe.matmul(ps[:, HEAD_BANKS[hd], 0:T], ones, head_sq[:, hd, :], start=True, stop=True).then_inc(sem("ss_head"), 1)

            job_evacuated(pe, HY + HG - 2)
            job_evacuated(pe, HY + HG - 1)
            for it in range(2 * NH):
                hd, bwd = it // 2, it % 2
                b = it % 2
                out = 1
                pe.wait_ge(sem("scan_in"), it + 1)
                if it >= 1:
                    pe.wait_ge(sem("scores"), it)
                    pe.wait_ge(sem("keys_t"), it)
                if it == 0:
                    pe.wait_ge(sem("vt"), NCH)
                for c in range(NCH):
                    last = pe.matmul(ps[0:CH, 6, c * CH:(c + 1) * CH], f_kk[:, b, c * CH:(c + 1) * CH],
                                     f_q[:, b, c * CH:(c + 1) * CH], start=(c == 0), stop=(c == NCH - 1), skip_group_check=True)
                last.then_inc(sem("scores_ps"), 1)
                for i in range(NCH - 1):
                    c = i + bwd
                    last = pe.transpose(ps[0:CH, 7, i * P:(i + 1) * P], f_kd[:, b, c * CH:(c + 1) * CH], ident)
                last.then_inc(sem("keys_ps"), 1)
                if 3 * it + 3 < 16:
                    conv_stage(3 * it + 3)
                pe.wait_ge(sem("keys_t"), it + 1)
                if it >= 1:
                    pe.wait_ge(sem("state"), it)
                for i in range(NCH - 1):
                    c = i + bwd
                    last = pe.matmul(ps[:, 0, i * P:(i + 1) * P], kd_t[0:CH, i, :], vt[0:CH, c, hd * P:(hd + 1) * P],
                                     start=(i == 0), stop=(i == NCH - 2), skip_group_check=True)
                last.then_inc(sem("state_ps"), 1)
                if 3 * it + 4 < 16:
                    conv_stage(3 * it + 4)
                pe.wait_ge(sem("scores"), it + 1)
                pe.wait_ge(sem("state"), it + 1)
                if hd >= 1 and not bwd:
                    pe.wait_ge(sem("head"), hd)
                for c in range(NCH):
                    last = pe.matmul(ps[:, out, c * CH:(c + 1) * CH], vt[0:CH, c, hd * P:(hd + 1) * P],
                                     sc_m[0:CH, b, c * CH:(c + 1) * CH], start=(c == 0 and not bwd), stop=False, skip_group_check=True)
                    if c != (NCH - 1 if bwd else 0):
                        i = c if bwd else c - 1
                        last = pe.matmul(ps[:, out, c * CH:(c + 1) * CH], states[:, b, i * P:(i + 1) * P],
                                         f_qe[:, b, c * CH:(c + 1) * CH], start=False, stop=False, skip_group_check=True)
                last.then_inc(sem("scan_ps"), 1)
                if 3 * it + 5 < 16:
                    conv_stage(3 * it + 5)
                if it == 6:
                    pe.wait_ge(sem("sq_hy"), 1)
                    norm_sum(pe, ones, hyena_sq, 4, ps[:, 4, 0:T], sem("ss_hy"))
                    head_sum(0)
                    head_sum(1)
                if it == 7:
                    head_sum(2)
            head_sum(NH - 1)
            pe.wait_ge(sem("mixed_hg"), NH)
            pe.wait_ge(sem("mixed_hy"), NH)
            pe.sem_inc(sem("unit_free"), 4)
            for j in range(HY + HG, HY + HG + KD):
                strip(j, j // 4, j % 4, lambda k: conv[:, k, META:T] if k < 4 else hg[:, k - 4, TP - SEQ:TP], SEQ)
            pe.wait_ge(sem("sq_ffn"), 1)
            pe.sem_inc(sem("unit_free"), 2)
            norm_sum(pe, ones, a[:, :, 0:SEQ], KD, ps[:, 2, 0:SEQ], sem("ss_ffn"))

            pe.wait_ge(sem("normed_ffn"), KD)
            pe.wait_ge(sem("in_router"), 16)
            for tt in range(2):
                for k in range(KD):
                    last = pe.matmul(ps[:, 7, tt * (NG + NE):(tt + 1) * (NG + NE)], a[:, k, tt * P:(tt + 1) * P], router[:, k, :],
                                     start=(k == 0), stop=(k == KD - 1))
            last.then_inc(sem("logits_ps"), 1)
            n = 0
            for tt in range(2):
                for k in range(KD):
                    if n >= 4:
                        pe.wait_ge(sem("xn"), n - 3)
                    pe.transpose(ps[:, 3 + n % 4, 0:P], a[:, k, tt * P:(tt + 1) * P], ident).then_inc(sem("xn_ps"), 1)
                    n += 1
            pe.wait_ge(sem("chosen"), 1)
            pe.matmul(ps[:, 7, 0:NE], C("before"), chosen[:, 0, :], start=True, stop=True)
            pe.matmul(ps[:, 7, NE:2 * NE], ones, chosen[:, 0, :], start=True, stop=False)
            pe.matmul(ps[:, 7, NE:2 * NE], C("before"), chosen[:, 1, :], start=False, stop=True)
            pe.matmul(ps[:, 7, 2 * NE:3 * NE], ones, chosen[:, 0, :], start=True, stop=False)
            pe.matmul(ps[:, 7, 2 * NE:3 * NE], ones, chosen[:, 1, :], start=False, stop=True).then_inc(sem("slots_ps"), 1)

            pe.wait_ge(sem("rounds"), 1)
            n_rounds = pe.value_load(rounds[0:1, 0:1], min_val=1, max_val=SEQ // CAP)
            with pe.Fori(0, n_rounds) as r:
                with pe.Fori(0, NGRP) as g:
                    it = pe.snap(r * NGRP + g)
                    pe.wait_ge(sem("onehot"), it + 1)
                    for k in range(KD):
                        for tt in range(2):
                            last = pe.matmul(ps[:, 4 + k // 4, (k % 4) * P:(k % 4 + 1) * P], xn[:, tt, k * P:(k + 1) * P],
                                             onehot[:, tt, :], start=(tt == 0), stop=(tt == 1))
                    last.then_inc(sem("gather_ps"), 1)
                    for tt in range(2):
                        last = pe.transpose(ps[:, 7, tt * P:(tt + 1) * P], weighted[:, tt, :], ident)
                    last.then_inc(sem("back_ps"), 1)
                    pe.wait_ge(sem("xg"), 2 * it + 2)
                    for v in range(8):
                        s = (v + 2) % RING
                        pe.wait_ge(sem(f"w2_in{s}"), it * 64 + (v // RING + 1) * 32)
                        w = ring[:, s, :].rearrange("p (k e n) -> p k e n", k=2, n=FE)
                        for k in range(2):
                            for e in range(GRP):
                                last = pe.matmul(ps[CAP * e:CAP * (e + 1), v // 4, :], xg[:, (v % 4) * 2 + k, CAP * e:CAP * (e + 1)],
                                                 w[:, k, e, :], start=(v % 4 == 0 and k == 0), stop=(v % 4 == 3 and k == 1))
                        last.then_inc(sem("unit_free"), 1)
                    pe.wait_ge(sem("mid"), it + 1)
                    for c in range(FE // P):
                        last = pe.transpose(ps[:, 6, c * P:(c + 1) * P], mid[:, c * P:(c + 1) * P], ident)
                    last.then_inc(sem("mid_ps"), 1)
                    pe.wait_ge(sem("mid_t"), it + 1)
                    for v in range(8, 12):
                        s = (v + 2) % RING
                        pe.wait_ge(sem(f"w2_in{s}"), it * 64 + (v // RING + 1) * 32)
                        w = ring[:, s, :].rearrange("p (e n) -> p e n", n=D)
                        for half in range(2):
                            for e in range(GRP):
                                last = pe.matmul(ps[CAP * e:CAP * (e + 1), 2 + half, :], mid_t[:, v - 8, CAP * e:CAP * (e + 1)],
                                                 w[:, e, half * 512:(half + 1) * 512], start=(v == 8), stop=(v == 11))
                        last.then_inc(sem("unit_free"), 1)
                    pe.wait_ge(sem("y_slot"), 2 * it + 2)
                    for k in range(KD):
                        last = pe.matmul(ps[:, 4 + k // 2, (k % 2) * SEQ:(k % 2 + 1) * SEQ], y_slot[:, k * P:(k + 1) * P], back,
                                         start=True, stop=True)
                    last.then_inc(sem("scatter_ps"), 1)
            pe.wait_ge(sem("sq_mem"), 1)
            norm_sum(pe, ones, mem_sq, KD, ps[:, 1, 0:SEQ], sem("ss_mem"))
            pe.wait_ge(sem("sq_final"), 1)
            norm_sum(pe, ones, an, KD, ps[:, 0, 0:SEQ], sem("ss_final"))

        @block.scalar
        def _(act):
            ac = Chain(act, sem("act_chain"))
            act.wait_ge(sem("in_h"), 16)
            norm_squares(act, xr(h), xr(a), sem("sq_mix"))
            act.wait_ge(sem("in_const"), 16)
            act.wait_ge(sem("ss_mix"), 1)
            norm_rstd(act, ac, rstd, ps[:, 3, 0:T], D, eps, sem("rstd_mix"))
            for i in range(2):
                act.wait_ge(sem("hid_arg"), i + 1)
                act.activation(hid[0:64, :], hid[0:64, :], ACT.Sin).then_inc(sem("hid_act"), 1)
            for j in range(HY + HG):
                if j == 4:
                    for n in range(12):
                        o, part, ft = n // 6, n // 3 % 2, n % 3
                        act.wait_ge(sem("spectrum_ps"), n + 1)
                        act.copy(spectra[0:TW[ft], ft, 2 * o + part, :], ps[0:TW[ft], 4 + n % 4, :]).then_inc(sem("spectrum"), 1)
                    act.wait_ge(sem("rope_arg"), 1)
                    act.activation(xr(rope), xr(rope), ACT.Sin).then_inc(sem("rope"), 1)
                    act.wait_ge(sem("lb_diff"), 1)
                    act.activation(lb[:, :, 0, :], lb[:, :, 0, :], ACT.Exp).then_inc(sem("lb_exp"), 1)
                act.wait_ge(sem("strip"), j + 1)
                if j < HY:
                    if j == 0:
                        act.wait_ge(sem("edges"), 1)
                    if j >= 4:
                        act.wait_ge(sem("convolved"), j - 3)
                    act.copy(padded[:, j % 4, 1:T + 1], strip_at(j)).then_inc(sem(f"strip_out{j % 2}"), 1)
                elif 24 <= j < 28:
                    act.wait_ge(sem("hg_zero"), 1)
                    act.copy(hg[:, j - HY, PADT:TP], strip_at(j)).then_inc(sem(f"strip_out{j % 2}"), 1)
                else:
                    act.activation(sig[:, j % 2, :], strip_at(j), ACT.Exp, scale=-1.0).then_inc(sem("strip_exp"), 1)
            for c in range(NCH):
                act.wait_ge(sem("vt_ps"), c + 1)
                act.copy(vt[0:CH, c, :], ps[0:CH, 6 + c % 2, :]).then_inc(sem("vt"), 1)

            def head_squares(hd):
                act.wait_ge(sem("head"), hd + 1)
                act.activation(head_sq[:, hd, :], hg[:, 4 + hd, PADT:TP], ACT.Square).then_inc(sem("sq_head"), 1)

            def head_rstd(hd):
                act.wait_ge(sem("ss_head"), hd + 1)
                norm_rstd(act, ac, head_sq[:, hd, :], ps[:, HEAD_BANKS[hd], 0:T], P, eps, sem("rstd_head"))

            for step in range(2 * NH + 1):
                new, old, b = step, step - 1, step % 2
                if new < 2 * NH:
                    act.wait_ge(sem("forget"), new + 1)
                    act.activation(f_lf[:, b, PADT:TP], f_lf[:, b, PADT:TP], ACT.Ln).then_inc(sem("log_f"), 1)
                if old >= 0:
                    act.wait_ge(sem("keys_ps"), old + 1)
                    if old >= 1:
                        act.wait_ge(sem("state_ps"), old)
                    act.copy(xr(kd_t[0:CH]), ps[0:CH, 7, 0:(NCH - 1) * P]).then_inc(sem("keys_t"), 1)
                if step == 8:
                    act.wait_ge(sem("ss_hy"), 1)
                    norm_rstd(act, ac, rstd, ps[:, 4, 0:T], HALF, eps, sem("rstd_hy"))
                    head_rstd(0)
                    head_rstd(1)
                if new < 2 * NH:
                    act.wait_ge(sem("cum"), new + 1)
                    act.activation(f_q[:, b, :], f_rel[:, b, :], ACT.Exp).then_inc(sem("scan_exp"), 1)
                    act.activation(f_kk[:, b, :], f_rel[:, b, :], ACT.Exp, scale=-1.0).then_inc(sem("scan_exp"), 1)
                    act.activation(f_qe[:, b, :], f_cum[:, b, :], ACT.Exp).then_inc(sem("scan_exp"), 1)
                    act.activation(f_kd[:, b, :], f_kd[:, b, :], ACT.Exp).then_inc(sem("scan_exp"), 1)
                    last_of = f_cum[:, b, 0:TP:CH] if b else f_cum[:, b, CH - 1:TP:CH]
                    act.activation(decay[:, b, :], last_of, ACT.Exp).then_inc(sem("scan_exp"), 1)
                if new % 2 and new >= 3:
                    head_squares(new // 2 - 1)
                if new == 6:
                    act.wait_ge(sem("z"), 12)
                    act.activation(hyena_sq, conv[:, 0:4, :], ACT.Square).then_inc(sem("sq_hy"), 1)
            head_squares(NH - 1)
            head_rstd(NH - 2)
            head_rstd(NH - 1)
            act.wait_ge(sem("strip_out0"), 20)
            act.wait_ge(sem("strip_out1"), 20)
            act.dma_start(xr(router), d["router"]).then_inc(sem("in_router"), 16)
            act.dma_start(xr(mem_raw), d["mem"]).then_inc(sem("in_mem"), 16)
            norm_squares(act, x_tok, an, sem("sq_ffn"))
            act.wait_ge(sem("ss_ffn"), 1)
            norm_rstd(act, ac, rstd[:, 0:SEQ], ps[:, 2, 0:SEQ], D, eps, sem("rstd_ffn"))
            for n in range(2 * KD):
                act.wait_ge(sem("xn_ps"), n + 1)
                act.copy(xn[:, n // KD, (n % KD) * P:(n % KD + 1) * P], ps[:, 3 + n % 4, 0:P]).then_inc(sem("xn"), 1)
            act.wait_ge(sem("route_arg"), 1)
            act.activation(small[:, 4:6, 0:8], small[:, 4:6, 0:8], ACT.Exp).then_inc(sem("route_exp"), 1)
            act.activation(small[:, 14:16, 0:1], small[:, 14:16, 0:1], ACT.Exp).then_inc(sem("route_exp"), 1)
            act.wait_ge(sem("in_mem"), 16)
            norm_squares(act, mem_raw, mem_sq, sem("sq_mem"))
            act.wait_ge(sem("rounds"), 1)
            n_rounds = act.value_load(rounds[0:1, 0:1], min_val=1, max_val=SEQ // CAP)
            with act.Fori(0, n_rounds) as r:
                with act.Fori(0, NGRP) as g:
                    it = act.snap(r * NGRP + g)
                    act.wait_ge(sem("back_ps"), it + 1)
                    act.copy(back, ps[:, 7, 0:SEQ]).then_inc(sem("back"), 1)
                    act.wait_ge(sem("unit_free"), it * 12 + 6 + 4)
                    act.activation(gate_e, ps[:, 0, :], ACT.Exp, scale=-1.0).then_inc(sem("gate_exp"), 1)
                    act.wait_ge(sem("mid_ps"), it + 1)
                    act.copy(xr(mid_t), ps[:, 6, :]).then_inc(sem("mid_t"), 1)
            act.wait_ge(sem("experts_done"), 1)
            norm_squares(act, x_tok, an, sem("sq_final"))
            act.wait_ge(sem("ss_mem"), 1)
            norm_rstd(act, ac, hn_mem, ps[:, 1, 0:SEQ], D, eps, sem("rstd_mem"))
            act.wait_ge(sem("ss_final"), 1)
            norm_rstd(act, ac, rstd[:, 0:SEQ], ps[:, 0, 0:SEQ], D, eps, sem("rstd_final"))

        @block.vector
        def _(dve):
            vc = Chain(dve, sem("dve_chain"))
            link, tick = vc.link, vc.tick
            dve.memset(padded[:, :, 0:1], 0.0)
            dve.memset(padded[:, :, T + 1:T + 2], 0.0).then_inc(sem("edges"), 1)
            dve.wait_ge(sem("in_param1"), 16)
            for i in range(2):
                dve.wait_ge(sem("hid"), i + 1)
                ph, wr = hid[0:64, :], wrap[0:64, :]
                link(dve.tensor_scalar(ph, ps[0:64, 2, 0:T], P1(f"filt_b{i + 1}", rows=64), P1("filt_freq", rows=64), ALU.add, ALU.mult))
                link(dve.tensor_scalar(wr, ph, 0.5 / math.pi, MAGIC, ALU.mult, ALU.add))
                link(dve.tensor_scalar(wr, wr, -MAGIC, None, ALU.add))
                link(dve.scalar_tensor_tensor(ph, wr, -TWO_PI_HI, ph, ALU.mult, ALU.add))
                link(dve.scalar_tensor_tensor(ph, wr, -TWO_PI_LO, ph, ALU.mult, ALU.add))
                dve.tensor_scalar(ph, ph, math.pi * (1 - 1e-7), -math.pi * (1 - 1e-7), ALU.min, ALU.max).then_inc(sem("hid_arg"), 1)
                if i == 0:
                    dve.wait_ge(sem("rstd_mix"), 1)
                    dve.wait_ge(sem("ss_mix"), 1)
                    for k in range(KD):
                        dve.scalar_tensor_tensor(a[:, k, :], h[:, k, :], P1("norm_mix", k), rstd, ALU.mult, ALU.mult).then_inc(sem("normed_mix"), 1)
            dve.wait_ge(sem("in_w3"), 32)
            n = 0
            for tt in range(3):
                for c in range(4):
                    dve.wait_ge(sem("filt_ps"), n + 1)
                    dve.tensor_tensor(filt[0:TW[tt], tt, c, :], ps[0:TW[tt], 4 + n % 4, :], window[0:TW[tt], tt, :], ALU.mult).then_inc(sem("filt"), 1)
                    n += 1
            dve.wait_ge(sem("filt"), 12)
            link(dve.memset(filt[0:1, 0, 2:4, :], 0.0))
            for rows, tiles in ((P, slice(0, 2)), (TW[2], slice(2, 3))):
                fwd = filt[0:rows, tiles, 0:2, :].rearrange("p t o n -> p t (o n)")
                bwd = filt[0:rows, tiles, 2:4, :].rearrange("p t o n -> p t (o n)")
                dve.tensor_tensor(bwd, fwd, bwd, ALU.subtract).then_inc(sem("filt_sd"), 1)
                dve.wait_ge(sem("filt_sd"), 1 if rows == P else 3)
                dve.scalar_tensor_tensor(fwd, fwd, 2.0, bwd, ALU.mult, ALU.subtract).then_inc(sem("filt_sd"), 1)
            dve.wait_ge(sem("in_pos"), 16)
            dve.wait_ge(sem("filt"), 12)
            ang, tmp = window[:, 0, 0:SEQ], window[:, 1, 0:SEQ]
            link(dve.tensor_copy(ang, pos_i[:, :]))
            link(dve.tensor_scalar(ang, ang, C("inv_freq"), None, ALU.mult))
            for i, turn in ((0, 0.0), (1, 0.25)):
                r = rope[:, i, :]
                link(dve.tensor_scalar(tmp, ang, 0.5 / math.pi, turn, ALU.mult, ALU.add))
                link(dve.tensor_scalar(tmp, tmp, MAGIC, None, ALU.add))
                link(dve.tensor_scalar(tmp, tmp, -MAGIC, None, ALU.add))
                link(dve.scalar_tensor_tensor(r, tmp, -TWO_PI_HI, ang, ALU.mult, ALU.add))
                link(dve.scalar_tensor_tensor(r, tmp, -TWO_PI_LO, r, ALU.mult, ALU.add))
                link(dve.tensor_scalar(r, r, 2 * math.pi * turn, None, ALU.add))
                link(dve.tensor_scalar(r, r, math.pi * (1 - 1e-7), -math.pi * (1 - 1e-7), ALU.min, ALU.max))
            dve.nop().then_inc(sem("rope_arg"), 1)
            raw = P1("lb").rearrange("p (d r h) -> p d r h", d=2, r=2)
            dve.tensor_tensor(lb[:, :, 0, :], raw[:, :, 1, :], raw[:, :, 0, :], ALU.subtract).then_inc(sem("lb_diff"), 1)
            dve.wait_ge(sem("lb_exp"), 1)
            link(dve.tensor_scalar(lb[:, :, 1, :], lb[:, :, 0, :], 1.0, None, ALU.add))
            link(dve.reciprocal(lb[:, :, 0, :], lb[:, :, 1, :]))
            link(dve.tensor_scalar(lb[:, :, 1, :], lb[:, :, 0, :], -1.0, 1.0, ALU.mult, ALU.add))
            dve.wait_ge(sem("filt_ps"), 12)
            link(dve.memset(hg[:, :, 0:PADT], 0.0))
            dve.memset(hg[:, 0:1, 0:1], 0.0).then_inc(sem("hg_zero"), 1)
            for j in range(HY + HG):
                if j < HY:
                    job_evacuated(dve, j)
                    src = padded[:, j % 4, :]
                    y = conv[:, j, :]
                    link(dve.tensor_scalar(y, src[:, 0:T], P1("conv_w", j), P1("conv_b", j), ALU.mult, ALU.add))
                    link(dve.scalar_tensor_tensor(y, src[:, 1:T + 1], P1("conv_w", HY + j), y, ALU.mult, ALU.add))
                    dve.scalar_tensor_tensor(y, src[:, 2:T + 2], P1("conv_w", 2 * HY + j), y, ALU.mult, ALU.add).then_inc(sem("convolved"), 1)
                    if j < 4:
                        dve.wait_ge(sem("convolved"), j + 1)
                        dve.nop().then_inc(sem("z"), 1)
                elif not 24 <= j < 28:
                    dve.wait_ge(sem("strip_exp"), j - HY + 1 - (4 if j >= 28 else 0))
                    e = sig[:, j % 2, :]
                    y = hg[:, j - HY, PADT:TP]
                    link(dve.tensor_scalar(e, e, 1.0, None, ALU.add))
                    out = sem(f"strip_out{j % 2}")
                    if 16 <= j < 24:
                        dve.reciprocal(y, e).then_inc(out, 1)
                    else:
                        link(dve.reciprocal(e, e))
                        dve.tensor_tensor(y, strip_at(j), e, ALU.mult).then_inc(out, 1)
            def conv_stage(n):
                o, k = n // 8, n % 8
                if k == 0:
                    for tt in range(3):
                        dve.wait_ge(sem("zt_ps"), 3 * o + tt + 1)
                        dve.tensor_copy(zt[0:TW[tt], tt, :], ps[0:TW[tt], 2 + tt % 2, :]).then_inc(sem("zt"), 1)
                elif k < 4:
                    ft = k - 1
                    n, w = 3 * o + ft, TW[ft]
                    dve.wait_ge(sem("uf_ps"), n + 1)
                    uc, us = ps[0:w, 4, :], ps[0:w, 5, :]
                    kc, ks = spectra[0:w, ft, 2 * o, :], spectra[0:w, ft, 2 * o + 1, :]
                    yc, ys = yf[0:w, ft, 0, :], yf[0:w, ft, 1, :]
                    t1, t2 = prod[0:w, 0, :], prod[0:w, 1, :]
                    if n == 0:
                        dve.wait_ge(sem("spectrum"), 12)
                    if n == 3:
                        dve.wait_ge(sem("conv_ps"), 4)
                    tick(dve.tensor_tensor(yc, uc, kc, ALU.mult))
                    tick(dve.tensor_tensor(t1, us, ks, ALU.mult))
                    tick(dve.tensor_tensor(ys, uc, ks, ALU.mult))
                    link(dve.tensor_tensor(t2, us, kc, ALU.mult))
                    tick(dve.tensor_tensor(yc, yc, t1, ALU.subtract))
                    dve.tensor_tensor(ys, ys, t2, ALU.add).then_inc(sem("yf"), 1)
                    dve.wait_ge(sem("yf"), n + 1)
                else:
                    c = k - 4
                    z = conv[:, c, :]
                    dve.wait_ge(sem("conv_ps"), 4 * o + c + 1)
                    link(dve.scalar_tensor_tensor(z, z, P1("skip", 4 * o + c), ps[:, 2 + c % 2, 0:T], ALU.mult, ALU.add))
                    dve.tensor_tensor(z, z, conv[:, 4 * (o + 1) + c, :], ALU.mult).then_inc(sem("z"), 1)
            tick(dve.memset(f_k[:, :, 0:PADT], 0.0))
            link(dve.memset(f_lf[:, :, 0:PADT], 0.0))
            def save_head(it):
                hd = it // 2
                dve.wait_ge(sem("scan_ps"), it + 1)
                dve.tensor_copy(hg[:, 4 + hd, PADT:TP], ps[:, 1, PADT:TP]).then_inc(sem("head"), 1)

            def head_scale(hd):
                dve.wait_ge(sem("rstd_head"), hd + 1)
                o = hg[:, 4 + hd, PADT:TP]
                link(dve.scalar_tensor_tensor(o, o, P1("hgrn_norm", hd), head_sq[:, hd, :], ALU.mult, ALU.mult))
                dve.tensor_tensor(hg[:, hd, PADT:TP], o, hg[:, 16 + hd, PADT:TP], ALU.mult).then_inc(sem("mixed_hg"), 1)

            for step in range(2 * NH + 1):
                new, old = step, step - 1
                if new < 2 * NH:
                    hd, bwd, b = new // 2, new % 2, new % 2
                    if new >= 2:
                        dve.wait_ge(sem("scan_ps"), new - 1)
                        if bwd:
                            save_head(new - 2)
                    s = hg[:, 4 + 4 * bwd + hd, PADT:TP]
                    link(dve.tensor_scalar(f_lf[:, b, PADT:TP], s, lb[:, bwd, 1, hd:hd + 1], lb[:, bwd, 0, hd:hd + 1], ALU.mult, ALU.add))
                    dve.tensor_scalar(f_k[:, b, PADT:TP], f_lf[:, b, PADT:TP], -1.0, 1.0, ALU.mult, ALU.add).then_inc(sem("forget"), 1)
                if old >= 0:
                    dve.wait_ge(sem("scores_ps"), old + 1)
                    mask = C("anticausal" if old % 2 else "causal", CH).unsqueeze(1).to_broadcast([CH, NCH, CH])
                    dve.tensor_tensor(sc_m[0:CH, old % 2, :].rearrange("p (c t) -> p c t", t=CH), ps[0:CH, 6, 0:TP].rearrange("p (c t) -> p c t", t=CH),
                                      mask, ALU.mult).then_inc(sem("scores"), 1)
                if new < 2 * NH:
                    dve.wait_ge(sem("log_f"), new + 1)
                    order = slice(None, None, -1) if bwd else slice(None)
                    cum, rel = f_cum[:, b, :], f_rel[:, b, :]
                    link(dve.tensor_tensor_scan(cum[:, order], C("run"), f_lf[:, b, :][:, order], 0.0, ALU.mult, ALU.add))
                    c3 = cum.rearrange("p (c t) -> p c t", t=CH)
                    mid_at, end_at = (CH - 1 - CH // 2, 0) if bwd else (CH // 2, CH - 1)
                    tick(dve.tensor_tensor(rel.rearrange("p (c t) -> p c t", t=CH), c3, c3[:, :, mid_at:mid_at + 1].to_broadcast([P, NCH, CH]), ALU.subtract))
                    dve.tensor_tensor(f_kd[:, b, :].rearrange("p (c t) -> p c t", t=CH), c3[:, :, end_at:end_at + 1].to_broadcast([P, NCH, CH]), c3,
                                      ALU.subtract).then_inc(sem("cum"), 1)
                if 3 * step < 16:
                    conv_stage(3 * step)
                if old >= 0:
                    dve.wait_ge(sem("state_ps"), old + 1)
                    st = states[:, old % 2, :].rearrange("p (c n) -> p c n", n=P)
                    u = ps[:, 0, :].rearrange("p (c n) -> p c n", n=P)
                    dec = decay[:, old % 2, :]
                    if old % 2:
                        link(dve.tensor_copy(st[:, 3, :], u[:, 3, :]))
                        for i in (2, 1):
                            link(dve.scalar_tensor_tensor(st[:, i, :], st[:, i + 1, :], dec[:, i + 1:i + 2], u[:, i, :], ALU.mult, ALU.add))
                        dve.scalar_tensor_tensor(st[:, 0, :], st[:, 1, :], dec[:, 1:2], u[:, 0, :], ALU.mult, ALU.add).then_inc(sem("state"), 1)
                    else:
                        link(dve.tensor_copy(st[:, 0, :], u[:, 0, :]))
                        for i in (1, 2):
                            link(dve.scalar_tensor_tensor(st[:, i, :], st[:, i - 1, :], dec[:, i:i + 1], u[:, i, :], ALU.mult, ALU.add))
                        dve.scalar_tensor_tensor(st[:, 3, :], st[:, 2, :], dec[:, 3:4], u[:, 3, :], ALU.mult, ALU.add).then_inc(sem("state"), 1)
                if 3 * step + 1 < 16:
                    conv_stage(3 * step + 1)
                if new < 2 * NH:
                    dve.wait_ge(sem("scan_exp"), 5 * new + 5)
                    tick(dve.tensor_tensor(f_q[:, b, :], f_q[:, b, :], hg[:, hd, :], ALU.mult))
                    tick(dve.tensor_tensor(f_kk[:, b, :], f_kk[:, b, :], f_k[:, b, :], ALU.mult))
                    tick(dve.tensor_tensor(f_qe[:, b, :], f_qe[:, b, :], hg[:, hd, :], ALU.mult))
                    dve.tensor_tensor(f_kd[:, b, :], f_kd[:, b, :], f_k[:, b, :], ALU.mult).then_inc(sem("scan_in"), 1)
                if 3 * step + 2 < 16:
                    conv_stage(3 * step + 2)
            dve.wait_ge(sem("z"), 12)
            dve.wait_ge(sem("rstd_hy"), 1)
            for c in range(4):
                dve.scalar_tensor_tensor(conv[:, c, :], conv[:, c, :], P1("hyena_norm", c), rstd, ALU.mult, ALU.mult).then_inc(sem("mixed_hy"), 1)
            head_scale(0)
            head_scale(1)
            save_head(2 * NH - 1)
            head_scale(2)
            head_scale(NH - 1)
            for c in range(KD):
                j = HY + HG + c
                dve.wait_ge(sem("strip"), j + 1)
                dve.tensor_tensor(h[:, c, META:T], h[:, c, META:T], ps[:, j % 2, 0:SEQ], ALU.add).then_inc(sem(f"strip_out{j % 2}"), 1)
            dve.wait_ge(sem("ss_ffn"), 1)
            dve.wait_ge(sem("rstd_ffn"), 1)
            for k in range(KD):
                dve.scalar_tensor_tensor(an[:, k, :], x_tok[:, k, :], P1("norm_ffn", k), rstd[:, 0:SEQ], ALU.mult, ALU.mult).then_inc(sem("normed_ffn"), 1)

            def sm(i, n=8):
                return small[:, 2 * i:2 * i + 2, 0:n]

            def bc(v, n):
                return v.to_broadcast([P, 2, n])

            def first_max(values, best, hot, t1):
                link(dve.tensor_reduce(best, values, AX, ALU.max))
                link(dve.tensor_tensor(t1, values, bc(best, 8), ALU.is_ge))
                link(dve.scalar_tensor_tensor(t1, t1, -64.0, eight, ALU.mult, ALU.add))
                link(dve.tensor_reduce(first, t1, AX, ALU.min))
                link(dve.tensor_tensor(hot, t1, bc(first, 8), ALU.is_equal))

            eight = C("eight").unsqueeze(1).to_broadcast([P, 2, 8])
            g_hot, e_sel, e1_hot, e2_hot, t1 = sm(3), sm(4), sm(5), sm(6), sm(8)
            g_max, e1_max, e2_max, second, first, total, top = (sm(i, 1) for i in (0, 1, 9, 7, 10, 11, 3))
            total, w1, w2 = small[:, 22:24, 0:1], small[:, 22:24, 1:2], small[:, 22:24, 2:3]
            dve.wait_ge(sem("logits_ps"), 1)
            link(dve.tensor_copy(xr(logits), ps[:, 7, 0:2 * (NG + NE)]))
            lg, le = logits[:, :, 0:NG], logits[:, :, NG:NG + NE]
            first_max(lg, g_max, g_hot, t1)
            link(dve.tensor_tensor(sm(2), lg, bc(g_max, 8), ALU.subtract))
            link(dve.tensor_tensor(pick.rearrange("p t (g e) -> p t g e", g=NG), le.rearrange("p t (g e) -> p t g e", g=NG),
                                   g_hot.unsqueeze(3).to_broadcast([P, 2, NG, EPG]), ALU.mult))
            for tt in range(2):
                (link if tt else tick)(dve.tensor_reduce(e_sel[:, tt, :], pick[:, tt, :].rearrange("p (g e) -> p e g", g=NG), AX, ALU.add))
            first_max(e_sel, e1_max, e1_hot, t1)
            link(dve.scalar_tensor_tensor(e_sel, e1_hot, -BIG, e_sel, ALU.mult, ALU.add))
            first_max(e_sel, e2_max, e2_hot, t1)
            dve.tensor_tensor(second, e2_max, e1_max, ALU.subtract).then_inc(sem("route_arg"), 1)

            def spread(out, per_expert):
                for tt in range(2):
                    ins = dve.tensor_tensor(out[:, tt, :].rearrange("p (g e) -> p g e", g=NG), g_hot[:, tt, :].unsqueeze(2).to_broadcast([P, NG, EPG]),
                                            per_expert[:, tt, :].unsqueeze(1).to_broadcast([P, NG, EPG]), ALU.mult)
                    (link if tt else tick)(ins)
            link(dve.tensor_tensor(t1, e1_hot, e2_hot, ALU.add))
            spread(chosen, t1)
            dve.nop().then_inc(sem("chosen"), 1)
            dve.wait_ge(sem("route_exp"), 2)
            link(dve.tensor_reduce(total, sm(2), AX, ALU.add))
            link(dve.tensor_scalar(w1, second, 1.0, None, ALU.add))
            link(dve.tensor_tensor(w1, w1, total, ALU.mult))
            link(dve.reciprocal(w1, w1))
            link(dve.tensor_tensor(w2, w1, second, ALU.mult))
            link(dve.tensor_tensor(e1_hot, e1_hot, bc(w1, 8), ALU.mult))
            link(dve.tensor_tensor(e2_hot, e2_hot, bc(w2, 8), ALU.mult))
            link(dve.tensor_tensor(e1_hot, e1_hot, e2_hot, ALU.add))

            spread(pick, e1_hot)
            dve.wait_ge(sem("slots_ps"), 1)
            link(dve.scalar_tensor_tensor(xr(slot_of), ps[:, 7, 0:2 * NE], 1.0, xr(chosen), ALU.add, ALU.mult))
            link(dve.tensor_scalar(xr(slot_of), xr(slot_of), -1.0, None, ALU.add))
            link(dve.tensor_reduce(first[:, 0, :], ps[:, 7, 2 * NE:3 * NE], AX, ALU.max))
            link(dve.tensor_scalar(first[:, 0, :], first[:, 0, :], 1.0 / CAP, 0.5 - 0.5 / CAP, ALU.mult, ALU.add))
            link(dve.tensor_scalar(first[:, 0, :], first[:, 0, :], MAGIC, -MAGIC, ALU.add, ALU.add))
            dve.tensor_copy(rounds[:, 0:1], first[:, 0, :]).then_inc(sem("rounds"), 1)
            dve.wait_ge(sem("rounds"), 1)
            n_rounds = dve.value_load(rounds[0:1, 0:1], min_val=1, max_val=SEQ // CAP)
            mc = Chain(dve, sem("expert_chain"))
            per = 4
            slots = C("slots").unsqueeze(1).to_broadcast([P, GRP, CAP])
            with dve.Fori(0, n_rounds) as r:
                with dve.Fori(0, NGRP) as g:
                    it = dve.snap(r * NGRP + g)
                    mc.turn(it, per, 0)
                    for tt in range(2):
                        mc.tick(dve.tensor_tensor(onehot[:, tt, :].rearrange("p (e s) -> p e s", e=GRP), slots,
                                                  slot_of[:, tt, bass.ds(g * GRP, GRP)].unsqueeze(2).to_broadcast([P, GRP, CAP]), ALU.is_equal))
                    dve.wait_ge(mc.sem, mc.base + mc.n)
                    for tt in range(2):
                        ins = dve.tensor_tensor(weighted[:, tt, :].rearrange("p (e s) -> p e s", e=GRP), onehot[:, tt, :].rearrange("p (e s) -> p e s", e=GRP),
                                                pick[:, tt, bass.ds(g * GRP, GRP)].unsqueeze(2).to_broadcast([P, GRP, CAP]), ALU.mult)
                    ins.then_inc(sem("onehot"), 1)
                    dve.wait_ge(sem("gather_ps"), it + 1)
                    for j in range(2):
                        dve.tensor_copy(xr(xg[:, 4 * j:4 * j + 4, :]), ps[:, 4 + j, :]).then_inc(sem("xg"), 1)
                    dve.wait_ge(sem("gate_exp"), it + 1)
                    mc.link(dve.tensor_scalar(gate_e, gate_e, 1.0, None, ALU.add))
                    mc.link(dve.reciprocal(gate_e, gate_e))
                    dve.tensor_tensor(gate_e, ps[:, 0, :], gate_e, ALU.mult).then_inc(sem("gated"), 1)
                    dve.wait_ge(sem("gated"), it + 1)
                    dve.wait_ge(sem("unit_free"), it * 12 + 6 + 8)
                    dve.tensor_tensor(mid, gate_e, ps[:, 1, :], ALU.mult).then_inc(sem("mid"), 1)
                    dve.wait_ge(sem("unit_free"), it * 12 + 6 + 12)
                    for half in range(2):
                        dve.tensor_copy(y_slot[:, half * 512:(half + 1) * 512], ps[:, 2 + half, :]).then_inc(sem("y_slot"), 1)
                    dve.wait_ge(sem("back"), it + 1)
                    dve.wait_ge(sem("scatter_ps"), it + 1)
                    for k in range(0, KD, 2):
                        dve.tensor_tensor(x_tok[:, k:k + 2, :], x_tok[:, k:k + 2, :], ps[:, 4 + k // 2, :].rearrange("p (k t) -> p k t", k=2),
                                          ALU.add).then_inc(sem("scattered"), 1)
                    dve.wait_ge(sem("scattered"), it * 4 + 4)
                    mc.end_turn(per)
                dve.tensor_scalar(xr(slot_of), xr(slot_of), -float(CAP), None, ALU.add).then_inc(sem("round_end"), 1)
                dve.wait_ge(sem("round_end"), r + 1)
            dve.nop().then_inc(sem("experts_done"), 1)
            dve.wait_ge(sem("ss_final"), 1)
            dve.wait_ge(sem("rstd_final"), 1)
            for k in range(KD):
                dve.scalar_tensor_tensor(x_tok[:, k, :], x_tok[:, k, :], P1("norm_final", k), rstd[:, 0:SEQ], ALU.mult, ALU.mult).then_inc(sem("x_final"), 1)

        block_one.close()
        nc.clear_and_free_semaphores(list(named.values()))
        named.clear()
        nc.all_engine_barrier()
        with nc.Block() as block:
            @block.sync
            def _(sp):
                layers_sync(sp)

            @block.tensor
            def _(pe):
                layers_pe(pe)

            @block.scalar
            def _(act):
                layers_act(act)

            @block.vector
            def _(dve):
                layers_dve(dve)


INPUTS = ["const", "fourier", "features", "param1", "filt_w1", "filt_w2", "filt_w3", "h", "w_first", "router",
          "w_gate", "w_up", "w_down", "positions", "mem", "w_layers", "param2", "w_if", "gm_ws", "gm_rows"]


def strips(w):
    w = np.asarray(w)
    n = w.shape[1] // P
    return w.reshape(KD, P, n, P).transpose(2, 1, 0, 3).reshape(n, P, KD * P)


def units(s):
    return s.reshape(-1, 4, P, KD * P).transpose(0, 2, 1, 3).reshape(-1, P, WSLOT)


def layout(a):
    out = {}
    shape, fourier, features, first = shape_constants(), filter_constants(), filter_features(), first_params(a)
    out["const"], out["fourier"], out["features"], out["param1"] = (c.array() for c in (shape, fourier, features, first))
    for n in ("filt_w1", "filt_w2", "filt_w3"):
        out[n] = a[n][0]
    tokens = np.concatenate([a["meta_tokens"], a["x"][0]], axis=0)
    out["h"] = tokens.T.reshape(KD, P, T).transpose(1, 0, 2).reshape(P, KD * T)
    out["w_first"] = np.concatenate([units(strips(a["w_in"][0])), units(strips(a["w_out"][0]))])
    router = np.concatenate([a["w_router_group"][0], a["w_router_expert"][0].reshape(D, NE)], axis=1)
    out["router"] = router.reshape(KD, P, NG + NE).transpose(1, 0, 2).reshape(P, -1)
    for n in ("w_gate", "w_up", "w_down"):
        out[n] = a[n][0]
    out["positions"] = a["positions_2"].reshape(SEQ)
    out["mem"] = a["mem_2"][0].T.reshape(KD, P, SEQ).transpose(1, 0, 2).reshape(P, -1)
    params = [layer_params(a, l) for l in range(LAYERS)]
    out["param2"] = np.stack([c.array() for c in params])
    w = HALF
    ml, gates = 4 * w, 9 * w
    gm = gates + 8
    rt, xa, mg = gm + 3 * w, gm + 7 * w, gm + 9 * w
    column = {"xa_q": xa, "xa_z": xa + w}
    column.update({f"sb_{n}": i * w for i, n in enumerate("qkvz")})
    column.update({f"ml_{n}": ml + i * w for i, n in enumerate("qkvoz")})
    column.update({f"gm_{n}": gm + i * w for i, n in enumerate("uvz")})
    column.update({f"rt_{n}": rt + i * w for i, n in enumerate("qkvz")})
    layers = []
    for l in range(LAYERS):
        w_in, kv = a["w_in_2"][l], a["w_mem_kv_2"][l]
        parts = []
        for n in (n for group in UNIT_GROUPS for n in group):
            if n in ("mem_k", "mem_v"):
                at = 0 if n == "mem_k" else w
                parts.append(units(strips(kv[:, at:at + w])))
            else:
                parts.append(units(strips(w_in[:, column[n]:column[n] + w])))
        gate = strips(w_in[:, mg:]).reshape(NBR, KD, P, KD * P)
        up = a["w_up_2"][l].reshape(NBR, 4, P, KD, P).transpose(0, 3, 2, 1, 4).reshape(NBR, KD, P, 4 * P)
        pair = np.concatenate([gate, up], axis=3)[list(MERGE_ORDER)].transpose(1, 0, 2, 3).reshape(-1, 2, P, 1536).transpose(0, 2, 1, 3).reshape(-1, P, 3072)
        parts.append(np.concatenate([pair, np.zeros((len(pair), P, WSLOT - 3072), np.float32)], axis=2))
        parts.append(units(strips(a["w_out_2"][l])))
        layers.append(np.concatenate(parts))
    out["w_layers"] = np.concatenate(layers)
    out["w_if"] = a["w_in_2"][:, :, gates:gates + 8].reshape(LAYERS, KD, P, 8).transpose(0, 2, 1, 3).reshape(LAYERS, P, -1)
    out["gm_ws"] = a["gm_ws_2"].transpose(0, 3, 1, 2).reshape(LAYERS, P, -1)
    out["gm_rows"] = np.stack([a["gm_ln_g_2"], a["gm_ln_b_2"], a["gm_bs_2"].reshape(LAYERS, HALF)], axis=1).reshape(LAYERS, -1)
    return out, {"shape": shape.at, "first": first.at, "layer": params[0].at}


def kernel(**inputs):
    import concourse.bacc as bacc
    from concourse.bass_utils import run_bass_kernel_spmd

    arrays, spot = layout({k: np.asarray(v) for k, v in inputs.items()})
    nc = bacc.Bacc("TRN2", target_bir_lowering=False, num_devices=1)
    send, d = {}, {}
    for name in INPUTS:
        v = np.ascontiguousarray(arrays[name])
        send[f"in_{name}"] = v
        d[name] = nc.dram_tensor(f"in_{name}", v.shape, mybir.dt.from_np(v.dtype), kind="ExternalInput").ap()
    d["out"] = nc.dram_tensor("out", (D, SEQ), F32, kind="ExternalOutput").ap()
    build_program(nc, d, spot)
    r = run_bass_kernel_spmd(nc, [send], core_ids=[0])
    return r.results[0]["out"].T.reshape(1, SEQ, D)
```
